# Optimizing a Trainium2 kernel written in Bass

```python
import jax
import jax.numpy as jnp
from jax import lax
import numpy as np

D_MODEL = 1024
BATCH = 1
SEQ = 128
DEPTH = 2
DEC_BATCH = 1
DEC_SEQ = 128
PAST_LEN = 128

GRID_W = 64
BR_WIDTH = 512
N_BRANCH = 3
RET_HEADS = 4
RET_DK = BR_WIDTH // RET_HEADS
RET_DV = BR_WIDTH // RET_HEADS
RET_CHUNK = 128
NA_HEADS = 4
NA_HD = BR_WIDTH // NA_HEADS
NA_ROWS = 8
NA_COLS = 16
NA_QBLOCK = 16
NA_KBLOCK = 32
CTX_QBLOCK = 128
HG_HEADS = 4
HG_DK = BR_WIDTH // HG_HEADS
HG_DV = BR_WIDTH // HG_HEADS
HG_CHUNK = 32
ROPE_BASE = 10000.0
D_FF = 2816
N_EXPERTS = 8
TOP_K = 2
N_DENSE = (DEPTH + 1) // 2
N_MOE = DEPTH // 2
N_MOD = 6
EPS = 1e-6
F_MIN = 1e-30
NEG_INF = -1e30
D_IN = 12 * BR_WIDTH + N_BRANCH * D_MODEL
SPLITS = [BR_WIDTH * i for i in range(1, 13)]
F32 = jnp.float32

kernel_name = 'hybrid_prefix_diffusion_trunk_step'

def rmsnorm(x, g):
    xf = x.astype(F32)
    y = xf * lax.rsqrt(jnp.mean(xf * xf, axis=-1, keepdims=True) + EPS)
    return (y * g.astype(F32)).astype(x.dtype)

def head_layernorm(o):
    of = o.astype(F32)
    mu = jnp.mean(of, axis=-1, keepdims=True)
    var = jnp.mean(jnp.square(of - mu), axis=-1, keepdims=True)
    return ((of - mu) * lax.rsqrt(var + 1e-5)).astype(o.dtype)

def heads(x, n):
    return x.reshape(x.shape[:-1] + (n, x.shape[-1] // n))

def flip(a):
    return jnp.flip(a, axis=1)

def rope_2d(x):
    T, hd = x.shape[1], x.shape[-1]
    nf = hd // 4
    t = jnp.arange(T)
    pos = jnp.stack([t // GRID_W, t % GRID_W], axis=-1).astype(F32)
    inv = ROPE_BASE ** (-jnp.arange(nf, dtype=F32) / nf)
    ang = pos[:, :, None] * inv
    cos = jnp.cos(ang)[None, :, None]
    sin = jnp.sin(ang)[None, :, None]
    xr = x.astype(F32).reshape(x.shape[:-1] + (2, 2, nf))
    x1, x2 = xr[..., 0, :], xr[..., 1, :]
    y = jnp.stack([x1 * cos - x2 * sin, x2 * cos + x1 * sin], axis=-2)
    return y.reshape(x.shape).astype(x.dtype)

def to_chunks(x, c):
    B, T, H, d = x.shape
    return x.reshape(B, T // c, c, H, d).transpose(1, 0, 3, 2, 4)

def from_chunks(y):
    N, B, H, c, d = y.shape
    return y.transpose(1, 0, 3, 2, 4).reshape(B, N * c, H, d)

def retention_scan(q, k, v, log_gamma, s0):
    dtype = v.dtype
    qc, kc, vc = (to_chunks(a.astype(F32), RET_CHUNK) for a in (q, k, v))
    idx = jnp.arange(RET_CHUNK, dtype=F32)
    diff = idx[:, None] - idx[None, :]
    lg = log_gamma.astype(F32)
    dmat = jnp.where(diff >= 0, jnp.exp(lg[:, None, None] * jnp.maximum(diff, 0.0)), 0.0)
    q_dec = jnp.exp(lg[:, None] * (idx + 1.0))[..., None]
    k_dec = jnp.exp(lg[:, None] * (RET_CHUNK - 1.0 - idx))[..., None]
    c_dec = jnp.exp(lg * RET_CHUNK)[:, None, None]

    def step(s, inp):
        qi, ki, vi = inp
        att = jnp.einsum('bhnd,bhmd->bhnm', qi, ki) * dmat
        o = jnp.einsum('bhnm,bhme->bhne', att, vi) + jnp.einsum('bhnd,bhde->bhne', qi * q_dec, s)
        s = s * c_dec + jnp.einsum('bhmd,bhme->bhde', ki * k_dec, vi)
        return s, o

    s, o = lax.scan(step, s0.astype(F32), (qc, kc, vc))
    return from_chunks(o).astype(dtype), s

def hgrn2_scan(q, k, v, logf, s0):
    dtype = v.dtype
    qc, kc, vc, gc = (to_chunks(a.astype(F32), HG_CHUNK) for a in (q, k, v, logf))
    causal = jnp.tril(jnp.ones((HG_CHUNK, HG_CHUNK), dtype=bool))[:, :, None]
    causal_f = causal.astype(F32)

    def step(s, inp):
        qi, ki, vi, gi = inp
        a = jnp.cumsum(gi, axis=2)
        diff = a[:, :, :, None, :] - a[:, :, None, :, :]
        pair = jnp.exp(jnp.where(causal, diff, 0.0)) * causal_f
        att = jnp.einsum('bhnd,bhmd,bhnmd->bhnm', qi, ki, pair)
        o = jnp.einsum('bhnm,bhme->bhne', att, vi) + jnp.einsum('bhnd,bhde->bhne', qi * jnp.exp(a), s)
        a_last = a[:, :, -1:, :]
        s = s * jnp.exp(a_last[:, :, 0, :, None]) + jnp.einsum('bhmd,bhme->bhde', ki * jnp.exp(a_last - a), vi)
        return s, o

    s, o = lax.scan(step, s0.astype(F32), (qc, kc, vc, gc))
    return from_chunks(o).astype(dtype), s

def ctx_attention(q, k, v):
    B, L, H, hd = q.shape
    nb = L // CTX_QBLOCK
    qb = q.reshape(B, nb, CTX_QBLOCK, H, hd).transpose(1, 0, 2, 3, 4)

    def blk(qi):
        s = jnp.einsum('bqhd,bkhd->bhqk', qi, k).astype(F32) * (hd ** -0.5)
        p = jax.nn.softmax(s, axis=-1).astype(v.dtype)
        return jnp.einsum('bhqk,bkhd->bqhd', p, v)

    o = lax.map(blk, qb)
    return o.transpose(1, 0, 2, 3, 4).reshape(B, L, H, hd)

def na_latent(q, k, v, k_ctx, v_ctx, rpb):
    B, T, H, hd = q.shape
    rows = T // GRID_W
    kr = min(NA_ROWS, rows)
    ncb = GRID_W // NA_QBLOCK
    scale = hd ** -0.5
    qcol = np.arange(GRID_W)
    cs = np.clip(qcol - NA_COLS // 2, 0, GRID_W - NA_COLS).reshape(ncb, NA_QBLOCK)
    kstart = np.clip(np.arange(ncb) * NA_QBLOCK - NA_COLS // 2, 0, GRID_W - NA_KBLOCK)
    kcol = kstart[:, None] + np.arange(NA_KBLOCK)
    qcol_b = qcol.reshape(ncb, NA_QBLOCK)
    col_ok = (kcol[:, None, :] >= cs[:, :, None]) & (kcol[:, None, :] < cs[:, :, None] + NA_COLS)
    col_off = np.clip(kcol[:, None, :] - qcol_b[:, :, None] + NA_COLS - 1, 0, 2 * NA_COLS - 2)
    kgc = k.reshape(B, rows, GRID_W, H, hd)[:, :, kcol]
    vgc = v.reshape(B, rows, GRID_W, H, hd)[:, :, kcol]
    q_rows = q.reshape(B, rows, ncb, NA_QBLOCK, H, hd).transpose(1, 0, 2, 3, 4, 5)
    nloc = kr * NA_KBLOCK

    def row_fn(args):
        r, q_r = args
        rs = jnp.clip(r - kr // 2, 0, rows - kr)
        k_r = lax.dynamic_slice_in_dim(kgc, rs, kr, axis=1)
        v_r = lax.dynamic_slice_in_dim(vgc, rs, kr, axis=1)
        row_off = rs + jnp.arange(kr) - r + (NA_ROWS - 1)
        bias = rpb[:, row_off][:, :, col_off].transpose(0, 2, 3, 1, 4)
        s_loc = jnp.einsum('bjqhd,bijchd->bhjqic', q_r, k_r).astype(F32) * scale + bias[None].astype(F32)
        s_loc = jnp.where(col_ok[None, None, :, :, None, :], s_loc, NEG_INF)
        s_ctx = jnp.einsum('bjqhd,bphd->bhjqp', q_r, k_ctx).astype(F32) * scale
        logits = jnp.concatenate([s_loc.reshape(s_loc.shape[:4] + (nloc,)), s_ctx], axis=-1)
        prob = jax.nn.softmax(logits, axis=-1).astype(v_r.dtype)
        p_loc = prob[..., :nloc].reshape(s_loc.shape)
        o = (jnp.einsum('bhjqic,bijchd->bjqhd', p_loc, v_r)
             + jnp.einsum('bhjqp,bphd->bjqhd', prob[..., nloc:], v_ctx))
        return o.reshape(B, GRID_W, H, hd)

    o = lax.map(row_fn, (jnp.arange(rows), q_rows))
    return o.transpose(1, 0, 2, 3, 4).reshape(B, T, H, hd)

def hg_logf(z, lb):
    f = lb + (1.0 - lb) * jax.nn.sigmoid(z.astype(F32))
    return jnp.log(jnp.maximum(f, F_MIN))

def token_mixers(h, l, P, hg_lower, cache):
    B, T, _ = h.shape
    u = h @ P['w_in'][l]
    rq, rk, rv, rg, nq, nk, nv, hq, hf_f, hf_b, hi, hgate, mg = jnp.split(u, SPLITS, axis=-1)
    latent = cache is not None
    if latent:
        k_ctx, v_ctx, s_ret0, s_hg0 = cache
    else:
        s_ret0 = jnp.zeros((B, 2, RET_HEADS, RET_DK, RET_DV), F32)
        s_hg0 = jnp.zeros((B, 2, HG_HEADS, HG_DK, HG_DV), F32)

    q = heads(rq, RET_HEADS)
    k = heads(rk, RET_HEADS) * (RET_DK ** -0.5)
    v = heads(rv, RET_HEADS)
    if latent:
        q, k = rope_2d(q), rope_2d(k)
    lg = jax.nn.log_sigmoid(P['ret_decay'][l].astype(F32))
    o_f, sr_f = retention_scan(q, k, v, lg[0], s_ret0[:, 0])
    o_b, sr_b = retention_scan(flip(q), flip(k), flip(v), lg[1], s_ret0[:, 1])
    ret_o = head_layernorm(o_f + flip(o_b)).reshape(B, T, BR_WIDTH) * jax.nn.silu(rg)

    na_q, na_k, na_v = heads(nq, NA_HEADS), heads(nk, NA_HEADS), heads(nv, NA_HEADS)
    if latent:
        na = na_latent(na_q, na_k, na_v, k_ctx, v_ctx, P['na_rpb'][l])
    else:
        na = ctx_attention(na_q, na_k, na_v)
    na_o = na.reshape(B, T, BR_WIDTH)

    lb = hg_lower[l]
    lf_f = heads(hg_logf(hf_f, lb[0]), HG_HEADS)
    lf_b = flip(heads(hg_logf(hf_b, lb[1]), HG_HEADS))
    gq = heads(jax.nn.silu(hq), HG_HEADS)
    gi = heads(hi, HG_HEADS)
    o_f, sh_f = hgrn2_scan(gq, -jnp.expm1(lf_f), gi, lf_f, s_hg0[:, 0])
    o_b, sh_b = hgrn2_scan(flip(gq), -jnp.expm1(lf_b), flip(gi), lf_b, s_hg0[:, 1])
    hg_o = rmsnorm(o_f + flip(o_b), P['hg_norm'][l].reshape(HG_HEADS, HG_DV)).reshape(B, T, BR_WIDTH) * jax.nn.silu(hgate)

    br = jnp.stack([ret_o, na_o, hg_o], axis=0)
    proj = jnp.einsum('nbtw,nwd->btnd', br, P['w_br'][l])
    gates = jax.nn.sigmoid(mg.reshape(B, T, N_BRANCH, D_MODEL))
    out = jnp.sum(gates * proj, axis=2) @ P['w_o'][l]
    if latent:
        return out, None
    return out, (na_k, na_v, jnp.stack([sr_f, sr_b], axis=1), jnp.stack([sh_f, sh_b], axis=1))

def swiglu(h, w_gu, w_down):
    a, b = jnp.split(h @ w_gu, 2, axis=-1)
    return (jax.nn.silu(a) * b) @ w_down

def moe(h, w_router, w_gu, w_down):
    logits = (h @ w_router).astype(F32)
    top_v, top_i = lax.top_k(logits, TOP_K)
    top_w = jax.nn.softmax(top_v, axis=-1)
    gate = jnp.sum(jax.nn.one_hot(top_i, N_EXPERTS, dtype=F32) * top_w[..., None], axis=-2).astype(h.dtype)
    out = jnp.zeros_like(h)
    for e in range(N_EXPERTS):
        out = out + gate[..., e:e + 1] * swiglu(h, w_gu[e], w_down[e])
    return out

def trunk_layer(x, cvec, l, P, hg_lower, cache):
    mod = jax.nn.silu(cvec) @ P['w_mod'][l] + P['b_mod'][l]
    mod = mod.reshape(cvec.shape[0], 1, N_MOD, D_MODEL)
    g = P['norm_g'][l]
    h = rmsnorm(x, g[0]) * (1.0 + mod[:, :, 1]) + mod[:, :, 0]
    m, ctx = token_mixers(h, l, P, hg_lower, cache)
    x = x + mod[:, :, 2] * rmsnorm(m, g[1])
    h = rmsnorm(x, g[2]) * (1.0 + mod[:, :, 4]) + mod[:, :, 3]
    if l % 2 == 0:
        f = swiglu(h, P['w_ffn_gu'][l // 2], P['w_ffn_down'][l // 2])
    else:
        f = moe(h, P['w_router'][l // 2], P['w_exp_gu'][l // 2], P['w_exp_down'][l // 2])
    x = x + mod[:, :, 5] * rmsnorm(f, g[3])
    return x, ctx

def setup_inputs(seed: int = 0) -> dict:
    key = jax.random.key(seed)
    ks = jax.random.split(key, 24)
    D, W = D_MODEL, BR_WIDTH

    def n(k, shape, s):
        return s * jax.random.normal(k, shape, F32)

    hh = jnp.arange(RET_HEADS, dtype=F32)
    gamma_logit = jnp.log1p(-(2.0 ** (-5.0 - hh))) + (5.0 + hh) * jnp.log(2.0)
    return {
        'x_prompt': n(ks[0], (BATCH, SEQ, D), 1.0),
        'x_sample': n(ks[1], (DEC_BATCH, DEC_SEQ, D), 1.0),
        'c': n(ks[2], (DEC_BATCH, D), 1.0),
        'cache_na_k': n(ks[3], (DEC_BATCH, DEPTH, PAST_LEN, NA_HEADS, NA_HD), 1.0),
        'cache_na_v': n(ks[4], (DEC_BATCH, DEPTH, PAST_LEN, NA_HEADS, NA_HD), 1.0),
        'state_ret': n(ks[5], (DEC_BATCH, DEPTH, 2, RET_HEADS, RET_DK, RET_DV), 1.0),
        'state_hgrn': n(ks[6], (DEC_BATCH, DEPTH, 2, HG_HEADS, HG_DK, HG_DV), 0.5),
        'c_ctx': n(ks[7], (D,), 1.0),
        'w_mod': n(ks[8], (DEPTH, D, N_MOD * D), 0.5 * D ** -0.5),
        'b_mod': n(ks[9], (DEPTH, N_MOD * D), 0.02),
        'norm_g': 1.0 + n(ks[10], (DEPTH, 4, D), 0.02),
        'w_in': n(ks[11], (DEPTH, D, D_IN), D ** -0.5),
        'ret_decay': gamma_logit + n(ks[12], (DEPTH, 2, RET_HEADS), 0.1),
        'na_rpb': n(ks[13], (DEPTH, NA_HEADS, 2 * NA_ROWS - 1, 2 * NA_COLS - 1), 0.1),
        'hg_lb': n(ks[14], (DEPTH, 2, HG_HEADS * HG_DK), 0.1),
        'hg_norm': 1.0 + n(ks[15], (DEPTH, HG_HEADS * HG_DV), 0.02),
        'w_br': n(ks[16], (DEPTH, N_BRANCH, W, D), W ** -0.5),
        'w_o': n(ks[17], (DEPTH, D, D), D ** -0.5),
        'w_ffn_gu': n(ks[18], (N_DENSE, D, 2 * D_FF), D ** -0.5),
        'w_ffn_down': n(ks[19], (N_DENSE, D_FF, D), D_FF ** -0.5),
        'w_router': n(ks[20], (N_MOE, D, N_EXPERTS), D ** -0.5),
        'w_exp_gu': n(ks[21], (N_MOE, N_EXPERTS, D, 2 * D_FF), D ** -0.5),
        'w_exp_down': n(ks[22], (N_MOE, N_EXPERTS, D_FF, D), D_FF ** -0.5),
    }

def reference(x_prompt, x_sample, c, cache_na_k, cache_na_v, state_ret, state_hgrn, c_ctx, w_mod, b_mod, norm_g,
              w_in, ret_decay, na_rpb, hg_lb, hg_norm, w_br, w_o, w_ffn_gu, w_ffn_down, w_router, w_exp_gu, w_exp_down):
    P = dict(w_mod=w_mod, b_mod=b_mod, norm_g=norm_g, w_in=w_in, ret_decay=ret_decay, na_rpb=na_rpb,
             hg_norm=hg_norm, w_br=w_br, w_o=w_o, w_ffn_gu=w_ffn_gu, w_ffn_down=w_ffn_down,
             w_router=w_router, w_exp_gu=w_exp_gu, w_exp_down=w_exp_down)
    p_lb = jax.nn.softmax(hg_lb.astype(F32), axis=0)
    hg_lower = jnp.cumsum(p_lb, axis=0) - p_lb[:1]

    x = x_prompt
    ks_l, vs_l, sr_l, sh_l = [], [], [], []
    for l in range(DEPTH):
        x, (k_l, v_l, s_r, s_h) = trunk_layer(x, c_ctx[None], l, P, hg_lower, None)
        ks_l.append(k_l)
        vs_l.append(v_l)
        sr_l.append(s_r)
        sh_l.append(s_h)
    y_prompt = x
    new_cache_na_k = jnp.stack(ks_l, axis=1)
    new_cache_na_v = jnp.stack(vs_l, axis=1)
    new_state_ret = jnp.stack(sr_l, axis=1)
    new_state_hgrn = jnp.stack(sh_l, axis=1)

    x = x_sample
    for l in range(DEPTH):
        cache = (cache_na_k[:, l], cache_na_v[:, l], state_ret[:, l], state_hgrn[:, l])
        x, _ = trunk_layer(x, c, l, P, hg_lower, cache)
    y_sample = x
    return (y_prompt, y_sample, new_cache_na_k, new_cache_na_v, new_state_ret, new_state_hgrn)


_drawn_inputs = setup_inputs


def setup_inputs(seed=0):
    import zlib

    import numpy as np

    out = dict(_drawn_inputs(seed))
    spreads = {}
    factors = {}
    for name, (base, spread) in spreads.items():
        noise = np.random.default_rng([zlib.crc32(name.encode()), seed]).standard_normal(out[name].shape)
        drawn = base * np.exp(spread * noise) if base else spread * noise
        out[name] = jnp.asarray(drawn.astype(out[name].dtype))
    for name, factor in factors.items():
        out[name] = (out[name] * factor).astype(out[name].dtype)
    return out
```

```python
from contextlib import ExitStack

import numpy as np

import concourse.bass as bass
from concourse import mybir

F32 = mybir.dt.float32
I32 = mybir.dt.int32
U32 = mybir.dt.uint32
ALU = mybir.AluOpType
ACT = mybir.ActivationFunctionType
AX_X = mybir.AxisListType.X

P = 128
D = 1024
KD = D // P
W = 512
H = 4
HD = W // H
L = 2
E = 8
FF = 2816
FS = 256
NFS = FF // FS
NMOD = 48
NWIN = 18
GRID_W, NA_COLS = 64, 16
EPS, F_MIN = 1e-6, 1e-30
SLOTS = 3
SLAB = KD * 2 * FS + 2 * D
NLEV = 7

CONST_W = {"ident": P, "cos": HD, "sin": HD, "above": P, "below": P, "mask_above": P, "mask_below": P,
           "ramp_up": P, "ramp_down": P, "window": P, "iota8": 8, "half": 2, "age": 2, "ones": 1}
CONST_AT = {}
_at = 0
for _k, _n in CONST_W.items():
    CONST_AT[_k] = _at
    _at += _n
NCONST = _at

BR_AFTER = {13: 0, 15: 1, 17: 2}
STAGED = [0, 1, 4, 5, 7, 8, 9]


def layer_slabs(l):
    slabs = [("mod", l, i) for i in range(12)]
    for j in range(NWIN):
        slabs.append(("win", l, j))
        if j in BR_AFTER:
            slabs.append(("br", l, BR_AFTER[j]))
    return slabs + [("wo", l, 0), ("wo", l, 1), ("skip", l, 0)]


def ring_plan():
    uses, before, at, plan = [0] * SLOTS, [None] * SLOTS, 0, {}
    for l in range(L):
        todo = layer_slabs(l)
        if l == 0:
            todo += [("ffn", 0, i) for i in range(NFS)] + [("skip", 0, 1)]
        for key in todo:
            s = at % SLOTS
            at += 1
            if key[0] != "skip":
                plan[key] = (s, uses[s], before[s])
                uses[s] += 1
                before[s] = key
    assert at % SLOTS == 0 and 12 % SLOTS == 0
    return plan, uses, before


def program(nc, x, c_t, b_mod_t, norm_t, lb_t, decay, hgn, rpb, cache_kt, cache_v, s_ret, s_hg, router, consts, levels,
            w_mod, w_in, w_br, w_o, w_ff, y, new_k, new_v, new_ret, new_hg):
    plan, uses0, before0 = ring_plan()
    per_expert = [len(range(s, NFS, SLOTS)) for s in range(SLOTS)]

    with ExitStack() as ctx:
        def sb(name, width, dt=F32):
            return ctx.enter_context(nc.sbuf_tensor(name, [P, width], dt))[:, :]

        def sem(name):
            return ctx.enter_context(nc.semaphore(name))

        ring = [sb(f"ring{s}", SLAB) for s in range(SLOTS)]
        x_sb = sb("x_sb", 2 * D).rearrange("p (g c) -> p g c", g=2)
        hT = sb("hT", 2 * D).rearrange("p (g k t) -> p g k t", g=2, k=KD)
        wide = sb("wide", 2 * D)
        xn = wide.rearrange("p (g c) -> p g c", g=2)
        stage = wide.rearrange("p (b g c) -> p b g c", b=2, g=2)
        merged = xn
        rv_hi = sb("rv_hi", 2 * W).rearrange("p (g c) -> p g c", g=2)
        rg_hg = sb("rg_hg", 2 * W).rearrange("p (g c) -> p g c", g=2)
        nv = sb("nv", 2 * W).rearrange("p (g c) -> p g c", g=2)
        gate = sb("gate", 2 * D)
        gates = gate.rearrange("p (g c) -> p g c", g=2)
        q_dec = gate[:, 0:2 * W].rearrange("p (d h t) -> p d h t", d=2, h=H)
        decays = gate[:, 2 * W:3 * W].rearrange("p (h t) -> p h t", h=H)
        bias = gate[:, 3 * W:4 * W].rearrange("p (h t) -> p h t", h=H)
        u1 = sb("u1", 6 * D)
        u2 = sb("u2", 5 * D)
        ght = "p (g h t) -> p g h t"
        rqT, rkT = (u1[:, i * D:(i + 1) * D].rearrange(ght, g=2, h=H) for i in (0, 1))
        kdec = u1[:, 2 * D:3 * D].rearrange("p (d c) -> p d c", d=2)
        ratt = u1[:, 3 * D:4 * D].rearrange(ght, g=2, h=H)
        qdec = u1[:, 4 * D:5 * D].rearrange("p (d h t) -> p d h t", d=2, h=H)
        rope = u1[:, 5 * D:6 * D].rearrange("p (b c) -> p b c", b=2)
        nqT, nkT = (u2[:, i * D:(i + 1) * D].rearrange(ght, g=2, h=H) for i in (0, 1))
        lg1 = u2[:, 2 * D:3 * D].rearrange("p (h s t) -> p h s t", h=H, s=2)
        lg0 = u2[:, 3 * D:3 * D + W].rearrange("p (h t) -> p h t", h=H)
        pT0 = u2[:, 3 * D + W:4 * D].rearrange("p (h t) -> p h t", h=H)
        pT1 = u2[:, 4 * D:5 * D].rearrange("p (s h t) -> p s h t", s=2, h=H)
        hq, f_pre, f_suf, k_f, k_b, f_sufx = (u1[:, i * D:(i + 1) * D] for i in range(6))
        b_prex, q_lev, k_lev = (u2[:, i * D:(i + 1) * D] for i in range(3))
        hatt = u2[:, 4 * D:5 * D]
        act_s = u1[:, 0:2 * W].rearrange("p (t c) -> p t c", t=2)[:, :, 0:FS]
        act_v = u1[:, D:2 * D].rearrange("p (b t c) -> p b t c", b=2, t=2)
        act_T = u1[:, 2 * D:3 * D].rearrange("p (b t j m) -> p b t j m", b=2, t=2, j=2)
        ff_y = u1[:, 3 * D:5 * D].rearrange("p (t c) -> p t c", t=2)

        brT = sb("brT", 2 * D).rearrange("p (b g k t) -> p b g k t", b=2, g=2, k=4)
        br = sb("br", 2 * D).rearrange("p (b g c) -> p b g c", b=2, g=2)
        state0 = sb("state0", 2 * W).rearrange("p (d h c) -> p d h c", d=2, h=H)
        ckT = sb("ckT", W).rearrange("p (h t) -> p h t", h=H)
        cv = sb("cv", W)
        state_out = sb("state_out", 2 * W)
        level_mask = sb("level_mask", 8 * P, I32).rearrange("p (v t) -> p v t", v=8)
        con = sb("con", NCONST)
        hgn_sb = sb("hgn_sb", W)
        rout_w = sb("rout_w", KD * E).rearrange("p (k e) -> p k e", k=KD)
        cond = sb("cond", KD * 2).rearrange("p (k g) -> p k g", k=KD)
        bm = sb("bm", L * NMOD).rearrange("p (l n) -> p l n", l=L)
        ng = sb("ng", L * 4 * KD).rearrange("p (l n k) -> p l n k", l=L, n=4)
        modc = sb("modc", NMOD * 2).rearrange("p (m k g) -> p m k g", m=6, k=KD)
        lbr = sb("lbr", L * 8).rearrange("p (l n) -> p l n", l=L)
        lbw = sb("lbw", 6 * 8).rearrange("p (n c) -> p n c", n=6)
        lb = sb("lb", L * 8).rearrange("p (l n) -> p l n", l=L)
        olb = sb("olb", L * 8).rearrange("p (l n) -> p l n", l=L)
        dec = sb("dec", L * 8)
        lgw = sb("lgw", 2 * L * 8).rearrange("p (n c) -> p n c", n=2)
        lg = sb("lg", L * 8).rearrange("p (l d h) -> p l d h", l=L, d=2)
        kd = sb("kd", L * 8).rearrange("p (l d h) -> p l d h", l=L, d=2)
        ss = sb("ss", 4)
        ms = sb("ms", 2)
        rs = sb("rs", 2)
        bnst = sb("bnst", 8 * 6).rearrange("p (n c) -> p n c", n=8)
        mv = sb("mv", 8 * 2).rearrange("p (n c) -> p n c", n=8)
        hms = sb("hms", 8)
        hss = sb("hss", 8)
        hrs = sb("hrs", 8)
        negmax = sb("negmax", 8)
        psums = sb("psums", 8)
        pinv = sb("pinv", 8)
        rl = sb("rl", 2 * E).rearrange("p (g e) -> p g e", g=2)
        rmax = sb("rmax", 2 * 8).rearrange("p (g e) -> p g e", g=2)
        ridx = sb("ridx", 2 * 8, U32).rearrange("p (g e) -> p g e", g=2)
        rif = sb("rif", 2 * 8).rearrange("p (g e) -> p g e", g=2)
        rw = sb("rw", 2 * 8).rearrange("p (g e) -> p g e", g=2)
        rgate = sb("rgate", E * 2)
        r1 = sb("r1", 2 * E).rearrange("p (g e) -> p g e", g=2)

        ps = ctx.enter_context(nc.psum_tensor("ps", [P, 8, 512], F32))

        def con_(name):
            return con[:, CONST_AT[name]:CONST_AT[name] + CONST_W[name]]

        ident = con_("ident")

        s_const = sem("constants_loaded")
        s_x = sem("x_loaded")
        slab_in = [sem(f"slab_in{s}") for s in range(SLOTS)]
        s_bias = sem("bias_loaded")
        s_cache = sem("cache_loaded")
        s_sret = sem("state_ret_loaded")
        s_shg = sem("state_hgrn_loaded")
        s_hgn = sem("hgrn_norm_loaded")
        s_kout = sem("new_k_stored")
        s_vout = sem("new_v_stored")
        s_srout = sem("new_ret_stored")
        s_shout = sem("new_hgrn_stored")
        s_yout = sem("y_stored")

        cond_ready = sem("cond_ready")
        dve_step = sem("dve_step")
        act_step = sem("act_step")
        pool_step = sem("pool_step")
        lbexp_ready = sem("lbexp_ready")
        lbsub_ready = sem("lbsub_ready")
        decabs_ready = sem("decabs_ready")
        declog_ready = sem("declog_ready")
        lg_ready = sem("lg_ready")
        kdx_ready = sem("kdx_ready")
        kdexp_ready = sem("kdexp_ready")
        kd_ready = sem("kd_ready")
        mod_done = sem("mod_slab_done")
        mod_ready = sem("mod_ready")
        sq_ready = sem("sq_ready")
        ms_ready = sem("ms_ready")
        rs_ready = sem("rs_ready")
        xn_ready = sem("xn_ready")
        xt_done = sem("xt_done")
        ht_dve = sem("ht_dve")
        ht_act = sem("ht_act")
        x_new = sem("x_new")
        win_done = sem("win_done")
        win_read = sem("win_read")
        exps_ready = sem("decay_exps_ready")
        decays_ready = sem("decays_ready")
        bias_ready = sem("bias_ready")
        rope_ready = sem("rope_ready")
        t_done = sem("turned")
        t_read_dve = sem("turned_read_dve")
        t_read_act = sem("turned_read_act")
        ratt_done = sem("ratt_done")
        ratt_ready = sem("ratt_ready")
        qdec_ready = sem("qdec_ready")
        kdec_ready = sem("kdec_ready")
        ro_done = sem("ro_done")
        ve_ready = sem("ve_ready")
        rsr_ready = sem("rsr_ready")
        ro_read = sem("ro_read")
        br_ready = sem("br_ready")
        rst_done = sem("ret_state_done")
        rst_read = sem("ret_state_read")
        na1_done = sem("na1_done")
        na1_read = sem("na1_read")
        na0_done = sem("na0_done")
        na0_read = sem("na0_read")
        max1_ready = sem("max1_ready")
        max0_ready = sem("max0_ready")
        p1_ready = sem("p1_ready")
        p0_ready = sem("p0_ready")
        pt1_done = sem("pt1_done")
        pt1_read = sem("pt1_read")
        pt0_done = sem("pt0_done")
        pt0_read = sem("pt0_read")
        pv_done = sem("pv_done")
        brt_done = sem("brt_done")
        brt_read = sem("brt_read")
        lev_ready = sem("lev_ready")
        lev_done = sem("lev_done")
        lev_read = sem("lev_read")
        qk_end = sem("state_products_ready")
        ho_done = sem("ho_done")
        hsq_ready = sem("hsq_ready")
        hms_ready = sem("hms_ready")
        hrs_ready = sem("hrs_ready")
        ks_done = sem("ks_done")
        ks_read = sem("ks_read")
        hst_done = sem("hgrn_state_done")
        hst_read = sem("hgrn_state_read")
        pr_done = sem("proj_done")
        pr_read = sem("proj_read")
        merged_ready = sem("merged_ready")
        mt_done = sem("merged_turned")
        mt_read = sem("merged_T_ready")
        wo_done = sem("wo_done")
        post_read = sem("post_scaled")
        gb_done = sem("gate_rows_done")
        gu_done = sem("gu_done")
        sil_ready = sem("silu_ready")
        act_ready = sem("act_ready")
        at_done = sem("act_turned")
        actT_ready = sem("act_T_ready")
        down_done = sem("down_done")
        acc_read = sem("ffn_acc_read")
        rlog_done = sem("router_done")
        rcopy_ready = sem("router_read")
        rdiff_ready = sem("router_diff_ready")
        rexp_ready = sem("router_exp_ready")

        block = ctx.enter_context(nc.Block())

        def released(key):
            kind, l, i = key
            return {"mod": (mod_done, 12 * l + i + 1), "win": (win_done, NWIN * l + i + 1),
                    "br": (pr_done, 6 * l + 2 * i + 2), "wo": (wo_done, 2 * l + i + 1),
                    "ffn": (down_done, i + 1)}[kind]

        @block.sync
        def _(sp):
            source = {"mod": w_mod, "win": w_in, "br": w_br, "wo": w_o, "ffn": w_ff}

            def load(key):
                s, _, before = plan[key]
                if before is not None:
                    sp.wait_ge(*released(before))
                src = source[key[0]][key[1], key[2]]
                sp.dma_start(ring[s][:, 0:src.shape[1]], src).then_inc(slab_in[s], 16)

            def load_expert(e, i):
                sp.dma_start(ring[i % SLOTS], w_ff[e + 1, i]).then_inc(slab_in[i % SLOTS], 16)

            for l in range(L):
                for i in range(SLOTS):
                    load(("mod", l, i))
                with sp.Fori(1, 12 // SLOTS) as t:
                    for s in range(SLOTS):
                        sp.wait_ge(mod_done, t * SLOTS + (12 * l + s - SLOTS + 1))
                        sp.dma_start(ring[s][:, 0:KD * 512], w_mod[l, t * SLOTS + s]).then_inc(slab_in[s], 16)
                for key in layer_slabs(l)[12:]:
                    if key[0] != "skip":
                        load(key)
                if l == 0:
                    for i in range(NFS):
                        load(("ffn", 0, i))
            for s in range(SLOTS):
                sp.wait_ge(*released(before0[s]))
                load_expert(0, s)

            def rest_of(e):
                for i in range(SLOTS, NFS):
                    sp.wait_ge(down_done, e * NFS + (NFS + i - SLOTS + 1))
                    load_expert(e, i)

            with sp.Fori(0, E - 1) as e:
                rest_of(e)
                for s in range(SLOTS):
                    sp.wait_ge(down_done, e * NFS + (NFS + max(i for i in range(NFS) if i % SLOTS == s) + 1))
                    load_expert(e + 1, s)
            rest_of(E - 1)
            for q in (s_kout, s_vout, s_srout, s_shout):
                sp.wait_ge(q, 16 * L)
            sp.wait_ge(s_yout, 16)

        @block.gpsimd
        def _(pool):
            for dst, src in ((con, consts), (cond, c_t), (bm, b_mod_t), (ng, norm_t), (lbr, lb_t), (dec, decay),
                             (rout_w, router), (level_mask, levels)):
                pool.dma_start(dst, src).then_inc(s_const, 16)
            pool.dma_start(x_sb, x).then_inc(s_x, 16)

            def power(out, in_, done, n):
                pool.tensor_tensor(out, in_, con_("half")[:, 0:1].broadcast_to([P, n]), ALU.pow).then_inc(done, 1)

            for l in range(L):
                if l:
                    pool.wait_ge(pr_read, 6 * l)
                pool.dma_start(bias, rpb[l]).then_inc(s_bias, 16)
                if l:
                    pool.wait_ge(pv_done, l)
                    pool.wait_ge(ho_done, l)
                pool.dma_start(ckT, cache_kt[l]).then_inc(s_cache, 16)
                pool.dma_start(cv, cache_v[l]).then_inc(s_cache, 16)
                pool.dma_start(state0, s_ret[l]).then_inc(s_sret, 16)
                if l:
                    pool.wait_ge(br_ready, 3 * l)
                pool.dma_start(hgn_sb, hgn[l]).then_inc(s_hgn, 16)
                if l == 0:
                    pool.wait_ge(s_const, 16 * 8)
                pool.wait_ge(ms_ready, 4 * l + 1)
                power(rs, ms, rs_ready, 2)
                pool.wait_ge(kd_ready, 1)
                pool.wait_ge(win_read, NWIN * l + 2)
                for d in range(2):
                    for h in range(H):
                        last = pool.tensor_scalar(kdec[:, d, h * HD:(h + 1) * HD], stage[:, 1, 0, h * HD:(h + 1) * HD],
                                                  kd[:, l, d, h:h + 1], None, ALU.mult)
                last.then_inc(kdec_ready, 1)
                pool.wait_ge(ve_ready, l + 1)
                power(hrs, hms, rsr_ready, 8)
                pool.wait_ge(win_read, NWIN * l + 6)
                pool.dma_start(new_k[l], stage[:, 1, 0, :]).then_inc(s_kout, 16)
                pool.wait_ge(win_read, NWIN * l + 7)
                pool.dma_start(new_v[l], nv[:, 0, :]).then_inc(s_vout, 16)
                pool.wait_ge(rst_read, l + 1)
                pool.dma_start(new_ret[l], state_out).then_inc(s_srout, 16)
                pool.wait_ge(ro_done, l + 1)
                pool.dma_start(state0, s_hg[l]).then_inc(s_shg, 16)
                pool.wait_ge(hms_ready, l + 1)
                power(hrs, hms, hrs_ready, 8)
                pool.wait_ge(hst_read, l + 1)
                pool.dma_start(new_hg[l], state_out).then_inc(s_shout, 16)
                for n in (1, 2, 3):
                    pool.wait_ge(ms_ready, 4 * l + n + 1)
                    power(rs, ms, rs_ready, 2)
            pool.wait_ge(x_new, 2 * L)
            pool.dma_start(y, x_sb).then_inc(s_yout, 16)

        @block.scalar
        def _(act):
            A = nc.scalar.activation
            chain = [0]

            def link(ins):
                chain[0] += 1
                ins.then_inc(act_step, 1)
                act.wait_ge(act_step, chain[0])

            act.wait_ge(s_const, 16 * 8)
            A(cond, cond, ACT.Silu).then_inc(cond_ready, 1)
            act.wait_ge(lbsub_ready, 1)
            A(lbw[:, 1:3, :], lbw[:, 1:3, :], ACT.Exp).then_inc(lbexp_ready, 1)
            act.wait_ge(decabs_ready, 1)
            link(A(lgw[:, 0, :], lgw[:, 0, :], ACT.Exp, scale=-1.0))
            A(lgw[:, 0, :], lgw[:, 0, :], ACT.Ln, bias=con_("ones")).then_inc(declog_ready, 1)
            act.wait_ge(kdx_ready, 1)
            A(kd, kd, ACT.Exp).then_inc(kdexp_ready, 1)

            def squares_x(l, n):
                if n == 0 and l == 0:
                    act.wait_ge(s_x, 16)
                else:
                    act.wait_ge(x_new, 2 * l + (n == 2))
                for g in range(2):
                    ins = A(xn[:, g, :], x_sb[:, g, :], ACT.Square, accum_out=ss[:, g:g + 1])
                ins.then_inc(sq_ready, 1)

            def turn_read(l, n):
                w = 4 * l + 2 * (n == 2)
                for g in range(2):
                    act.wait_ge(xt_done, w + g + 1)
                    for k in range(4, KD):
                        m = 0 if n == 0 else 3
                        ins = A(hT[:, g, k, :], ps[:, 5 + 2 * g, (k - 4) * P:(k - 3) * P], ACT.Identity,
                                scale=modc[:, m + 1, k, g:g + 1], bias=modc[:, m, k, g:g + 1])
                    ins.then_inc(ht_act, 1)

            def post_norm(l, n, src):
                for g in range(2):
                    ins = A(xn[:, g, :], src[g], ACT.Square, accum_out=ss[:, g:g + 1])
                ins.then_inc(sq_ready, 1)
                act.wait_ge(rs_ready, 4 * l + n + 1)
                for g in range(2):
                    ins = A(xn[:, g, :], src[g], ACT.Copy, scale=rs[:, g:g + 1])
                ins.then_inc(post_read, 1)

            def softmax(l, lgt, off, done, ready):
                act.wait_ge(done, l + 1)
                for h in range(H):
                    v = lgt[:, h] if off else lgt[:, h, :]
                    v = v.rearrange("p s t -> p (s t)") if off else v
                    ins = A(v, v, ACT.Exp, bias=negmax[:, off + h:off + h + 1],
                            accum_out=psums[:, off + h:off + h + 1])
                ins.then_inc(ready, 1)

            def panel(l, j):
                act.wait_ge(win_done, NWIN * l + j + 1)
                func = ACT.Copy
                if j in STAGED:
                    q = STAGED.index(j)
                    if q >= 2:
                        act.wait_ge(t_done, 7 * l + q - 1)
                    if q == 3:
                        act.wait_ge(kdec_ready, l + 1)
                    if q == 5:
                        act.wait_ge(s_kout, 16 * (l + 1))
                    dst = [stage[:, q % 2, g, :] for g in range(2)]
                    if j == 7:
                        func = ACT.Silu
                elif j in (2, 10):
                    dst = [rv_hi[:, g, :] for g in range(2)]
                elif j in (3, 11):
                    if j == 11:
                        act.wait_ge(br_ready, 3 * l + 1)
                    dst = [rg_hg[:, g, :] for g in range(2)]
                    func = ACT.Silu
                elif j == 6:
                    if l:
                        act.wait_ge(s_vout, 16 * l)
                    dst = [nv[:, g, :] for g in range(2)]
                else:
                    if j == 12:
                        act.wait_ge(na1_read, l + 1)
                    elif j > 13:
                        act.wait_ge(pr_read, 6 * l + j - 13)
                    o = 512 * (j % 2)
                    dst = [gates[:, g, o:o + 512] for g in range(2)]
                    func = ACT.Sigmoid
                for g in range(2):
                    ins = A(dst[g], ps[:, 2 * (j % 2) + g, :], func)
                ins.then_inc(win_read, 1)

            def ffn(tiles, base, first=0):
                for i in range(NFS + 1):
                    if i:
                        act.wait_ge(at_done, base + i)
                        A(act_T[:, (i - 1) % 2].rearrange("p t j m -> p t (j m)"), ps[:, 6:8, 0:FS], ACT.Copy)\
                            .then_inc(actT_ready, 1)
                    if i < NFS:
                        for t in range(tiles):
                            act.wait_ge(gu_done, 2 * base + 2 * i + t + 1)
                            if i:
                                act.wait_ge(act_ready, 2 * base + 2 * i + t - 1)
                            A(act_s[:, t, :], ps[:, 4 + t, 0:FS], ACT.Silu).then_inc(sil_ready, 1)

            for l in range(L):
                squares_x(l, 0)
                act.wait_ge(lg_ready, 1)
                if l:
                    act.wait_ge(pr_read, 6 * l)
                for d in range(2):
                    for h in range(H):
                        A(ratt[:, d, h, :], con_(("above", "below")[d]), ACT.Exp, scale=lg[:, l, d, h:h + 1])
                        ins = A(q_dec[:, d, h, :], con_(("ramp_up", "ramp_down")[d]), ACT.Exp,
                                scale=lg[:, l, d, h:h + 1])
                ins.then_inc(exps_ready, 1)
                act.wait_ge(mod_ready, l + 1)
                turn_read(l, 0)
                for j in range(NWIN):
                    panel(l, j)
                    if j == 6:
                        act.wait_ge(rst_done, l + 1)
                        if l:
                            act.wait_ge(s_shout, 16 * l)
                        A(state_out.rearrange("p (b c) -> p b c", b=2), ps[:, 4:6, :], ACT.Copy).then_inc(rst_read, 1)
                    if j == 8:
                        softmax(l, lg1, 4, max1_ready, p1_ready)
                    if j == 9:
                        softmax(l, lg0, 0, max0_ready, p0_ready)
                    if j in (9, 10):
                        q = j - 4
                        act.wait_ge(t_done, 7 * l + q + 1)
                        dst = (f_pre, f_suf)[q - 5].rearrange("p (g c) -> p g c", g=2)
                        A(dst, ps[:, 6:8, :], ACT.Sigmoid).then_inc(t_read_act, 1)
                act.wait_ge(ho_done, l + 1)
                for g in range(2):
                    for h in range(H):
                        ins = A(f_pre[:, (4 * g + h) * HD:(4 * g + h + 1) * HD], ps[:, 6 + g, h * HD:(h + 1) * HD], ACT.Square,
                                accum_out=hss[:, 4 * g + h:4 * g + h + 1])
                ins.then_inc(hsq_ready, 1)
                act.wait_ge(ks_done, l + 1)
                A(q_lev.rearrange("p (b c) -> p b c", b=2), ps[:, 4:6, :], ACT.Copy).then_inc(ks_read, 1)
                act.wait_ge(hst_done, l + 1)
                act.wait_ge(s_srout, 16 * (l + 1))
                A(state_out.rearrange("p (b c) -> p b c", b=2), ps[:, 4:6, :], ACT.Copy).then_inc(hst_read, 1)
                act.wait_ge(wo_done, 2 * l + 2)
                post_norm(l, 1, [ps[:, 2 * g:2 * g + 2, :].rearrange("p b c -> p (b c)") for g in range(2)])
                squares_x(l, 2)
                turn_read(l, 2)
                if l == 0:
                    ffn(2, 0)
                    act.wait_ge(down_done, NFS)
                    post_norm(l, 3, [ps[:, 2 * g:2 * g + 2, :].rearrange("p b c -> p (b c)") for g in range(2)])
                else:
                    act.wait_ge(rdiff_ready, 1)
                    A(rw[:, :, 1:2], rw[:, :, 1:2], ACT.Exp).then_inc(rexp_ready, 1)
                    with act.Fori(0, E) as e:
                        ffn(2, e * NFS + NFS)
                    act.wait_ge(acc_read, E + 1)
                    post_norm(l, 3, [ff_y[:, g, :] for g in range(2)])

        @block.tensor
        def _(pe):
            mm = nc.tensor.matmul

            def slab(key, blocks):
                s, u, _ = plan[key]
                pe.wait_ge(slab_in[s], 16 * (u + 1))
                return ring[s][:, 0:KD * 512].rearrange("p (k c) -> p k c", k=blocks)

            def modulation(l):
                if l == 0:
                    pe.wait_ge(cond_ready, 1)
                else:
                    pe.wait_ge(x_new, 2 * l)
                with pe.Fori(0, 12 // SLOTS) as t:
                    for s in range(SLOTS):
                        pe.wait_ge(slab_in[s], t * 16 + 16 * (plan[("mod", l, s)][1] + 1))
                        w = ring[s][:, 0:KD * 512].rearrange("p (k c) -> p k c", k=KD)
                        for c in range(4):
                            out = ps[:, 0, bass.ds(t * (8 * SLOTS) + (8 * s + 2 * c), 2)]
                            for k in range(KD):
                                ins = mm(out, w[:, k, c * P:(c + 1) * P], cond[:, k, :], start=(k == 0), stop=(k == KD - 1))
                        ins.then_inc(mod_done, 1)

            def turn_rows(l, n):
                w = 4 * l + 2 * (n == 2)
                for g in range(2):
                    pe.wait_ge(xn_ready, w + g + 1)
                    for k in range(KD):
                        ins = nc.tensor.transpose(ps[:, 4 + 2 * g + k // 4, (k % 4) * P:(k % 4 + 1) * P],
                                                  xn[:, g, k * P:(k + 1) * P], ident)
                    ins.then_inc(xt_done, 1)

            def panel(l, j):
                w = slab(("win", l, j), KD)
                if j == 0:
                    pe.wait_ge(ht_dve, 4 * l + 2)
                    pe.wait_ge(ht_act, 4 * l + 2)
                    pe.wait_ge(mod_ready, l + 1)
                elif j >= 2:
                    pe.wait_ge(win_read, NWIN * l + j - 1)
                if j >= 14:
                    pe.wait_ge(pr_read, 6 * l + j - 13)
                for g in range(2):
                    for k in range(KD):
                        ins = mm(ps[:, 2 * (j % 2) + g, :], hT[:, g, k, :], w[:, k, :], start=(k == 0), stop=(k == KD - 1))
                ins.then_inc(win_done, 1)

            def turn_panel(l, q):
                pe.wait_ge(win_read, NWIN * l + STAGED[q] + 1)
                if q < 2:
                    pe.wait_ge(rope_ready, 2 * l + q + 1)
                if 1 <= q <= 5:
                    pe.wait_ge(t_read_dve, 5 * l + q)
                elif q == 6:
                    pe.wait_ge(t_read_act, 2 * l + 1)
                for g in range(2):
                    src = rope[:, 0, :] if (q < 2 and g == 1) else stage[:, q % 2, g, :]
                    for h in range(H):
                        ins = nc.tensor.transpose(ps[:, 6 + g, h * P:(h + 1) * P], src[:, h * HD:(h + 1) * HD], ident)
                ins.then_inc(t_done, 1)

            def turn_heads(l, n, src, bank):
                pe.wait_ge(br_ready, 3 * l + n + 1)
                for g in range(2):
                    for h in range(H):
                        ins = nc.tensor.transpose(ps[:, bank + g, h * P:(h + 1) * P], src[:, g, h * HD:(h + 1) * HD], ident)
                ins.then_inc(brt_done, 1)

            def level(l, v):
                pe.wait_ge(lev_ready, 8 * l + v + 1)
                if v == 0:
                    pe.wait_ge(t_read_act, 2 * l + 2)
                else:
                    pe.wait_ge(lev_read, 8 * l + v)
                q = hq if v == NLEV else q_lev
                for u in range(8):
                    ins = mm(ps[:, 6 + u // 4, (u % 4) * P:(u % 4 + 1) * P], k_lev[:, u * P:(u + 1) * P],
                             q[:, u * P:(u + 1) * P], start=True, stop=True)
                ins.then_inc(lev_done, 1)

            def project(l, n):
                w = slab(("br", l, n), 4)
                pe.wait_ge(brt_read, 3 * l + n + 1)
                pe.wait_ge(win_read, NWIN * l + 14 + 2 * n)
                for half in range(2):
                    for g in range(2):
                        for k in range(4):
                            ins = mm(ps[:, 2 * half + g, :], brT[:, n % 2, g, k, :], w[:, k, half * 512:(half + 1) * 512],
                                     start=(k == 0), stop=(k == 3))
                    ins.then_inc(pr_done, 1)

            def turn_merged(l):
                pe.wait_ge(merged_ready, l + 1)
                pe.wait_ge(hst_read, l + 1)
                for g in range(2):
                    for k in range(KD):
                        ins = nc.tensor.transpose(ps[:, 4 + 2 * g + k // 4, (k % 4) * P:(k % 4 + 1) * P],
                                                  merged[:, g, k * P:(k + 1) * P], ident)
                    ins.then_inc(mt_done, 1)

            def output(l):
                pe.wait_ge(mt_read, 2 * l + 2)
                pe.wait_ge(pr_read, 6 * l + 6)
                for half in range(2):
                    w = slab(("wo", l, half), KD)
                    for g in range(2):
                        for k in range(KD):
                            ins = mm(ps[:, 2 * g + half, :], hT[:, g, k, :], w[:, k, :], start=(k == 0), stop=(k == KD - 1))
                    ins.then_inc(wo_done, 1)

            def gate_rows(l, n, m):
                if n == 1:
                    pe.wait_ge(actT_ready, NFS if l == 0 else NFS * (E + 1))
                    pe.wait_ge(act_ready, 2 * (NFS if l == 0 else NFS * (E + 1)))
                for g in range(2):
                    for k in range(KD):
                        col = modc[:, m, k, g:g + 1].broadcast_to([P, P])
                        ins = mm(ps[:, 4 + 2 * g + k // 4, (k % 4) * P:(k % 4 + 1) * P], col, ident, start=True, stop=True)
                ins.then_inc(gb_done, 1)

            def ffn(tiles, base, slot_wait, acc_wait):
                for i in range(NFS + 1):
                    if i:
                        pe.wait_ge(act_ready, 2 * base + 2 * i)
                        for t in range(tiles):
                            for j in range(2):
                                ins = nc.tensor.transpose(ps[:, 6 + t, j * P:(j + 1) * P],
                                                          act_v[:, (i - 1) % 2, t, j * P:(j + 1) * P], ident)
                        ins.then_inc(at_done, 1)
                    if i < NFS:
                        slot_wait(i)
                        w = ring[i % SLOTS][:, 0:KD * 512].rearrange("p (k c) -> p k c", k=KD)
                        for t in range(tiles):
                            for k in range(KD):
                                ins = mm(ps[:, 4 + t, :], hT[:, t, k, :], w[:, k, :], start=(k == 0), stop=(k == KD - 1))
                            ins.then_inc(gu_done, 1)
                    if i:
                        w = ring[(i - 1) % SLOTS][:, KD * 512:SLAB].rearrange("p (k c) -> p k c", k=2)
                        pe.wait_ge(actT_ready, base + i)
                        if i == 1:
                            acc_wait()
                        for t in range(tiles):
                            for half in range(2):
                                for j in range(2):
                                    ins = mm(ps[:, 2 * t + half, :], act_T[:, (i - 1) % 2, t, j, :],
                                             w[:, j, half * 512:(half + 1) * 512],
                                             start=(i == 1 and j == 0), stop=(i == NFS and j == 1), skip_group_check=True)
                        ins.then_inc(down_done, 1)

            def pieces(l, j):
                if j in (1, 2, 5, 6, 8, 9, 10):
                    turn_panel(l, (1, 2, 5, 6, 8, 9, 10).index(j))
                if j == 3:
                    pe.wait_ge(t_read_dve, 5 * l + 2)
                    for g in range(2):
                        for h in range(H):
                            ins = mm(ps[:, 4 + g, h * P:(h + 1) * P], rkT[:, g, h, :], rqT[:, g, h, :], start=True, stop=True)
                    ins.then_inc(ratt_done, 1)
                if j == 4:
                    pe.wait_ge(ratt_ready, l + 1)
                    pe.wait_ge(qdec_ready, l + 1)
                    pe.wait_ge(s_sret, 16 * (l + 1))
                    pe.wait_ge(win_read, NWIN * l + 3)
                    for g in range(2):
                        for h in range(H):
                            out = ps[:, 4 + g, h * HD:(h + 1) * HD]
                            ins = mm(out, ratt[:, g, h, :], rv_hi[:, g, h * HD:(h + 1) * HD], start=True, stop=(g == 0))
                            if g:
                                mm(out, qdec[:, 0, h, :], state0[:, 0, h, :], start=False, stop=False)
                                ins = mm(out, qdec[:, 1, h, :], state0[:, 1, h, :], start=False, stop=True)
                    ins.then_inc(ro_done, 1)
                if j == 6:
                    pe.wait_ge(ro_read, l + 1)
                    pe.wait_ge(kdec_ready, l + 1)
                    for d in range(2):
                        for h in range(H):
                            ins = mm(ps[:, 4 + d, h * HD:(h + 1) * HD], kdec[:, d, h * HD:(h + 1) * HD],
                                     rv_hi[:, 0, h * HD:(h + 1) * HD], start=True, stop=True)
                    ins.then_inc(rst_done, 1)
                if j == 7:
                    pe.wait_ge(t_read_dve, 5 * l + 4)
                    pe.wait_ge(s_cache, 32 * (l + 1))
                    pe.wait_ge(rst_read, l + 1)
                    for s, keys in ((0, nkT[:, 1]), (1, ckT)):
                        for h in range(H):
                            ins = mm(ps[:, 4 + s, h * P:(h + 1) * P], nqT[:, 1, h, :], keys[:, h, :], start=True, stop=True)
                    ins.then_inc(na1_done, 1)
                if j == 8:
                    pe.wait_ge(na1_read, l + 1)
                    for h in range(H):
                        ins = mm(ps[:, 4, h * P:(h + 1) * P], nqT[:, 0, h, :], nkT[:, 0, h, :], start=True, stop=True)
                    ins.then_inc(na0_done, 1)
                if j == 9:
                    pe.wait_ge(p1_ready, l + 1)
                    pe.wait_ge(na0_read, l + 1)
                    for s in range(2):
                        for h in range(H):
                            ins = nc.tensor.transpose(ps[:, 4 + s, h * P:(h + 1) * P], lg1[:, h, s, :], ident)
                    ins.then_inc(pt1_done, 1)
                if j == 10:
                    pe.wait_ge(p0_ready, l + 1)
                    pe.wait_ge(pt1_read, l + 1)
                    for h in range(H):
                        ins = nc.tensor.transpose(ps[:, 4, h * P:(h + 1) * P], lg0[:, h, :], ident)
                    ins.then_inc(pt0_done, 1)
                if j == 11:
                    pe.wait_ge(pt0_read, l + 1)
                    for h in range(H):
                        hc = slice(h * HD, (h + 1) * HD)
                        mm(ps[:, 4, hc], pT0[:, h, :], nv[:, 0, hc], start=True, stop=True)
                    for h in range(H):
                        hc = slice(h * HD, (h + 1) * HD)
                        mm(ps[:, 5, hc], pT1[:, 0, h, :], nv[:, 1, hc], start=True, stop=False)
                        ins = mm(ps[:, 5, hc], pT1[:, 1, h, :], cv[:, hc], start=False, stop=True)
                    ins.then_inc(pv_done, 1)
                    level(l, 0)
                if j == 12:
                    pe.wait_ge(br_ready, 3 * l + 2)
                    turn_heads(l, 0, br[:, 0], 4)
                    level(l, 1)
                if j == 13:
                    pe.wait_ge(brt_read, 3 * l + 1)
                    turn_heads(l, 1, br[:, 1], 4)
                    level(l, 2)
                if j in (14, 15):
                    level(l, j - 10)
                if j == 16:
                    level(l, NLEV)
                if j == 17:
                    recurrence_out(l)

            def recurrence_out(l):
                pe.wait_ge(lev_read, 8 * l + 8)
                pe.wait_ge(qk_end, l + 1)
                pe.wait_ge(s_shg, 16 * (l + 1))
                for g in range(2):
                    for h in range(H):
                        hc = slice(h * HD, (h + 1) * HD)
                        u = 4 * g + h
                        ins = mm(ps[:, 6 + g, hc], hatt[:, u * P:(u + 1) * P], rv_hi[:, g, hc], start=True, stop=(g == 0))
                        if g:
                            mm(ps[:, 7, hc], q_lev[:, hc], state0[:, 0, h, :], start=False, stop=False)
                            ins = mm(ps[:, 7, hc], q_lev[:, W + h * HD:W + (h + 1) * HD], state0[:, 1, h, :],
                                     start=False, stop=True)
                ins.then_inc(ho_done, 1)
                pe.wait_ge(brt_read, 3 * l + 2)
                for d in range(2):
                    for h in range(H):
                        a = d * W + h * HD
                        ins = nc.tensor.transpose(ps[:, 4 + d, h * P:(h + 1) * P], k_lev[:, a:a + HD], ident)
                ins.then_inc(ks_done, 1)
                pe.wait_ge(ks_read, l + 1)
                for d in range(2):
                    for h in range(H):
                        hc = slice(h * HD, (h + 1) * HD)
                        ins = mm(ps[:, 4 + d, hc], q_lev[:, d * W + h * HD:d * W + (h + 1) * HD], rv_hi[:, 0, hc],
                                 start=True, stop=True)
                ins.then_inc(hst_done, 1)
                turn_heads(l, 2, br[:, 0], 6)

            for l in range(L):
                modulation(l)
                turn_rows(l, 0)
                for j in range(NWIN):
                    panel(l, j)
                    pieces(l, j)
                    if j in BR_AFTER:
                        project(l, BR_AFTER[j])
                        if j < NWIN - 1:
                            level(l, 3 if j == 13 else 6)
                turn_merged(l)
                output(l)
                gate_rows(l, 0, 2)
                turn_rows(l, 2)
                pe.wait_ge(ht_dve, 4 * l + 4)
                pe.wait_ge(ht_act, 4 * l + 4)
                if l == 0:
                    ffn(2, 0, lambda i: slab(("ffn", 0, i), KD), lambda: pe.wait_ge(post_read, 1))
                else:
                    for g in range(2):
                        for k in range(KD):
                            ins = mm(ps[:, 0, g * E:(g + 1) * E], hT[:, g, k, :], rout_w[:, k, :], start=(k == 0), stop=(k == KD - 1))
                    ins.then_inc(rlog_done, 1)
                    pe.wait_ge(rcopy_ready, 1)
                    with pe.Fori(0, E) as e:
                        ffn(2, e * NFS + NFS,
                            lambda i: pe.wait_ge(slab_in[i % SLOTS], e * (16 * per_expert[i % SLOTS])
                                                 + 16 * (uses0[i % SLOTS] + i // SLOTS + 1)),
                            lambda: pe.wait_ge(acc_read, e + 1))
                gate_rows(l, 1, 5)

        @block.vector
        def _(dve):
            V = nc.vector
            chain = [0]

            def link(ins):
                chain[0] += 1
                ins.then_inc(dve_step, 1)
                dve.wait_ge(dve_step, chain[0])

            def own(ins, s, value):
                ins.then_inc(s, 1)
                dve.wait_ge(s, value)

            dve.wait_ge(s_const, 16 * 8)
            link(V.tensor_tensor(lbw[:, 0, :], lbr[:, 0, :], lbr[:, 1, :], ALU.max))
            V.tensor_tensor(lbw[:, 1, :], lbr[:, 0, :], lbw[:, 0, :], ALU.subtract)
            V.tensor_tensor(lbw[:, 2, :], lbr[:, 1, :], lbw[:, 0, :], ALU.subtract).then_inc(lbsub_ready, 1)
            dve.wait_ge(lbexp_ready, 1)
            link(V.tensor_tensor(lbw[:, 3, :], lbw[:, 1, :], lbw[:, 2, :], ALU.add))
            link(V.reciprocal(lbw[:, 4, :], lbw[:, 3, :]))
            link(V.tensor_tensor(lbw[:, 1:3, :], lbw[:, 1:3, :], lbw[:, 4, :].unsqueeze(1).broadcast_to([P, 2, 8]), ALU.mult))
            V.tensor_tensor(lb[:, 0, :], lbw[:, 1, :], lbw[:, 1, :], ALU.subtract)
            link(V.tensor_tensor(lbw[:, 5, :], lbw[:, 1, :], lbw[:, 2, :], ALU.add))
            link(V.tensor_tensor(lb[:, 1, :], lbw[:, 5, :], lbw[:, 1, :], ALU.subtract))
            V.tensor_scalar(olb, lb, -1.0, 1.0, ALU.mult, ALU.add)
            V.scalar_tensor_tensor(lgw[:, 0, :], dec, -1.0, dec, ALU.mult, ALU.max).then_inc(decabs_ready, 1)
            dve.wait_ge(declog_ready, 1)
            lgf = lg.rearrange("p l d h -> p (l d h)")
            own(V.scalar_tensor_tensor(lgf, dec, 0.0, lgw[:, 0, :], ALU.min, ALU.subtract), lg_ready, 1)
            for d in range(2):
                ins = V.tensor_scalar(kd[:, :, d, :], lg[:, :, d, :], con_("age")[:, d:d + 1], None, ALU.mult)
            ins.then_inc(kdx_ready, 1)
            dve.wait_ge(kdexp_ready, 1)
            V.tensor_scalar(kd, kd, HD ** -0.5, None, ALU.mult).then_inc(kd_ready, 1)

            def mean_square(l, n):
                dve.wait_ge(sq_ready, 4 * l + n + 1)
                V.tensor_scalar(ms, ss[:, 0:2], 1.0 / D, EPS, ALU.mult, ALU.add).then_inc(ms_ready, 1)

            def rows(l, n):
                dve.wait_ge(rs_ready, 4 * l + n + 1)
                for g in range(2):
                    V.tensor_scalar(xn[:, g, :], x_sb[:, g, :], rs[:, g:g + 1], None, ALU.mult).then_inc(xn_ready, 1)

            def turn_read(l, n):
                w = 4 * l + 2 * (n == 2)
                m = 0 if n == 0 else 3
                for g in range(2):
                    dve.wait_ge(xt_done, w + g + 1)
                    for k in range(4):
                        ins = V.tensor_scalar(hT[:, g, k, :], ps[:, 4 + 2 * g, k * P:(k + 1) * P],
                                              modc[:, m + 1, k, g:g + 1], modc[:, m, k, g:g + 1], ALU.mult, ALU.add)
                    ins.then_inc(ht_dve, 1)

            def modulation(l):
                dve.wait_ge(mod_done, 12 * (l + 1))
                link(V.tensor_tensor(modc.rearrange("p m k g -> p (m k) g"),
                                     ps[:, 0, 0:2 * NMOD].rearrange("p (n g) -> p n g", g=2),
                                     bm[:, l, :].unsqueeze(2).broadcast_to([P, NMOD, 2]), ALU.add))
                for m, n in ((1, 0), (4, 2)):
                    V.scalar_tensor_tensor(modc[:, m], modc[:, m], 1.0, ng[:, l, n, :].unsqueeze(2).broadcast_to([P, KD, 2]),
                                           ALU.add, ALU.mult)
                for m, n in ((2, 1), (5, 3)):
                    ins = V.tensor_tensor(modc[:, m], modc[:, m], ng[:, l, n, :].unsqueeze(2).broadcast_to([P, KD, 2]), ALU.mult)
                ins.then_inc(mod_ready, 1)
                dve.wait_ge(mod_ready, l + 1)

            def rotate(l, q):
                dve.wait_ge(win_read, NWIN * l + q + 1)
                if q:
                    dve.wait_ge(t_done, 7 * l + 1)
                haf = dict(h=H, a=2, two=2)
                split = "p (h a two f) -> p h a two f"
                src = stage[:, q % 2, 1, :]
                V.tensor_tensor(rope[:, 0, :].rearrange("p (h c) -> p h c", h=H), src.rearrange("p (h c) -> p h c", h=H),
                                con_("cos").unsqueeze(1).broadcast_to([P, H, HD]), ALU.mult)
                sin = con_("sin").rearrange("p (a two f) -> p a two f", a=2, two=2)
                for two in range(2):
                    ins = V.tensor_tensor(rope[:, 1, :].rearrange(split, **haf)[:, :, :, two, :],
                                          src.rearrange(split, **haf)[:, :, :, 1 - two, :],
                                          sin[:, :, two, :].unsqueeze(1).broadcast_to([P, H, 2, HD // 4]), ALU.mult)
                link(ins)
                V.tensor_tensor(rope[:, 0, :], rope[:, 0, :], rope[:, 1, :], ALU.add).then_inc(rope_ready, 1)

            def turned(l, q, dst):
                dve.wait_ge(t_done, 7 * l + q + 1)
                V.tensor_copy(dst, ps[:, 6:8, :]).then_inc(t_read_dve, 1)

            def pair(v):
                return v.rearrange("p (b c) -> p b c", b=2)

            def retention(l):
                dve.wait_ge(ratt_done, l + 1)
                V.tensor_tensor(ratt.rearrange("p g h t -> p g (h t)"), ps[:, 4:6, :],
                                decays.rearrange("p h t -> p (h t)").unsqueeze(1).broadcast_to([P, 2, W]), ALU.mult)\
                    .then_inc(ratt_ready, 1)
                V.tensor_tensor(qdec.rearrange("p d h t -> p d (h t)"), q_dec.rearrange("p d h t -> p d (h t)"),
                                rqT[:, 1].rearrange("p h t -> p (h t)").unsqueeze(1).broadcast_to([P, 2, W]), ALU.mult)\
                    .then_inc(qdec_ready, 1)
                dve.wait_ge(ro_done, l + 1)
                for u in range(8):
                    ins = V.bn_stats(bnst[:, u, :], ps[:, 4 + u // 4, (u % 4) * HD:(u % 4 + 1) * HD])
                link(ins)
                for u in range(8):
                    ins = V.bn_aggr(mv[:, u, :], bnst[:, u, :])
                link(ins)
                V.tensor_scalar(hms, mv[:, :, 1], 1e-5, None, ALU.add).then_inc(ve_ready, 1)
                dve.wait_ge(rsr_ready, l + 1)
                for u in range(8):
                    hc = slice((u % 4) * HD, (u % 4 + 1) * HD)
                    ins = V.tensor_scalar(br[:, 0, u // 4, hc], ps[:, 4 + u // 4, hc], mv[:, u, 0:1], hrs[:, u:u + 1],
                                          ALU.subtract, ALU.mult)
                own(ins, ro_read, l + 1)
                dve.wait_ge(win_read, NWIN * l + 4)
                V.tensor_tensor(br[:, 0], br[:, 0], rg_hg, ALU.mult).then_inc(br_ready, 1)

            def logits1(l):
                dve.wait_ge(na1_done, l + 1)
                V.scalar_tensor_tensor(lg1[:, :, 0, :], ps[:, 4, :].rearrange("p (h t) -> p h t", h=H), HD ** -0.5, bias,
                                       ALU.mult, ALU.add)
                own(V.tensor_scalar(lg1[:, :, 1, :], ps[:, 5, :].rearrange("p (h t) -> p h t", h=H), HD ** -0.5, None, ALU.mult),
                    na1_read, l + 1)
                link(V.tensor_reduce(negmax[:, 4:8], lg1.rearrange("p h s t -> p h (s t)"), AX_X, ALU.max))
                V.tensor_scalar(negmax[:, 4:8], negmax[:, 4:8], -1.0, None, ALU.mult).then_inc(max1_ready, 1)

            def logits0(l):
                dve.wait_ge(na0_done, l + 1)
                own(V.tensor_scalar(lg0, ps[:, 4, :].rearrange("p (h t) -> p h t", h=H), HD ** -0.5, None, ALU.mult),
                    na0_read, l + 1)
                link(V.tensor_reduce(negmax[:, 0:4], lg0, AX_X, ALU.max))
                V.tensor_scalar(negmax[:, 0:4], negmax[:, 0:4], -1.0, None, ALU.mult).then_inc(max0_ready, 1)

            def attention_out(l):
                dve.wait_ge(p1_ready, l + 1)
                dve.wait_ge(p0_ready, l + 1)
                link(V.reciprocal(pinv, psums))
                dve.wait_ge(pv_done, l + 1)
                for u in range(8):
                    hc = slice((u % 4) * HD, (u % 4 + 1) * HD)
                    ins = V.tensor_scalar(br[:, 1, u // 4, hc], ps[:, 4 + u // 4, hc], pinv[:, u:u + 1], None, ALU.mult)
                ins.then_inc(br_ready, 1)

            def forget(l, d, f, k):
                dve.wait_ge(t_read_act, 2 * l + d + 1)
                for h in range(H):
                    v = f.rearrange("p (g h t) -> p g h t", g=2, h=H)[:, :, h, :]
                    c = 4 * d + h
                    ins = V.tensor_scalar(v, v, olb[:, l, c:c + 1], lb[:, l, c:c + 1], ALU.mult, ALU.add)
                link(ins)
                link(V.tensor_scalar(f, f, F_MIN, None, ALU.max))
                link(V.tensor_scalar(k, f, -1.0, 1.0, ALU.mult, ALU.add))

            def halves(v, s):
                w = v.rearrange("p (b two s) -> p b two s", two=2, s=s)
                return w[:, :, 0, :], w[:, :, 1, :]

            def products(l, v):
                if v:
                    dve.wait_ge(lev_done, 8 * l + v)
                if v == NLEV:
                    V.tensor_tensor(k_lev, k_f, k_b, ALU.add).then_inc(lev_ready, 1)
                    return
                s = 1 << v
                (ql, qr), (kl, kr), (hl, hr) = halves(q_lev, s), halves(k_lev, s), halves(hq, s)
                V.tensor_tensor(qr, hr, halves(f_pre, s)[1], ALU.mult)
                V.tensor_tensor(ql, hl, halves(f_suf, s)[0], ALU.mult)
                V.tensor_tensor(kl, halves(k_f, s)[0], halves(f_sufx, s)[0], ALU.mult)
                V.tensor_tensor(kr, halves(k_b, s)[1], halves(b_prex, s)[1], ALU.mult).then_inc(lev_ready, 1)
                shape = [P, 2 * D // (4 * s), s]
                (pl, pr), (sl, sr) = halves(f_pre, s), halves(f_suf, s)
                xl, xr = halves(f_sufx, s)[0], halves(b_prex, s)[1]
                V.tensor_tensor(xl, xl, pr[:, :, s - 1:s].broadcast_to(shape), ALU.mult)
                link(V.tensor_tensor(xr, xr, sl[:, :, 0:1].broadcast_to(shape), ALU.mult))
                V.tensor_tensor(pr, pr, pl[:, :, s - 1:s].broadcast_to(shape), ALU.mult)
                link(V.tensor_tensor(sl, sl, sr[:, :, 0:1].broadcast_to(shape), ALU.mult))

            def level_read(l, v):
                dve.wait_ge(lev_done, 8 * l + v + 1)
                V.copy_predicated(hatt.rearrange("p (u t) -> p u t", u=8),
                                  level_mask[:, v, :].unsqueeze(1).broadcast_to([P, 8, P]),
                                  ps[:, 6:8, :].rearrange("p b (h t) -> p (b h) t", h=H)).then_inc(lev_read, 1)

            def heads_turned(l, n, bank):
                dve.wait_ge(brt_done, 3 * l + n + 1)
                V.tensor_copy(brT[:, n % 2].rearrange("p g k t -> p g (k t)"), ps[:, bank:bank + 2, :]).then_inc(brt_read, 1)

            def gated(l, n):
                if n:
                    dve.wait_ge(brt_done, 3 * l + 2)
                dve.wait_ge(win_read, NWIN * l + 14 + 2 * n)
                for half in range(2):
                    dve.wait_ge(pr_done, 6 * l + 2 * n + half + 1)
                    cols = slice(half * 512, (half + 1) * 512)
                    src = ps[:, 2 * half:2 * half + 2, :]
                    dst = merged[:, :, cols] if n == 0 else br[:, 1]
                    ins = V.tensor_tensor(dst, src, gates[:, :, cols], ALU.mult)
                    own(ins, pr_read, 6 * l + 2 * n + half + 1)
                    if n:
                        ins = V.tensor_tensor(merged[:, :, cols], merged[:, :, cols], br[:, 1], ALU.add)
                        if n == 2 and half == 1:
                            ins.then_inc(merged_ready, 1)
                        else:
                            link(ins)

            def recurrence_out(l):
                V.tensor_tensor(q_lev[:, 0:W], hq[:, W:2 * W], f_pre[:, W:2 * W], ALU.mult)
                V.tensor_tensor(q_lev[:, W:2 * W], hq[:, W:2 * W], f_suf[:, W:2 * W], ALU.mult)
                dve.wait_ge(lev_done, 8 * l + 8)
                V.tensor_tensor(k_lev[:, 0:W], k_f[:, 0:W], f_sufx[:, 0:W], ALU.mult)
                V.tensor_tensor(k_lev[:, W:2 * W], k_b[:, 0:W], b_prex[:, 0:W], ALU.mult).then_inc(qk_end, 1)
                dve.wait_ge(win_read, NWIN * l + 12)
                dve.wait_ge(s_hgn, 16 * (l + 1))
                V.tensor_tensor(rg_hg, rg_hg, hgn_sb.unsqueeze(1).broadcast_to([P, 2, W]), ALU.mult)
                dve.wait_ge(hsq_ready, l + 1)
                V.tensor_scalar(hms, hss, 1.0 / HD, EPS, ALU.mult, ALU.add).then_inc(hms_ready, 1)
                dve.wait_ge(hrs_ready, l + 1)
                for u in range(8):
                    hc = slice((u % 4) * HD, (u % 4 + 1) * HD)
                    ins = V.scalar_tensor_tensor(br[:, 0, u // 4, hc], ps[:, 6 + u // 4, hc], hrs[:, u:u + 1],
                                                 rg_hg[:, u // 4, hc], ALU.mult, ALU.mult)
                ins.then_inc(br_ready, 1)

            def residual(l, n):
                mean_square(l, n)
                w = 2 * l + (n == 3) + 1
                dve.wait_ge(post_read, w)
                dve.wait_ge(gb_done, w)
                link(V.tensor_tensor(pair(wide).rearrange("p g (b c) -> p (g b) c", b=2),
                                     pair(wide).rearrange("p g (b c) -> p (g b) c", b=2), ps[:, 4:8, :], ALU.mult))
                own(V.tensor_tensor(x_sb, x_sb, xn, ALU.add), x_new, w)

            def ffn(tiles, base):
                for i in range(NFS):
                    for t in range(tiles):
                        dve.wait_ge(sil_ready, 2 * base + 2 * i + t + 1)
                        V.tensor_tensor(act_v[:, i % 2, t, :], act_s[:, t, :], ps[:, 4 + t, FS:2 * FS], ALU.mult)\
                            .then_inc(act_ready, 1)

            def routing():
                dve.wait_ge(rlog_done, 1)
                own(V.tensor_copy(rl.rearrange("p g e -> p (g e)"), ps[:, 0, 0:2 * E]), rcopy_ready, 1)
                for g in range(2):
                    link(V.max(rmax[:, g, :], rl[:, g, :]))
                for g in range(2):
                    ins = V.max_index(ridx[:, g, :], rmax[:, g, :], rl[:, g, :])
                V.tensor_tensor(rw[:, :, 1:2], rmax[:, :, 1:2], rmax[:, :, 0:1], ALU.subtract).then_inc(rdiff_ready, 1)
                dve.wait_ge(rexp_ready, 1)
                link(V.tensor_copy(rif, ridx))
                link(V.tensor_scalar(rw[:, :, 2:3], rw[:, :, 1:2], 1.0, None, ALU.add))
                link(V.reciprocal(rw[:, :, 3:4], rw[:, :, 2:3]))
                link(V.tensor_tensor(rw[:, :, 4:5], rw[:, :, 1:2], rw[:, :, 3:4], ALU.mult))
                rg = rgate.rearrange("p (e g) -> p g e", g=2)
                for g in range(2):
                    V.tensor_scalar(rg[:, g, :], con_("iota8"), rif[:, g, 0:1], rw[:, g, 3:4], ALU.is_equal, ALU.mult)
                    link(V.tensor_scalar(r1[:, g, :], con_("iota8"), rif[:, g, 1:2], rw[:, g, 4:5], ALU.is_equal, ALU.mult))
                link(V.tensor_tensor(rg, rg, r1, ALU.add))

            for l in range(L):
                mean_square(l, 0)
                dve.wait_ge(exps_ready, l + 1)
                for d, name in ((0, "mask_above"), (1, "mask_below")):
                    ins = V.tensor_tensor(ratt[:, d], ratt[:, d], con_(name).unsqueeze(1).broadcast_to([P, H, P]), ALU.mult)
                link(ins)
                V.tensor_tensor(decays, ratt[:, 0], ratt[:, 1], ALU.add)
                dve.wait_ge(s_bias, 16 * (l + 1))
                link(V.tensor_tensor(bias, bias, con_("window").unsqueeze(1).broadcast_to([P, H, P]), ALU.add))
                rows(l, 0)
                modulation(l)
                turn_read(l, 0)
                rotate(l, 0)
                turned(l, 0, pair(u1[:, 0:D]))
                rotate(l, 1)
                turned(l, 1, pair(u1[:, D:2 * D]))
                retention(l)
                V.memset(f_sufx, 1.0)
                turned(l, 2, pair(u2[:, 0:D]))
                turned(l, 3, pair(u2[:, D:2 * D]))
                logits1(l)
                turned(l, 4, pair(hq))
                logits0(l)
                V.memset(b_prex, 1.0)
                dve.wait_ge(pt1_done, l + 1)
                V.tensor_copy(pT1.rearrange("p s h t -> p s (h t)"), ps[:, 4:6, :]).then_inc(pt1_read, 1)
                forget(l, 0, f_pre, k_f)
                dve.wait_ge(pt0_done, l + 1)
                V.tensor_copy(pT0.rearrange("p h t -> p (h t)"), ps[:, 4, :]).then_inc(pt0_read, 1)
                forget(l, 1, f_suf, k_b)
                products(l, 0)
                attention_out(l)
                level_read(l, 0)
                products(l, 1)
                heads_turned(l, 0, 4)
                level_read(l, 1)
                products(l, 2)
                heads_turned(l, 1, 4)
                level_read(l, 2)
                products(l, 3)
                gated(l, 0)
                level_read(l, 3)
                products(l, 4)
                level_read(l, 4)
                products(l, 5)
                level_read(l, 5)
                products(l, 6)
                gated(l, 1)
                level_read(l, 6)
                products(l, NLEV)
                level_read(l, NLEV)
                recurrence_out(l)
                heads_turned(l, 2, 6)
                gated(l, 2)
                for g in range(2):
                    dve.wait_ge(mt_done, 2 * l + g + 1)
                    V.tensor_copy(hT[:, g].rearrange("p (b k) t -> p b (k t)", b=2), ps[:, 4 + 2 * g:6 + 2 * g, :])\
                        .then_inc(mt_read, 1)
                residual(l, 1)
                mean_square(l, 2)
                rows(l, 2)
                turn_read(l, 2)
                if l == 0:
                    ffn(2, 0)
                else:
                    routing()
                    own(V.memset(ff_y, 0.0), acc_read, 1)
                    with dve.Fori(0, E) as e:
                        ffn(2, e * NFS + NFS)
                        dve.wait_ge(down_done, e * NFS + 2 * NFS)
                        dve.wait_ge(acc_read, e + 1)
                        for t in range(2):
                            ins = V.scalar_tensor_tensor(ff_y[:, t].rearrange("p (b c) -> p b c", b=2), ps[:, 2 * t:2 * t + 2, :],
                                                         rgate[:, bass.ds(e * 2 + t, 1)],
                                                         ff_y[:, t].rearrange("p (b c) -> p b c", b=2), ALU.mult, ALU.add)
                        ins.then_inc(acc_read, 1)
                residual(l, 3)


def _layout(a):
    c = np.ascontiguousarray
    g = lambda n: np.asarray(a[n])
    rows = np.arange(P)

    def panels(w, width, blocks):
        lead = w.shape[:-2]
        n = w.shape[-1] // width
        v = w.reshape(lead + (blocks, P, n, width))
        k = len(lead)
        return v.transpose(tuple(range(k)) + (k + 2, k + 1, k, k + 3)).reshape(lead + (n, P, blocks * width))

    out = {}
    out["x"] = np.concatenate([g("x_prompt")[0], g("x_sample")[0]], axis=1)
    out["c_t"] = np.stack([g("c_ctx"), g("c")[0]]).reshape(2, KD, P).transpose(2, 1, 0).reshape(P, KD, 2)
    out["b_mod_t"] = g("b_mod").reshape(L, NMOD, P).transpose(2, 0, 1)
    out["norm_t"] = g("norm_g").reshape(L, 4, KD, P).transpose(3, 0, 1, 2)
    out["lb_t"] = g("hg_lb").reshape(L, 2, H, HD).transpose(3, 0, 1, 2).reshape(P, L, 8)
    out["decay"] = np.broadcast_to(g("ret_decay").reshape(1, L * 8), (P, L * 8))
    out["hgn"] = np.broadcast_to(g("hg_norm")[:, None, :], (L, P, W))
    r, q = rows // GRID_W, rows % GRID_W
    row_off = r[None, :] - r[:, None] + 7
    col_off = np.clip(q[None, :] - q[:, None] + NA_COLS - 1, 0, 2 * NA_COLS - 2)
    out["rpb"] = g("na_rpb")[:, :, row_off, col_off].transpose(0, 2, 1, 3)
    out["cache_kt"] = g("cache_na_k")[0].transpose(0, 3, 2, 1)
    out["cache_v"] = g("cache_na_v")[0].reshape(L, P, W)
    out["s_ret"] = g("state_ret")[0].transpose(0, 3, 1, 2, 4)
    out["s_hg"] = g("state_hgrn")[0].transpose(0, 3, 1, 2, 4)
    out["router"] = g("w_router")[0].reshape(KD, P, E).transpose(1, 0, 2)
    out["consts"] = _constants(rows)
    m, n = rows[:, None], rows[None, :]
    levels = [((m >> (v + 1)) == (n >> (v + 1))) & ((m >> v) != (n >> v)) for v in range(NLEV)] + [m == n]
    out["levels"] = np.stack(levels, axis=1).astype(np.int32)
    out["w_mod"] = panels(g("w_mod"), 512, KD)
    out["w_in"] = panels(g("w_in"), 512, KD)
    out["w_br"] = panels(g("w_br"), D, 4)[:, :, 0]
    out["w_o"] = panels(g("w_o"), 512, KD)
    gu = np.concatenate([g("w_ffn_gu"), g("w_exp_gu")[0]])
    gu = gu.reshape(E + 1, KD, P, 2, NFS, FS).transpose(0, 4, 2, 1, 3, 5).reshape(E + 1, NFS, P, KD * 2 * FS)
    down = np.concatenate([g("w_ffn_down"), g("w_exp_down")[0]])
    down = down.reshape(E + 1, NFS, 2, P, D).transpose(0, 1, 3, 2, 4).reshape(E + 1, NFS, P, 2 * D)
    out["w_ff"] = np.concatenate([gu, down], axis=3)
    return {k: c(v) for k, v in out.items()}


def _constants(rows):
    m, n = rows[:, None].astype(np.float64), rows[None, :].astype(np.float64)
    nf = HD // 4
    inv = 10000.0 ** (-np.arange(nf, dtype=np.float32) / np.float32(nf))
    pos = np.stack([rows // GRID_W, rows % GRID_W], axis=-1).astype(np.float32)
    ang = (pos[:, :, None] * inv.astype(np.float32)).astype(np.float32)
    cos = np.repeat(np.cos(ang)[:, :, None, :], 2, axis=2).reshape(P, HD)
    sin = np.stack([-np.sin(ang), np.sin(ang)], axis=2).reshape(P, HD)
    q = rows % GRID_W
    first = np.clip(q - NA_COLS // 2, 0, GRID_W - NA_COLS)[:, None]
    inside = (q[None, :] >= first) & (q[None, :] < first + NA_COLS)
    parts = {
        "ident": np.eye(P), "cos": cos, "sin": sin,
        "above": np.maximum(n - m, 0), "below": np.maximum(m - n, 0),
        "mask_above": (n >= m) * HD ** -0.5, "mask_below": (n <= m) * HD ** -0.5,
        "ramp_up": np.broadcast_to(n + 1, (P, P)), "ramp_down": np.broadcast_to(P - n, (P, P)),
        "window": np.where(inside, 0.0, -1e30), "iota8": np.broadcast_to(np.arange(8), (P, 8)),
        "half": np.full((P, 2), -0.5), "age": np.concatenate([P - 1 - m, m], axis=1), "ones": np.ones((P, 1)),
    }
    return np.concatenate([parts[k] for k in CONST_W], axis=1).astype(np.float32)


_INS = ["x", "c_t", "b_mod_t", "norm_t", "lb_t", "decay", "hgn", "rpb", "cache_kt", "cache_v", "s_ret", "s_hg", "router",
        "consts", "levels", "w_mod", "w_in", "w_br", "w_o", "w_ff"]
_OUTS = [(P, 2 * D), (L, P, W), (L, P, W), (L, P, 2 * W), (L, P, 2 * W)]


def kernel(**inputs):
    import numpy as _np
    import concourse.bacc as _bacc
    from concourse import mybir as _mybir
    from concourse.bass_utils import run_bass_kernel_spmd as _run

    nc = _bacc.Bacc("TRN2", target_bir_lowering=False, num_devices=1)
    laid = _layout(inputs)
    arrays, args = {}, []
    for name in _INS:
        a = laid[name]
        arrays[f"in_{name}"] = a
        args.append(nc.dram_tensor(f"in_{name}", a.shape, _mybir.dt.from_np(a.dtype), kind="ExternalInput").ap())
    for i, shape in enumerate(_OUTS):
        args.append(nc.dram_tensor(f"out_{i}", shape, _mybir.dt.float32, kind="ExternalOutput").ap())
    program(nc, *args)
    r = _run(nc, [arrays], core_ids=[0])
    y, k, v, sr, sh = (r.results[0][f"out_{i}"] for i in range(len(_OUTS)))
    y = _np.asarray(y).reshape(P, 2, D)
    states = [_np.asarray(s).reshape(L, P, 2, H, HD).transpose(0, 2, 3, 1, 4)[None] for s in (sr, sh)]
    return (_np.ascontiguousarray(y[:, 0])[None], _np.ascontiguousarray(y[:, 1])[None],
            _np.asarray(k).reshape(1, L, P, H, HD), _np.asarray(v).reshape(1, L, P, H, HD),
            _np.ascontiguousarray(states[0]), _np.ascontiguousarray(states[1]))
```

```python
from contextlib import ExitStack

import numpy as np

import concourse.bass as bass
from concourse import mybir

F32 = mybir.dt.float32
I32 = mybir.dt.int32
U32 = mybir.dt.uint32
ALU = mybir.AluOpType
ACT = mybir.ActivationFunctionType
AX_X = mybir.AxisListType.X

P = 128
D = 1024
KD = D // P
W = 512
H = 4
HD = W // H
L = 2
E = 8
FF = 2816
FS = 256
NFS = FF // FS
NMOD = 48
NWIN = 18
GRID_W, NA_COLS = 64, 16
EPS, F_MIN = 1e-6, 1e-30
SLOTS = 3
SLAB = KD * 2 * FS + 2 * D
NLEV = 7

CONST_W = {"ident": P, "cos": HD, "sin": HD, "above": P, "below": P, "mask_above": P, "mask_below": P,
           "ramp_up": P, "ramp_down": P, "window": P, "iota": 2 * P, "half": 2, "age": 2, "before": P, "ones": P}
CONST_AT = {}
_at = 0
for _k, _n in CONST_W.items():
    CONST_AT[_k] = _at
    _at += _n
NCONST = _at

BR_AFTER = {13: 0, 15: 1, 17: 2}
STAGED = [0, 1, 4, 5, 7, 8, 9]


def layer_slabs(l):
    slabs = [("mod", l, i) for i in range(12)]
    for j in range(NWIN):
        slabs.append(("win", l, j))
        if j in BR_AFTER:
            slabs.append(("br", l, BR_AFTER[j]))
    return slabs + [("wo", l, 0), ("wo", l, 1), ("skip", l, 0)]


def ring_plan():
    uses, before, at, plan = [0] * SLOTS, [None] * SLOTS, 0, {}
    for l in range(L):
        todo = layer_slabs(l)
        if l == 0:
            todo += [("ffn", 0, i) for i in range(NFS)] + [("skip", 0, 1)]
        for key in todo:
            s = at % SLOTS
            at += 1
            if key[0] != "skip":
                plan[key] = (s, uses[s], before[s])
                uses[s] += 1
                before[s] = key
    assert at % SLOTS == 0 and 12 % SLOTS == 0
    return plan, uses, before


def program(nc, x, c_t, b_mod_t, norm_t, lb_t, decay, hgn, rpb, cache_kt, cache_v, s_ret, s_hg, router, consts, levels,
            w_mod, w_in, w_br, w_o, w_ff, y, new_k, new_v, new_ret, new_hg):
    plan, uses0, before0 = ring_plan()
    per_expert = [len(range(s, NFS, SLOTS)) for s in range(SLOTS)]

    with ExitStack() as ctx:
        def sb(name, width, dt=F32):
            return ctx.enter_context(nc.sbuf_tensor(name, [P, width], dt))[:, :]

        def sem(name):
            return ctx.enter_context(nc.semaphore(name))

        ring = [sb(f"ring{s}", SLAB) for s in range(SLOTS)]
        x_sb = sb("x_sb", 2 * D).rearrange("p (g c) -> p g c", g=2)
        hT = sb("hT", 2 * D).rearrange("p (g k t) -> p g k t", g=2, k=KD)
        wide = sb("wide", 2 * D)
        xn = wide.rearrange("p (g c) -> p g c", g=2)
        stage = wide.rearrange("p (b g c) -> p b g c", b=2, g=2)
        merged = xn
        rv_hi = sb("rv_hi", 2 * W).rearrange("p (g c) -> p g c", g=2)
        rg_hg = sb("rg_hg", 2 * W).rearrange("p (g c) -> p g c", g=2)
        nv = sb("nv", 2 * W).rearrange("p (g c) -> p g c", g=2)
        gate = sb("gate", 2 * D)
        gates = gate.rearrange("p (g c) -> p g c", g=2)
        q_dec = gate[:, 0:2 * W].rearrange("p (d h t) -> p d h t", d=2, h=H)
        decays = gate[:, 2 * W:3 * W].rearrange("p (h t) -> p h t", h=H)
        bias = gate[:, 3 * W:4 * W].rearrange("p (h t) -> p h t", h=H)
        u = sb("u", 11 * D)
        u1, u2 = u[:, 0:6 * D], u[:, 6 * D:11 * D]
        ght = "p (g h t) -> p g h t"
        rqT, rkT = (u1[:, i * D:(i + 1) * D].rearrange(ght, g=2, h=H) for i in (0, 1))
        kdec = u1[:, 2 * D:3 * D].rearrange("p (d c) -> p d c", d=2)
        ratt = u1[:, 3 * D:4 * D].rearrange(ght, g=2, h=H)
        qdec = u1[:, 4 * D:5 * D].rearrange("p (d h t) -> p d h t", d=2, h=H)
        rope = u1[:, 5 * D:6 * D].rearrange("p (b c) -> p b c", b=2)
        nqT, nkT = (u2[:, i * D:(i + 1) * D].rearrange(ght, g=2, h=H) for i in (0, 1))
        lg1 = u2[:, 2 * D:3 * D].rearrange("p (h s t) -> p h s t", h=H, s=2)
        lg0 = u2[:, 3 * D:3 * D + W].rearrange("p (h t) -> p h t", h=H)
        pT0 = u2[:, 3 * D + W:4 * D].rearrange("p (h t) -> p h t", h=H)
        pT1 = u2[:, 4 * D:5 * D].rearrange("p (s h t) -> p s h t", s=2, h=H)
        hq, f_pre, f_suf, k_f, k_b, f_sufx = (u1[:, i * D:(i + 1) * D] for i in range(6))
        b_prex, q_lev, k_lev = (u2[:, i * D:(i + 1) * D] for i in range(3))
        hatt = u2[:, 4 * D:5 * D]
        act_s = u[:, 0:2 * W].rearrange("p (t c) -> p t c", t=2)[:, :, 0:FS]
        act_v = u[:, D:2 * D].rearrange("p (b t c) -> p b t c", b=2, t=2)
        act_T = u[:, 2 * D:3 * D].rearrange("p (b t j m) -> p b t j m", b=2, t=2, j=2)
        e_out = u[:, 3 * D:11 * D]

        brT_ = sb("brT", 2 * D)
        brT = brT_.rearrange("p (b g k t) -> p b g k t", b=2, g=2, k=4)
        hgT = brT_.rearrange("p (t k m) -> p t k m", t=2, k=KD)
        br_ = sb("br", 2 * D)
        br = br_.rearrange("p (b g c) -> p b g c", b=2, g=2)
        ff_y = br_.rearrange("p (g c) -> p g c", g=2)
        h_rows = xn
        pick = gate[:, 0:4 * P].rearrange("p (g m) -> p g m", g=2)
        weigh = gate[:, 4 * P:8 * P].rearrange("p (b g m) -> p b g m", b=2, g=2)
        weighT = gate[:, 8 * P:12 * P].rearrange("p (b g m) -> p b g m", b=2, g=2)
        over_out = rv_hi.rearrange("p g c -> p (g c)")
        state0 = sb("state0", 2 * W).rearrange("p (d h c) -> p d h c", d=2, h=H)
        ckT = sb("ckT", W).rearrange("p (h t) -> p h t", h=H)
        cv = sb("cv", W)
        state_out = sb("state_out", 2 * W)
        level_mask = sb("level_mask", 8 * P, I32).rearrange("p (v t) -> p v t", v=8)
        con = sb("con", NCONST)
        hgn_sb = sb("hgn_sb", W)
        rout_w = sb("rout_w", KD * E).rearrange("p (k e) -> p k e", k=KD)
        cond = sb("cond", KD * 2).rearrange("p (k g) -> p k g", k=KD)
        bm = sb("bm", L * NMOD).rearrange("p (l n) -> p l n", l=L)
        ng = sb("ng", L * 4 * KD).rearrange("p (l n k) -> p l n k", l=L, n=4)
        modc = sb("modc", NMOD * 2).rearrange("p (m k g) -> p m k g", m=6, k=KD)
        lbr = sb("lbr", L * 8).rearrange("p (l n) -> p l n", l=L)
        lbw = sb("lbw", 6 * 8).rearrange("p (n c) -> p n c", n=6)
        lb = sb("lb", L * 8).rearrange("p (l n) -> p l n", l=L)
        olb = sb("olb", L * 8).rearrange("p (l n) -> p l n", l=L)
        dec = sb("dec", L * 8)
        lgw = sb("lgw", 2 * L * 8).rearrange("p (n c) -> p n c", n=2)
        lg = sb("lg", L * 8).rearrange("p (l d h) -> p l d h", l=L, d=2)
        kd = sb("kd", L * 8).rearrange("p (l d h) -> p l d h", l=L, d=2)
        ss = sb("ss", 4)
        ms = sb("ms", 2)
        rs = sb("rs", 2)
        bnst = sb("bnst", 8 * 6).rearrange("p (n c) -> p n c", n=8)
        mv = sb("mv", 8 * 2).rearrange("p (n c) -> p n c", n=8)
        hms = sb("hms", 8)
        hss = sb("hss", 8)
        hrs = sb("hrs", 8)
        negmax = sb("negmax", 8)
        psums = sb("psums", 8)
        pinv = sb("pinv", 8)
        rl = sb("rl", 2 * E).rearrange("p (g e) -> p g e", g=2)
        rmax = sb("rmax", 2 * 8).rearrange("p (g e) -> p g e", g=2)
        ridx = sb("ridx", 2 * 8, U32).rearrange("p (g e) -> p g e", g=2)
        rif = sb("rif", 2 * 8).rearrange("p (g e) -> p g e", g=2)
        rw = sb("rw", 2 * 8).rearrange("p (g e) -> p g e", g=2)
        rgate = sb("rgate", 2 * E).rearrange("p (g e) -> p g e", g=2)
        sel = sb("sel", 2 * E).rearrange("p (g e) -> p g e", g=2)
        place = sb("place", 2 * E).rearrange("p (g e) -> p g e", g=2)
        count = sb("count", E, I32)
        r1 = sb("r1", 2 * E).rearrange("p (g e) -> p g e", g=2)

        ps = ctx.enter_context(nc.psum_tensor("ps", [P, 8, 512], F32))

        def con_(name):
            return con[:, CONST_AT[name]:CONST_AT[name] + CONST_W[name]]

        ident = con_("ident")

        s_const = sem("constants_loaded")
        s_x = sem("x_loaded")
        slab_in = [sem(f"slab_in{s}") for s in range(SLOTS)]
        s_bias = sem("bias_loaded")
        s_cache = sem("cache_loaded")
        s_sret = sem("state_ret_loaded")
        s_shg = sem("state_hgrn_loaded")
        s_hgn = sem("hgrn_norm_loaded")
        s_kout = sem("new_k_stored")
        s_vout = sem("new_v_stored")
        s_srout = sem("new_ret_stored")
        s_shout = sem("new_hgrn_stored")
        s_yout = sem("y_stored")

        cond_ready = sem("cond_ready")
        dve_step = sem("dve_step")
        act_step = sem("act_step")
        pool_step = sem("pool_step")
        lbexp_ready = sem("lbexp_ready")
        lbsub_ready = sem("lbsub_ready")
        decabs_ready = sem("decabs_ready")
        declog_ready = sem("declog_ready")
        lg_ready = sem("lg_ready")
        kdx_ready = sem("kdx_ready")
        kdexp_ready = sem("kdexp_ready")
        kd_ready = sem("kd_ready")
        mod_done = sem("mod_slab_done")
        mod_ready = sem("mod_ready")
        sq_ready = sem("sq_ready")
        ms_ready = sem("ms_ready")
        rs_ready = sem("rs_ready")
        xn_ready = sem("xn_ready")
        xt_done = sem("xt_done")
        ht_dve = sem("ht_dve")
        ht_act = sem("ht_act")
        x_new = sem("x_new")
        win_done = sem("win_done")
        win_read = sem("win_read")
        exps_ready = sem("decay_exps_ready")
        decays_ready = sem("decays_ready")
        bias_ready = sem("bias_ready")
        rope_ready = sem("rope_ready")
        t_done = sem("turned")
        t_read_dve = sem("turned_read_dve")
        t_read_act = sem("turned_read_act")
        ratt_done = sem("ratt_done")
        ratt_ready = sem("ratt_ready")
        qdec_ready = sem("qdec_ready")
        kdec_ready = sem("kdec_ready")
        ro_done = sem("ro_done")
        ve_ready = sem("ve_ready")
        rsr_ready = sem("rsr_ready")
        ro_read = sem("ro_read")
        br_ready = sem("br_ready")
        rst_done = sem("ret_state_done")
        rst_read = sem("ret_state_read")
        na1_done = sem("na1_done")
        na1_read = sem("na1_read")
        na0_done = sem("na0_done")
        na0_read = sem("na0_read")
        max1_ready = sem("max1_ready")
        max0_ready = sem("max0_ready")
        p1_ready = sem("p1_ready")
        p0_ready = sem("p0_ready")
        pt1_done = sem("pt1_done")
        pt1_read = sem("pt1_read")
        pt0_done = sem("pt0_done")
        pt0_read = sem("pt0_read")
        pv_done = sem("pv_done")
        brt_done = sem("brt_done")
        brt_read = sem("brt_read")
        lev_ready = sem("lev_ready")
        lev_done = sem("lev_done")
        lev_read = sem("lev_read")
        qk_end = sem("state_products_ready")
        ho_done = sem("ho_done")
        hsq_ready = sem("hsq_ready")
        hms_ready = sem("hms_ready")
        hrs_ready = sem("hrs_ready")
        ks_done = sem("ks_done")
        ks_read = sem("ks_read")
        hst_done = sem("hgrn_state_done")
        hst_read = sem("hgrn_state_read")
        pr_done = sem("proj_done")
        pr_read = sem("proj_read")
        merged_ready = sem("merged_ready")
        mt_done = sem("merged_turned")
        mt_read = sem("merged_T_ready")
        wo_done = sem("wo_done")
        post_read = sem("post_scaled")
        gb_done = sem("gate_rows_done")
        gu_done = sem("gu_done")
        sil_ready = sem("silu_ready")
        act_ready = sem("act_ready")
        at_done = sem("act_turned")
        actT_ready = sem("act_T_ready")
        down_done = sem("down_done")
        acc_read = sem("ffn_acc_read")
        pick_ready = sem("pick_ready")
        gather_done = sem("gather_done")
        gather_read_dve = sem("gather_read_dve")
        gather_read_act = sem("gather_read_act")
        over_pick_ready = sem("over_pick_ready")
        over_gather_done = sem("over_gather_done")
        over_read_dve = sem("over_read_dve")
        over_read_act = sem("over_read_act")
        over_acc_read = sem("over_acc_read")
        over_sum_done = sem("over_sum_done")
        over_sum_read = sem("over_sum_read")
        sel_ready = sem("sel_ready")
        place_done = sem("place_done")
        place_ready = sem("place_ready")
        back_done = sem("h_rows_done")
        back_read = sem("h_rows_ready")
        weigh_ready = sem("weigh_ready")
        weigh_done = sem("weigh_turned")
        weigh_read = sem("weigh_T_ready")
        sum_done = sem("expert_sums_done")
        y_ready = sem("ffn_rows_ready")
        rlog_done = sem("router_done")
        rcopy_ready = sem("router_read")
        rdiff_ready = sem("router_diff_ready")
        rexp_ready = sem("router_exp_ready")

        block = ctx.enter_context(nc.Block())

        def released(key):
            kind, l, i = key
            return {"mod": (mod_done, 12 * l + i + 1), "win": (win_done, NWIN * l + i + 1),
                    "br": (pr_done, 6 * l + 2 * i + 2), "wo": (wo_done, 2 * l + i + 1),
                    "ffn": (down_done, i + 1)}[kind]

        @block.sync
        def _(sp):
            source = {"mod": w_mod, "win": w_in, "br": w_br, "wo": w_o, "ffn": w_ff}

            def load(key):
                s, _, before = plan[key]
                if before is not None:
                    sp.wait_ge(*released(before))
                src = source[key[0]][key[1], key[2]]
                sp.dma_start(ring[s][:, 0:src.shape[1]], src).then_inc(slab_in[s], 16)

            def load_expert(e, i):
                sp.dma_start(ring[i % SLOTS], w_ff[e + 1, i]).then_inc(slab_in[i % SLOTS], 16)

            for l in range(L):
                for i in range(SLOTS):
                    load(("mod", l, i))
                with sp.Fori(1, 12 // SLOTS) as t:
                    for s in range(SLOTS):
                        sp.wait_ge(mod_done, t * SLOTS + (12 * l + s - SLOTS + 1))
                        sp.dma_start(ring[s][:, 0:KD * 512], w_mod[l, t * SLOTS + s]).then_inc(slab_in[s], 16)
                for key in layer_slabs(l)[12:]:
                    if key[0] != "skip":
                        load(key)
                if l == 0:
                    for i in range(NFS):
                        load(("ffn", 0, i))
            for s in range(SLOTS):
                sp.wait_ge(*released(before0[s]))
                load_expert(0, s)

            def rest_of(e):
                for i in range(SLOTS, NFS):
                    sp.wait_ge(down_done, e * NFS + (NFS + i - SLOTS + 1))
                    load_expert(e, i)

            with sp.Fori(0, E - 1) as e:
                rest_of(e)
                for s in range(SLOTS):
                    sp.wait_ge(down_done, e * NFS + (NFS + max(i for i in range(NFS) if i % SLOTS == s) + 1))
                    load_expert(e + 1, s)
            rest_of(E - 1)
            for q in (s_kout, s_vout, s_srout, s_shout):
                sp.wait_ge(q, 16 * L)
            sp.wait_ge(s_yout, 16)

        @block.gpsimd
        def _(pool):
            for dst, src in ((con, consts), (cond, c_t), (bm, b_mod_t), (ng, norm_t), (lbr, lb_t), (dec, decay),
                             (rout_w, router), (level_mask, levels)):
                pool.dma_start(dst, src).then_inc(s_const, 16)
            pool.dma_start(x_sb, x).then_inc(s_x, 16)

            def power(out, in_, done, n):
                pool.tensor_tensor(out, in_, con_("half")[:, 0:1].broadcast_to([P, n]), ALU.pow).then_inc(done, 1)

            for l in range(L):
                if l:
                    pool.wait_ge(pr_read, 6 * l)
                pool.dma_start(bias, rpb[l]).then_inc(s_bias, 16)
                if l:
                    pool.wait_ge(pv_done, l)
                    pool.wait_ge(ho_done, l)
                pool.dma_start(ckT, cache_kt[l]).then_inc(s_cache, 16)
                pool.dma_start(cv, cache_v[l]).then_inc(s_cache, 16)
                pool.dma_start(state0, s_ret[l]).then_inc(s_sret, 16)
                if l:
                    pool.wait_ge(br_ready, 3 * l)
                pool.dma_start(hgn_sb, hgn[l]).then_inc(s_hgn, 16)
                if l == 0:
                    pool.wait_ge(s_const, 16 * 8)
                pool.wait_ge(ms_ready, 4 * l + 1)
                power(rs, ms, rs_ready, 2)
                pool.wait_ge(kd_ready, 1)
                pool.wait_ge(win_read, NWIN * l + 2)
                for d in range(2):
                    for h in range(H):
                        last = pool.tensor_scalar(kdec[:, d, h * HD:(h + 1) * HD], stage[:, 1, 0, h * HD:(h + 1) * HD],
                                                  kd[:, l, d, h:h + 1], None, ALU.mult)
                last.then_inc(kdec_ready, 1)
                pool.wait_ge(ve_ready, l + 1)
                power(hrs, hms, rsr_ready, 8)
                pool.wait_ge(win_read, NWIN * l + 6)
                pool.dma_start(new_k[l], stage[:, 1, 0, :]).then_inc(s_kout, 16)
                pool.wait_ge(win_read, NWIN * l + 7)
                pool.dma_start(new_v[l], nv[:, 0, :]).then_inc(s_vout, 16)
                pool.wait_ge(rst_read, l + 1)
                pool.dma_start(new_ret[l], state_out).then_inc(s_srout, 16)
                pool.wait_ge(ro_done, l + 1)
                pool.dma_start(state0, s_hg[l]).then_inc(s_shg, 16)
                pool.wait_ge(hms_ready, l + 1)
                power(hrs, hms, hrs_ready, 8)
                pool.wait_ge(hst_read, l + 1)
                pool.dma_start(new_hg[l], state_out).then_inc(s_shout, 16)
                for n in (1, 2, 3):
                    pool.wait_ge(ms_ready, 4 * l + n + 1)
                    power(rs, ms, rs_ready, 2)
            pool.wait_ge(x_new, 2 * L)
            pool.dma_start(y, x_sb).then_inc(s_yout, 16)

        @block.scalar
        def _(act):
            A = nc.scalar.activation
            chain = [0]

            def pair(v):
                return v.rearrange("p (b c) -> p b c", b=2)

            def link(ins):
                chain[0] += 1
                ins.then_inc(act_step, 1)
                act.wait_ge(act_step, chain[0])

            act.wait_ge(s_const, 16 * 8)
            A(cond, cond, ACT.Silu).then_inc(cond_ready, 1)
            act.wait_ge(lbsub_ready, 1)
            A(lbw[:, 1:3, :], lbw[:, 1:3, :], ACT.Exp).then_inc(lbexp_ready, 1)
            act.wait_ge(decabs_ready, 1)
            link(A(lgw[:, 0, :], lgw[:, 0, :], ACT.Exp, scale=-1.0))
            A(lgw[:, 0, :], lgw[:, 0, :], ACT.Ln, bias=con_("ones")[:, 0:1]).then_inc(declog_ready, 1)
            act.wait_ge(kdx_ready, 1)
            A(kd, kd, ACT.Exp).then_inc(kdexp_ready, 1)

            def squares_x(l, n):
                if n == 0 and l == 0:
                    act.wait_ge(s_x, 16)
                else:
                    act.wait_ge(x_new, 2 * l + (n == 2))
                for g in range(2):
                    ins = A(xn[:, g, :], x_sb[:, g, :], ACT.Square, accum_out=ss[:, g:g + 1])
                ins.then_inc(sq_ready, 1)

            def turn_read(l, n):
                w = 4 * l + 2 * (n == 2)
                for g in range(2):
                    act.wait_ge(xt_done, w + g + 1)
                    for k in range(4, KD):
                        m = 0 if n == 0 else 3
                        ins = A(hT[:, g, k, :], ps[:, 5 + 2 * g, (k - 4) * P:(k - 3) * P], ACT.Identity,
                                scale=modc[:, m + 1, k, g:g + 1], bias=modc[:, m, k, g:g + 1])
                    ins.then_inc(ht_act, 1)

            def post_norm(l, n, src):
                for g in range(2):
                    ins = A(xn[:, g, :], src[g], ACT.Square, accum_out=ss[:, g:g + 1])
                ins.then_inc(sq_ready, 1)
                act.wait_ge(rs_ready, 4 * l + n + 1)
                for g in range(2):
                    ins = A(xn[:, g, :], src[g], ACT.Copy, scale=rs[:, g:g + 1])
                ins.then_inc(post_read, 1)

            def softmax(l, lgt, off, done, ready):
                act.wait_ge(done, l + 1)
                for h in range(H):
                    v = lgt[:, h] if off else lgt[:, h, :]
                    v = v.rearrange("p s t -> p (s t)") if off else v
                    ins = A(v, v, ACT.Exp, bias=negmax[:, off + h:off + h + 1],
                            accum_out=psums[:, off + h:off + h + 1])
                ins.then_inc(ready, 1)

            def panel(l, j):
                act.wait_ge(win_done, NWIN * l + j + 1)
                func = ACT.Copy
                if j in STAGED:
                    q = STAGED.index(j)
                    if q >= 2:
                        act.wait_ge(t_done, 7 * l + q - 1)
                    if q == 3:
                        act.wait_ge(kdec_ready, l + 1)
                    if q == 5:
                        act.wait_ge(s_kout, 16 * (l + 1))
                    dst = [stage[:, q % 2, g, :] for g in range(2)]
                    if j == 7:
                        func = ACT.Silu
                elif j in (2, 10):
                    dst = [rv_hi[:, g, :] for g in range(2)]
                elif j in (3, 11):
                    if j == 11:
                        act.wait_ge(br_ready, 3 * l + 1)
                    dst = [rg_hg[:, g, :] for g in range(2)]
                    func = ACT.Silu
                elif j == 6:
                    if l:
                        act.wait_ge(s_vout, 16 * l)
                    dst = [nv[:, g, :] for g in range(2)]
                else:
                    if j == 12:
                        act.wait_ge(na1_read, l + 1)
                    elif j > 13:
                        act.wait_ge(pr_read, 6 * l + j - 13)
                    o = 512 * (j % 2)
                    dst = [gates[:, g, o:o + 512] for g in range(2)]
                    func = ACT.Sigmoid
                for g in range(2):
                    ins = A(dst[g], ps[:, 2 * (j % 2) + g, :], func)
                ins.then_inc(win_read, 1)

            def ffn(tiles, base):
                for i in range(NFS + 1):
                    if i:
                        act.wait_ge(at_done, base + i)
                        A(act_T[:, (i - 1) % 2, 0:tiles].rearrange("p t j m -> p t (j m)"), ps[:, 6:6 + tiles, 0:FS], ACT.Copy)\
                            .then_inc(actT_ready, 1)
                    if i < NFS:
                        act.wait_ge(gu_done, base + i + 1)
                        if i:
                            act.wait_ge(act_ready, base + i)
                        A(act_s[:, 0:tiles, :], ps[:, 4:4 + tiles, 0:FS], ACT.Silu).then_inc(sil_ready, 1)

            def expert(e, base):
                act.wait_ge(gather_done, e + 1)
                A(hgT[:, 0, 4:KD, :].rearrange("p k m -> p (k m)"), ps[:, 5, :], ACT.Copy).then_inc(gather_read_act, 1)
                rows_out = e_out[:, bass.ds(e * D, D)].rearrange("p (b c) -> p b c", b=2)

                def read_sums():
                    act.wait_ge(down_done, base + NFS)
                    A(rows_out, ps[:, 0:2, :], ACT.Copy).then_inc(acc_read, 1)

                n = act.value_load(count[0:1, bass.ds(e, 1)])
                with act.If(n > P):
                    act.wait_ge(over_gather_done, e + 1)
                    A(weighT[:, 0], ps[:, 6, 0:2 * P].rearrange("p (g m) -> p g m", g=2), ACT.Copy).then_inc(over_read_act, 1)
                    ffn(2, base)
                    read_sums()
                    A(pair(over_out), ps[:, 2:4, :], ACT.Copy).then_inc(over_acc_read, 1)
                with act.Else():
                    act.sem_inc(over_read_act, 1)
                    act.sem_inc(over_acc_read, 1)
                    ffn(1, base)
                    read_sums()

            for l in range(L):
                squares_x(l, 0)
                act.wait_ge(lg_ready, 1)
                if l:
                    act.wait_ge(pr_read, 6 * l)
                for d in range(2):
                    for h in range(H):
                        A(ratt[:, d, h, :], con_(("above", "below")[d]), ACT.Exp, scale=lg[:, l, d, h:h + 1])
                        ins = A(q_dec[:, d, h, :], con_(("ramp_up", "ramp_down")[d]), ACT.Exp,
                                scale=lg[:, l, d, h:h + 1])
                ins.then_inc(exps_ready, 1)
                act.wait_ge(mod_ready, l + 1)
                turn_read(l, 0)
                for j in range(NWIN):
                    panel(l, j)
                    if j == 6:
                        act.wait_ge(rst_done, l + 1)
                        if l:
                            act.wait_ge(s_shout, 16 * l)
                        A(state_out.rearrange("p (b c) -> p b c", b=2), ps[:, 4:6, :], ACT.Copy).then_inc(rst_read, 1)
                    if j == 8:
                        softmax(l, lg1, 4, max1_ready, p1_ready)
                    if j == 9:
                        softmax(l, lg0, 0, max0_ready, p0_ready)
                    if j in (9, 10):
                        q = j - 4
                        act.wait_ge(t_done, 7 * l + q + 1)
                        dst = (f_pre, f_suf)[q - 5].rearrange("p (g c) -> p g c", g=2)
                        A(dst, ps[:, 6:8, :], ACT.Sigmoid).then_inc(t_read_act, 1)
                act.wait_ge(ho_done, l + 1)
                for g in range(2):
                    for h in range(H):
                        ins = A(f_pre[:, (4 * g + h) * HD:(4 * g + h + 1) * HD], ps[:, 6 + g, h * HD:(h + 1) * HD], ACT.Square,
                                accum_out=hss[:, 4 * g + h:4 * g + h + 1])
                ins.then_inc(hsq_ready, 1)
                act.wait_ge(ks_done, l + 1)
                A(q_lev.rearrange("p (b c) -> p b c", b=2), ps[:, 4:6, :], ACT.Copy).then_inc(ks_read, 1)
                act.wait_ge(hst_done, l + 1)
                act.wait_ge(s_srout, 16 * (l + 1))
                A(state_out.rearrange("p (b c) -> p b c", b=2), ps[:, 4:6, :], ACT.Copy).then_inc(hst_read, 1)
                act.wait_ge(wo_done, 2 * l + 2)
                post_norm(l, 1, [ps[:, 2 * g:2 * g + 2, :].rearrange("p b c -> p (b c)") for g in range(2)])
                squares_x(l, 2)
                turn_read(l, 2)
                if l == 0:
                    ffn(2, 0)
                    act.wait_ge(down_done, NFS)
                    post_norm(l, 3, [ps[:, 2 * g:2 * g + 2, :].rearrange("p b c -> p (b c)") for g in range(2)])
                else:
                    act.wait_ge(rdiff_ready, 1)
                    A(rw[:, :, 1:2], rw[:, :, 1:2], ACT.Exp).then_inc(rexp_ready, 1)
                    act.wait_ge(place_ready, 1)
                    act.sem_inc(acc_read, 1)
                    with act.Fori(0, E) as e:
                        expert(e, e * NFS + NFS)
                    for e in range(E):
                        act.wait_ge(weigh_done, e + 1)
                        A(weighT[:, e % 2], ps[:, 4 + e % 2, 0:2 * P].rearrange("p (g m) -> p g m", g=2), ACT.Copy)\
                            .then_inc(weigh_read, 1)
                    act.wait_ge(y_ready, 1)
                    post_norm(l, 3, [ff_y[:, g, :] for g in range(2)])

        @block.tensor
        def _(pe):
            mm = nc.tensor.matmul

            def slab(key, blocks):
                s, u, _ = plan[key]
                pe.wait_ge(slab_in[s], 16 * (u + 1))
                return ring[s][:, 0:KD * 512].rearrange("p (k c) -> p k c", k=blocks)

            def modulation(l):
                if l == 0:
                    pe.wait_ge(cond_ready, 1)
                else:
                    pe.wait_ge(x_new, 2 * l)
                with pe.Fori(0, 12 // SLOTS) as t:
                    for s in range(SLOTS):
                        pe.wait_ge(slab_in[s], t * 16 + 16 * (plan[("mod", l, s)][1] + 1))
                        w = ring[s][:, 0:KD * 512].rearrange("p (k c) -> p k c", k=KD)
                        for c in range(4):
                            out = ps[:, 0, bass.ds(t * (8 * SLOTS) + (8 * s + 2 * c), 2)]
                            for k in range(KD):
                                ins = mm(out, w[:, k, c * P:(c + 1) * P], cond[:, k, :], start=(k == 0), stop=(k == KD - 1))
                        ins.then_inc(mod_done, 1)

            def turn_rows(l, n):
                w = 4 * l + 2 * (n == 2)
                for g in range(2):
                    pe.wait_ge(xn_ready, w + g + 1)
                    for k in range(KD):
                        ins = nc.tensor.transpose(ps[:, 4 + 2 * g + k // 4, (k % 4) * P:(k % 4 + 1) * P],
                                                  xn[:, g, k * P:(k + 1) * P], ident)
                    ins.then_inc(xt_done, 1)

            def panel(l, j):
                w = slab(("win", l, j), KD)
                if j == 0:
                    pe.wait_ge(ht_dve, 4 * l + 2)
                    pe.wait_ge(ht_act, 4 * l + 2)
                    pe.wait_ge(mod_ready, l + 1)
                elif j >= 2:
                    pe.wait_ge(win_read, NWIN * l + j - 1)
                if j >= 14:
                    pe.wait_ge(pr_read, 6 * l + j - 13)
                for g in range(2):
                    for k in range(KD):
                        ins = mm(ps[:, 2 * (j % 2) + g, :], hT[:, g, k, :], w[:, k, :], start=(k == 0), stop=(k == KD - 1))
                ins.then_inc(win_done, 1)

            def turn_panel(l, q):
                pe.wait_ge(win_read, NWIN * l + STAGED[q] + 1)
                if q < 2:
                    pe.wait_ge(rope_ready, 2 * l + q + 1)
                if 1 <= q <= 5:
                    pe.wait_ge(t_read_dve, 5 * l + q)
                elif q == 6:
                    pe.wait_ge(t_read_act, 2 * l + 1)
                for g in range(2):
                    src = rope[:, 0, :] if (q < 2 and g == 1) else stage[:, q % 2, g, :]
                    for h in range(H):
                        ins = nc.tensor.transpose(ps[:, 6 + g, h * P:(h + 1) * P], src[:, h * HD:(h + 1) * HD], ident)
                ins.then_inc(t_done, 1)

            def turn_heads(l, n, src, bank):
                pe.wait_ge(br_ready, 3 * l + n + 1)
                for g in range(2):
                    for h in range(H):
                        ins = nc.tensor.transpose(ps[:, bank + g, h * P:(h + 1) * P], src[:, g, h * HD:(h + 1) * HD], ident)
                ins.then_inc(brt_done, 1)

            def level(l, v):
                pe.wait_ge(lev_ready, 8 * l + v + 1)
                if v == 0:
                    pe.wait_ge(t_read_act, 2 * l + 2)
                else:
                    pe.wait_ge(lev_read, 8 * l + v)
                q = hq if v == NLEV else q_lev
                for u in range(8):
                    ins = mm(ps[:, 6 + u // 4, (u % 4) * P:(u % 4 + 1) * P], k_lev[:, u * P:(u + 1) * P],
                             q[:, u * P:(u + 1) * P], start=True, stop=True)
                ins.then_inc(lev_done, 1)

            def project(l, n):
                w = slab(("br", l, n), 4)
                pe.wait_ge(brt_read, 3 * l + n + 1)
                pe.wait_ge(win_read, NWIN * l + 14 + 2 * n)
                for half in range(2):
                    for g in range(2):
                        for k in range(4):
                            ins = mm(ps[:, 2 * half + g, :], brT[:, n % 2, g, k, :], w[:, k, half * 512:(half + 1) * 512],
                                     start=(k == 0), stop=(k == 3))
                    ins.then_inc(pr_done, 1)

            def turn_merged(l):
                pe.wait_ge(merged_ready, l + 1)
                pe.wait_ge(hst_read, l + 1)
                for g in range(2):
                    for k in range(KD):
                        ins = nc.tensor.transpose(ps[:, 4 + 2 * g + k // 4, (k % 4) * P:(k % 4 + 1) * P],
                                                  merged[:, g, k * P:(k + 1) * P], ident)
                    ins.then_inc(mt_done, 1)

            def output(l):
                pe.wait_ge(mt_read, 2 * l + 2)
                pe.wait_ge(pr_read, 6 * l + 6)
                for half in range(2):
                    w = slab(("wo", l, half), KD)
                    for g in range(2):
                        for k in range(KD):
                            ins = mm(ps[:, 2 * g + half, :], hT[:, g, k, :], w[:, k, :], start=(k == 0), stop=(k == KD - 1))
                    ins.then_inc(wo_done, 1)

            def gate_rows(l, n, m):
                if n == 1:
                    pe.wait_ge(actT_ready, NFS if l == 0 else NFS * (E + 1))
                    pe.wait_ge(act_ready, NFS if l == 0 else NFS * (E + 1))
                    if l:
                        pe.wait_ge(weigh_read, E)
                for g in range(2):
                    for k in range(KD):
                        col = modc[:, m, k, g:g + 1].broadcast_to([P, P])
                        ins = mm(ps[:, 4 + 2 * g + k // 4, (k % 4) * P:(k % 4 + 1) * P], col, ident, start=True, stop=True)
                ins.then_inc(gb_done, 1)

            def ffn(tiles, base, h, slot_wait, acc_wait):
                for i in range(NFS + 1):
                    if i:
                        pe.wait_ge(act_ready, base + i)
                        for t in range(tiles):
                            for j in range(2):
                                ins = nc.tensor.transpose(ps[:, 6 + t, j * P:(j + 1) * P],
                                                          act_v[:, (i - 1) % 2, t, j * P:(j + 1) * P], ident)
                        ins.then_inc(at_done, 1)
                    if i < NFS:
                        slot_wait(i)
                        w = ring[i % SLOTS][:, 0:KD * 512].rearrange("p (k c) -> p k c", k=KD)
                        for t in range(tiles):
                            for k in range(KD):
                                ins = mm(ps[:, 4 + t, :], h[:, t, k, :], w[:, k, :], start=(k == 0), stop=(k == KD - 1))
                        ins.then_inc(gu_done, 1)
                    if i:
                        w = ring[(i - 1) % SLOTS][:, KD * 512:SLAB].rearrange("p (k c) -> p k c", k=2)
                        pe.wait_ge(actT_ready, base + i)
                        if i == 1:
                            acc_wait()
                        for t in range(tiles):
                            for half in range(2):
                                for j in range(2):
                                    ins = mm(ps[:, 2 * t + half, :], act_T[:, (i - 1) % 2, t, j, :],
                                             w[:, j, half * 512:(half + 1) * 512],
                                             start=(i == 1 and j == 0), stop=(i == NFS and j == 1), skip_group_check=True)
                        ins.then_inc(down_done, 1)

            def gather(t):
                for k in range(KD):
                    for g in range(2):
                        ins = mm(ps[:, 4 + k // 4, (k % 4) * P:(k % 4 + 1) * P], h_rows[:, g, k * P:(k + 1) * P],
                                 pick[:, g, t * P:(t + 1) * P], start=(g == 0), stop=(g == 1))
                return ins

            def expert(e, base):
                pe.wait_ge(pick_ready, e + 1)
                gather(0).then_inc(gather_done, 1)
                pe.wait_ge(gather_read_dve, e + 1)
                pe.wait_ge(gather_read_act, e + 1)

                def slot_wait(i):
                    s = i % SLOTS
                    pe.wait_ge(slab_in[s], e * (16 * per_expert[s]) + 16 * (uses0[s] + i // SLOTS + 1))

                def acc_wait():
                    pe.wait_ge(acc_read, e + 1)

                n = pe.value_load(count[0:1, bass.ds(e, 1)])
                with pe.If(n > P):
                    pe.wait_ge(over_pick_ready, e + 1)
                    gather(1)
                    for g in range(2):
                        ins = nc.tensor.transpose(ps[:, 6, g * P:(g + 1) * P], weigh[:, 0, g, :], ident)
                    ins.then_inc(over_gather_done, 1)
                    pe.wait_ge(over_read_dve, e + 1)
                    pe.wait_ge(over_read_act, e + 1)
                    ffn(2, base, hgT, slot_wait, acc_wait)
                    pe.wait_ge(over_acc_read, e + 1)
                    for g in range(2):
                        for half in range(2):
                            ins = mm(ps[:, 4 + 2 * g + half, :], weighT[:, 0, g, :], over_out[:, half * 512:(half + 1) * 512],
                                     start=True, stop=True)
                    ins.then_inc(over_sum_done, 1)
                    pe.wait_ge(over_sum_read, e + 2)
                with pe.Else():
                    pe.sem_inc(over_gather_done, 1)
                    pe.sem_inc(over_sum_done, 1)
                    ffn(1, base, hgT, slot_wait, acc_wait)

            def pieces(l, j):
                if j in (1, 2, 5, 6, 8, 9, 10):
                    turn_panel(l, (1, 2, 5, 6, 8, 9, 10).index(j))
                if j == 3:
                    pe.wait_ge(t_read_dve, 5 * l + 2)
                    for g in range(2):
                        for h in range(H):
                            ins = mm(ps[:, 4 + g, h * P:(h + 1) * P], rkT[:, g, h, :], rqT[:, g, h, :], start=True, stop=True)
                    ins.then_inc(ratt_done, 1)
                if j == 4:
                    pe.wait_ge(ratt_ready, l + 1)
                    pe.wait_ge(qdec_ready, l + 1)
                    pe.wait_ge(s_sret, 16 * (l + 1))
                    pe.wait_ge(win_read, NWIN * l + 3)
                    for g in range(2):
                        for h in range(H):
                            out = ps[:, 4 + g, h * HD:(h + 1) * HD]
                            ins = mm(out, ratt[:, g, h, :], rv_hi[:, g, h * HD:(h + 1) * HD], start=True, stop=(g == 0))
                            if g:
                                mm(out, qdec[:, 0, h, :], state0[:, 0, h, :], start=False, stop=False)
                                ins = mm(out, qdec[:, 1, h, :], state0[:, 1, h, :], start=False, stop=True)
                    ins.then_inc(ro_done, 1)
                if j == 6:
                    pe.wait_ge(ro_read, l + 1)
                    pe.wait_ge(kdec_ready, l + 1)
                    for d in range(2):
                        for h in range(H):
                            ins = mm(ps[:, 4 + d, h * HD:(h + 1) * HD], kdec[:, d, h * HD:(h + 1) * HD],
                                     rv_hi[:, 0, h * HD:(h + 1) * HD], start=True, stop=True)
                    ins.then_inc(rst_done, 1)
                if j == 7:
                    pe.wait_ge(t_read_dve, 5 * l + 4)
                    pe.wait_ge(s_cache, 32 * (l + 1))
                    pe.wait_ge(rst_read, l + 1)
                    for s, keys in ((0, nkT[:, 1]), (1, ckT)):
                        for h in range(H):
                            ins = mm(ps[:, 4 + s, h * P:(h + 1) * P], nqT[:, 1, h, :], keys[:, h, :], start=True, stop=True)
                    ins.then_inc(na1_done, 1)
                if j == 8:
                    pe.wait_ge(na1_read, l + 1)
                    for h in range(H):
                        ins = mm(ps[:, 4, h * P:(h + 1) * P], nqT[:, 0, h, :], nkT[:, 0, h, :], start=True, stop=True)
                    ins.then_inc(na0_done, 1)
                if j == 9:
                    pe.wait_ge(p1_ready, l + 1)
                    pe.wait_ge(na0_read, l + 1)
                    for s in range(2):
                        for h in range(H):
                            ins = nc.tensor.transpose(ps[:, 4 + s, h * P:(h + 1) * P], lg1[:, h, s, :], ident)
                    ins.then_inc(pt1_done, 1)
                if j == 10:
                    pe.wait_ge(p0_ready, l + 1)
                    pe.wait_ge(pt1_read, l + 1)
                    for h in range(H):
                        ins = nc.tensor.transpose(ps[:, 4, h * P:(h + 1) * P], lg0[:, h, :], ident)
                    ins.then_inc(pt0_done, 1)
                if j == 11:
                    pe.wait_ge(pt0_read, l + 1)
                    for h in range(H):
                        hc = slice(h * HD, (h + 1) * HD)
                        mm(ps[:, 4, hc], pT0[:, h, :], nv[:, 0, hc], start=True, stop=True)
                    for h in range(H):
                        hc = slice(h * HD, (h + 1) * HD)
                        mm(ps[:, 5, hc], pT1[:, 0, h, :], nv[:, 1, hc], start=True, stop=False)
                        ins = mm(ps[:, 5, hc], pT1[:, 1, h, :], cv[:, hc], start=False, stop=True)
                    ins.then_inc(pv_done, 1)
                    level(l, 0)
                if j == 12:
                    pe.wait_ge(br_ready, 3 * l + 2)
                    turn_heads(l, 0, br[:, 0], 4)
                    level(l, 1)
                if j == 13:
                    pe.wait_ge(brt_read, 3 * l + 1)
                    turn_heads(l, 1, br[:, 1], 4)
                    level(l, 2)
                if j in (14, 15):
                    level(l, j - 10)
                if j == 16:
                    level(l, NLEV)
                if j == 17:
                    recurrence_out(l)

            def recurrence_out(l):
                pe.wait_ge(lev_read, 8 * l + 8)
                pe.wait_ge(qk_end, l + 1)
                pe.wait_ge(s_shg, 16 * (l + 1))
                for g in range(2):
                    for h in range(H):
                        hc = slice(h * HD, (h + 1) * HD)
                        u = 4 * g + h
                        ins = mm(ps[:, 6 + g, hc], hatt[:, u * P:(u + 1) * P], rv_hi[:, g, hc], start=True, stop=(g == 0))
                        if g:
                            mm(ps[:, 7, hc], q_lev[:, hc], state0[:, 0, h, :], start=False, stop=False)
                            ins = mm(ps[:, 7, hc], q_lev[:, W + h * HD:W + (h + 1) * HD], state0[:, 1, h, :],
                                     start=False, stop=True)
                ins.then_inc(ho_done, 1)
                pe.wait_ge(brt_read, 3 * l + 2)
                for d in range(2):
                    for h in range(H):
                        a = d * W + h * HD
                        ins = nc.tensor.transpose(ps[:, 4 + d, h * P:(h + 1) * P], k_lev[:, a:a + HD], ident)
                ins.then_inc(ks_done, 1)
                pe.wait_ge(ks_read, l + 1)
                for d in range(2):
                    for h in range(H):
                        hc = slice(h * HD, (h + 1) * HD)
                        ins = mm(ps[:, 4 + d, hc], q_lev[:, d * W + h * HD:d * W + (h + 1) * HD], rv_hi[:, 0, hc],
                                 start=True, stop=True)
                ins.then_inc(hst_done, 1)
                turn_heads(l, 2, br[:, 0], 6)

            for l in range(L):
                modulation(l)
                turn_rows(l, 0)
                for j in range(NWIN):
                    panel(l, j)
                    pieces(l, j)
                    if j in BR_AFTER:
                        project(l, BR_AFTER[j])
                        if j < NWIN - 1:
                            level(l, 3 if j == 13 else 6)
                turn_merged(l)
                output(l)
                gate_rows(l, 0, 2)
                turn_rows(l, 2)
                pe.wait_ge(ht_dve, 4 * l + 4)
                pe.wait_ge(ht_act, 4 * l + 4)
                if l == 0:
                    ffn(2, 0, hT, lambda i: slab(("ffn", 0, i), KD), lambda: pe.wait_ge(post_read, 1))
                else:
                    for g in range(2):
                        for k in range(KD):
                            ins = mm(ps[:, 0, g * E:(g + 1) * E], hT[:, g, k, :], rout_w[:, k, :], start=(k == 0), stop=(k == KD - 1))
                    ins.then_inc(rlog_done, 1)
                    for g in range(2):
                        for k in range(KD):
                            ins = nc.tensor.transpose(ps[:, 4 + 2 * g + k // 4, (k % 4) * P:(k % 4 + 1) * P], hT[:, g, k, :], ident)
                    ins.then_inc(back_done, 1)
                    pe.wait_ge(sel_ready, 1)
                    mm(ps[:, 0, 0:E], con_("before"), sel[:, 0, :], start=True, stop=True)
                    mm(ps[:, 0, E:2 * E], con_("before"), sel[:, 1, :], start=True, stop=False)
                    mm(ps[:, 0, E:2 * E], con_("ones"), sel[:, 0, :], start=False, stop=True)
                    for g in range(2):
                        ins = mm(ps[:, 0, 2 * E:3 * E], con_("ones"), sel[:, g, :], start=(g == 0), stop=(g == 1))
                    ins.then_inc(place_done, 1)
                    pe.wait_ge(place_ready, 1)
                    pe.wait_ge(back_read, 1)
                    with pe.Fori(0, E) as e:
                        expert(e, e * NFS + NFS)
                    pe.wait_ge(acc_read, E + 1)
                    for e in range(E + 1):
                        if e < E:
                            pe.wait_ge(weigh_ready, e + 1)
                            if e >= 2:
                                pe.wait_ge(weigh_read, e - 1)
                            for g in range(2):
                                ins = nc.tensor.transpose(ps[:, 4 + e % 2, g * P:(g + 1) * P], weigh[:, e % 2, g, :], ident)
                            ins.then_inc(weigh_done, 1)
                        if e:
                            pe.wait_ge(weigh_read, e)
                            for g in range(2):
                                for half in range(2):
                                    a = (e - 1) * D + half * 512
                                    ins = mm(ps[:, 2 * g + half, :], weighT[:, (e - 1) % 2, g, :], e_out[:, a:a + 512],
                                             start=(e == 1), stop=(e == E), skip_group_check=True)
                    ins.then_inc(sum_done, 1)
                gate_rows(l, 1, 5)

        @block.vector
        def _(dve):
            V = nc.vector
            chain = [0]

            def link(ins):
                chain[0] += 1
                ins.then_inc(dve_step, 1)
                dve.wait_ge(dve_step, chain[0])

            def own(ins, s, value):
                ins.then_inc(s, 1)
                dve.wait_ge(s, value)

            dve.wait_ge(s_const, 16 * 8)
            link(V.tensor_tensor(lbw[:, 0, :], lbr[:, 0, :], lbr[:, 1, :], ALU.max))
            V.tensor_tensor(lbw[:, 1, :], lbr[:, 0, :], lbw[:, 0, :], ALU.subtract)
            V.tensor_tensor(lbw[:, 2, :], lbr[:, 1, :], lbw[:, 0, :], ALU.subtract).then_inc(lbsub_ready, 1)
            dve.wait_ge(lbexp_ready, 1)
            link(V.tensor_tensor(lbw[:, 3, :], lbw[:, 1, :], lbw[:, 2, :], ALU.add))
            link(V.reciprocal(lbw[:, 4, :], lbw[:, 3, :]))
            link(V.tensor_tensor(lbw[:, 1:3, :], lbw[:, 1:3, :], lbw[:, 4, :].unsqueeze(1).broadcast_to([P, 2, 8]), ALU.mult))
            V.tensor_tensor(lb[:, 0, :], lbw[:, 1, :], lbw[:, 1, :], ALU.subtract)
            link(V.tensor_tensor(lbw[:, 5, :], lbw[:, 1, :], lbw[:, 2, :], ALU.add))
            link(V.tensor_tensor(lb[:, 1, :], lbw[:, 5, :], lbw[:, 1, :], ALU.subtract))
            V.tensor_scalar(olb, lb, -1.0, 1.0, ALU.mult, ALU.add)
            V.scalar_tensor_tensor(lgw[:, 0, :], dec, -1.0, dec, ALU.mult, ALU.max).then_inc(decabs_ready, 1)
            dve.wait_ge(declog_ready, 1)
            lgf = lg.rearrange("p l d h -> p (l d h)")
            own(V.scalar_tensor_tensor(lgf, dec, 0.0, lgw[:, 0, :], ALU.min, ALU.subtract), lg_ready, 1)
            for d in range(2):
                ins = V.tensor_scalar(kd[:, :, d, :], lg[:, :, d, :], con_("age")[:, d:d + 1], None, ALU.mult)
            ins.then_inc(kdx_ready, 1)
            dve.wait_ge(kdexp_ready, 1)
            V.tensor_scalar(kd, kd, HD ** -0.5, None, ALU.mult).then_inc(kd_ready, 1)

            def mean_square(l, n):
                dve.wait_ge(sq_ready, 4 * l + n + 1)
                V.tensor_scalar(ms, ss[:, 0:2], 1.0 / D, EPS, ALU.mult, ALU.add).then_inc(ms_ready, 1)

            def rows(l, n):
                dve.wait_ge(rs_ready, 4 * l + n + 1)
                for g in range(2):
                    V.tensor_scalar(xn[:, g, :], x_sb[:, g, :], rs[:, g:g + 1], None, ALU.mult).then_inc(xn_ready, 1)

            def turn_read(l, n):
                w = 4 * l + 2 * (n == 2)
                m = 0 if n == 0 else 3
                for g in range(2):
                    dve.wait_ge(xt_done, w + g + 1)
                    for k in range(4):
                        ins = V.tensor_scalar(hT[:, g, k, :], ps[:, 4 + 2 * g, k * P:(k + 1) * P],
                                              modc[:, m + 1, k, g:g + 1], modc[:, m, k, g:g + 1], ALU.mult, ALU.add)
                    ins.then_inc(ht_dve, 1)

            def modulation(l):
                dve.wait_ge(mod_done, 12 * (l + 1))
                link(V.tensor_tensor(modc.rearrange("p m k g -> p (m k) g"),
                                     ps[:, 0, 0:2 * NMOD].rearrange("p (n g) -> p n g", g=2),
                                     bm[:, l, :].unsqueeze(2).broadcast_to([P, NMOD, 2]), ALU.add))
                for m, n in ((1, 0), (4, 2)):
                    V.scalar_tensor_tensor(modc[:, m], modc[:, m], 1.0, ng[:, l, n, :].unsqueeze(2).broadcast_to([P, KD, 2]),
                                           ALU.add, ALU.mult)
                for m, n in ((2, 1), (5, 3)):
                    ins = V.tensor_tensor(modc[:, m], modc[:, m], ng[:, l, n, :].unsqueeze(2).broadcast_to([P, KD, 2]), ALU.mult)
                ins.then_inc(mod_ready, 1)
                dve.wait_ge(mod_ready, l + 1)

            def rotate(l, q):
                dve.wait_ge(win_read, NWIN * l + q + 1)
                if q:
                    dve.wait_ge(t_done, 7 * l + 1)
                haf = dict(h=H, a=2, two=2)
                split = "p (h a two f) -> p h a two f"
                src = stage[:, q % 2, 1, :]
                V.tensor_tensor(rope[:, 0, :].rearrange("p (h c) -> p h c", h=H), src.rearrange("p (h c) -> p h c", h=H),
                                con_("cos").unsqueeze(1).broadcast_to([P, H, HD]), ALU.mult)
                sin = con_("sin").rearrange("p (a two f) -> p a two f", a=2, two=2)
                for two in range(2):
                    ins = V.tensor_tensor(rope[:, 1, :].rearrange(split, **haf)[:, :, :, two, :],
                                          src.rearrange(split, **haf)[:, :, :, 1 - two, :],
                                          sin[:, :, two, :].unsqueeze(1).broadcast_to([P, H, 2, HD // 4]), ALU.mult)
                link(ins)
                V.tensor_tensor(rope[:, 0, :], rope[:, 0, :], rope[:, 1, :], ALU.add).then_inc(rope_ready, 1)

            def turned(l, q, dst):
                dve.wait_ge(t_done, 7 * l + q + 1)
                V.tensor_copy(dst, ps[:, 6:8, :]).then_inc(t_read_dve, 1)

            def pair(v):
                return v.rearrange("p (b c) -> p b c", b=2)

            def retention(l):
                dve.wait_ge(ratt_done, l + 1)
                V.tensor_tensor(ratt.rearrange("p g h t -> p g (h t)"), ps[:, 4:6, :],
                                decays.rearrange("p h t -> p (h t)").unsqueeze(1).broadcast_to([P, 2, W]), ALU.mult)\
                    .then_inc(ratt_ready, 1)
                V.tensor_tensor(qdec.rearrange("p d h t -> p d (h t)"), q_dec.rearrange("p d h t -> p d (h t)"),
                                rqT[:, 1].rearrange("p h t -> p (h t)").unsqueeze(1).broadcast_to([P, 2, W]), ALU.mult)\
                    .then_inc(qdec_ready, 1)
                dve.wait_ge(ro_done, l + 1)
                for u in range(8):
                    ins = V.bn_stats(bnst[:, u, :], ps[:, 4 + u // 4, (u % 4) * HD:(u % 4 + 1) * HD])
                link(ins)
                for u in range(8):
                    ins = V.bn_aggr(mv[:, u, :], bnst[:, u, :])
                link(ins)
                V.tensor_scalar(hms, mv[:, :, 1], 1e-5, None, ALU.add).then_inc(ve_ready, 1)
                dve.wait_ge(rsr_ready, l + 1)
                for u in range(8):
                    hc = slice((u % 4) * HD, (u % 4 + 1) * HD)
                    ins = V.tensor_scalar(br[:, 0, u // 4, hc], ps[:, 4 + u // 4, hc], mv[:, u, 0:1], hrs[:, u:u + 1],
                                          ALU.subtract, ALU.mult)
                own(ins, ro_read, l + 1)
                dve.wait_ge(win_read, NWIN * l + 4)
                V.tensor_tensor(br[:, 0], br[:, 0], rg_hg, ALU.mult).then_inc(br_ready, 1)

            def logits1(l):
                dve.wait_ge(na1_done, l + 1)
                V.scalar_tensor_tensor(lg1[:, :, 0, :], ps[:, 4, :].rearrange("p (h t) -> p h t", h=H), HD ** -0.5, bias,
                                       ALU.mult, ALU.add)
                own(V.tensor_scalar(lg1[:, :, 1, :], ps[:, 5, :].rearrange("p (h t) -> p h t", h=H), HD ** -0.5, None, ALU.mult),
                    na1_read, l + 1)
                link(V.tensor_reduce(negmax[:, 4:8], lg1.rearrange("p h s t -> p h (s t)"), AX_X, ALU.max))
                V.tensor_scalar(negmax[:, 4:8], negmax[:, 4:8], -1.0, None, ALU.mult).then_inc(max1_ready, 1)

            def logits0(l):
                dve.wait_ge(na0_done, l + 1)
                own(V.tensor_scalar(lg0, ps[:, 4, :].rearrange("p (h t) -> p h t", h=H), HD ** -0.5, None, ALU.mult),
                    na0_read, l + 1)
                link(V.tensor_reduce(negmax[:, 0:4], lg0, AX_X, ALU.max))
                V.tensor_scalar(negmax[:, 0:4], negmax[:, 0:4], -1.0, None, ALU.mult).then_inc(max0_ready, 1)

            def attention_out(l):
                dve.wait_ge(p1_ready, l + 1)
                dve.wait_ge(p0_ready, l + 1)
                link(V.reciprocal(pinv, psums))
                dve.wait_ge(pv_done, l + 1)
                for u in range(8):
                    hc = slice((u % 4) * HD, (u % 4 + 1) * HD)
                    ins = V.tensor_scalar(br[:, 1, u // 4, hc], ps[:, 4 + u // 4, hc], pinv[:, u:u + 1], None, ALU.mult)
                ins.then_inc(br_ready, 1)

            def forget(l, d, f, k):
                dve.wait_ge(t_read_act, 2 * l + d + 1)
                for h in range(H):
                    v = f.rearrange("p (g h t) -> p g h t", g=2, h=H)[:, :, h, :]
                    c = 4 * d + h
                    ins = V.tensor_scalar(v, v, olb[:, l, c:c + 1], lb[:, l, c:c + 1], ALU.mult, ALU.add)
                link(ins)
                link(V.tensor_scalar(f, f, F_MIN, None, ALU.max))
                link(V.tensor_scalar(k, f, -1.0, 1.0, ALU.mult, ALU.add))

            def halves(v, s):
                w = v.rearrange("p (b two s) -> p b two s", two=2, s=s)
                return w[:, :, 0, :], w[:, :, 1, :]

            def products(l, v):
                if v:
                    dve.wait_ge(lev_done, 8 * l + v)
                if v == NLEV:
                    V.tensor_tensor(k_lev, k_f, k_b, ALU.add).then_inc(lev_ready, 1)
                    return
                s = 1 << v
                (ql, qr), (kl, kr), (hl, hr) = halves(q_lev, s), halves(k_lev, s), halves(hq, s)
                V.tensor_tensor(qr, hr, halves(f_pre, s)[1], ALU.mult)
                V.tensor_tensor(ql, hl, halves(f_suf, s)[0], ALU.mult)
                V.tensor_tensor(kl, halves(k_f, s)[0], halves(f_sufx, s)[0], ALU.mult)
                V.tensor_tensor(kr, halves(k_b, s)[1], halves(b_prex, s)[1], ALU.mult).then_inc(lev_ready, 1)
                shape = [P, 2 * D // (4 * s), s]
                (pl, pr), (sl, sr) = halves(f_pre, s), halves(f_suf, s)
                xl, xr = halves(f_sufx, s)[0], halves(b_prex, s)[1]
                V.tensor_tensor(xl, xl, pr[:, :, s - 1:s].broadcast_to(shape), ALU.mult)
                link(V.tensor_tensor(xr, xr, sl[:, :, 0:1].broadcast_to(shape), ALU.mult))
                V.tensor_tensor(pr, pr, pl[:, :, s - 1:s].broadcast_to(shape), ALU.mult)
                link(V.tensor_tensor(sl, sl, sr[:, :, 0:1].broadcast_to(shape), ALU.mult))

            def level_read(l, v):
                dve.wait_ge(lev_done, 8 * l + v + 1)
                V.copy_predicated(hatt.rearrange("p (u t) -> p u t", u=8),
                                  level_mask[:, v, :].unsqueeze(1).broadcast_to([P, 8, P]),
                                  ps[:, 6:8, :].rearrange("p b (h t) -> p (b h) t", h=H)).then_inc(lev_read, 1)

            def heads_turned(l, n, bank):
                dve.wait_ge(brt_done, 3 * l + n + 1)
                V.tensor_copy(brT[:, n % 2].rearrange("p g k t -> p g (k t)"), ps[:, bank:bank + 2, :]).then_inc(brt_read, 1)

            def gated(l, n):
                if n:
                    dve.wait_ge(brt_done, 3 * l + 2)
                dve.wait_ge(win_read, NWIN * l + 14 + 2 * n)
                for half in range(2):
                    dve.wait_ge(pr_done, 6 * l + 2 * n + half + 1)
                    cols = slice(half * 512, (half + 1) * 512)
                    src = ps[:, 2 * half:2 * half + 2, :]
                    dst = merged[:, :, cols] if n == 0 else br[:, 1]
                    ins = V.tensor_tensor(dst, src, gates[:, :, cols], ALU.mult)
                    own(ins, pr_read, 6 * l + 2 * n + half + 1)
                    if n:
                        ins = V.tensor_tensor(merged[:, :, cols], merged[:, :, cols], br[:, 1], ALU.add)
                        if n == 2 and half == 1:
                            ins.then_inc(merged_ready, 1)
                        else:
                            link(ins)

            def recurrence_out(l):
                V.tensor_tensor(q_lev[:, 0:W], hq[:, W:2 * W], f_pre[:, W:2 * W], ALU.mult)
                V.tensor_tensor(q_lev[:, W:2 * W], hq[:, W:2 * W], f_suf[:, W:2 * W], ALU.mult)
                dve.wait_ge(lev_done, 8 * l + 8)
                V.tensor_tensor(k_lev[:, 0:W], k_f[:, 0:W], f_sufx[:, 0:W], ALU.mult)
                V.tensor_tensor(k_lev[:, W:2 * W], k_b[:, 0:W], b_prex[:, 0:W], ALU.mult).then_inc(qk_end, 1)
                dve.wait_ge(win_read, NWIN * l + 12)
                dve.wait_ge(s_hgn, 16 * (l + 1))
                V.tensor_tensor(rg_hg, rg_hg, hgn_sb.unsqueeze(1).broadcast_to([P, 2, W]), ALU.mult)
                dve.wait_ge(hsq_ready, l + 1)
                V.tensor_scalar(hms, hss, 1.0 / HD, EPS, ALU.mult, ALU.add).then_inc(hms_ready, 1)
                dve.wait_ge(hrs_ready, l + 1)
                for u in range(8):
                    hc = slice((u % 4) * HD, (u % 4 + 1) * HD)
                    ins = V.scalar_tensor_tensor(br[:, 0, u // 4, hc], ps[:, 6 + u // 4, hc], hrs[:, u:u + 1],
                                                 rg_hg[:, u // 4, hc], ALU.mult, ALU.mult)
                ins.then_inc(br_ready, 1)

            def residual(l, n):
                mean_square(l, n)
                w = 2 * l + (n == 3) + 1
                dve.wait_ge(post_read, w)
                dve.wait_ge(gb_done, w)
                link(V.tensor_tensor(pair(wide).rearrange("p g (b c) -> p (g b) c", b=2),
                                     pair(wide).rearrange("p g (b c) -> p (g b) c", b=2), ps[:, 4:8, :], ALU.mult))
                own(V.tensor_tensor(x_sb, x_sb, xn, ALU.add), x_new, w)

            def ffn(tiles, base):
                for i in range(NFS):
                    dve.wait_ge(sil_ready, base + i + 1)
                    V.tensor_tensor(act_v[:, i % 2, 0:tiles, :], act_s[:, 0:tiles, :], ps[:, 4:4 + tiles, FS:2 * FS], ALU.mult)\
                        .then_inc(act_ready, 1)

            def routing():
                dve.wait_ge(rlog_done, 1)
                own(V.tensor_copy(rl.rearrange("p g e -> p (g e)"), ps[:, 0, 0:2 * E]), rcopy_ready, 1)
                for g in range(2):
                    ins = V.max(rmax[:, g, :], rl[:, g, :])
                link(ins)
                for g in range(2):
                    ins = V.max_index(ridx[:, g, :], rmax[:, g, :], rl[:, g, :])
                V.tensor_tensor(rw[:, :, 1:2], rmax[:, :, 1:2], rmax[:, :, 0:1], ALU.subtract).then_inc(rdiff_ready, 1)
                dve.wait_ge(rdiff_ready, 1)
                link(V.tensor_copy(rif, ridx))
                iota8 = con_("iota")[:, 0:E]
                for g in range(2):
                    V.tensor_scalar(sel[:, g, :], iota8, rif[:, g, 0:1], None, ALU.is_equal)
                    ins = V.tensor_scalar(r1[:, g, :], iota8, rif[:, g, 1:2], None, ALU.is_equal)
                link(ins)
                own(V.tensor_tensor(sel, sel, r1, ALU.add), sel_ready, 1)
                dve.wait_ge(back_done, 1)
                V.tensor_copy(h_rows.rearrange("p g (b c) -> p (g b) c", b=2), ps[:, 4:8, :]).then_inc(back_read, 1)
                dve.wait_ge(rexp_ready, 1)
                link(V.tensor_scalar(rw[:, :, 2:3], rw[:, :, 1:2], 1.0, None, ALU.add))
                link(V.reciprocal(rw[:, :, 3:4], rw[:, :, 2:3]))
                link(V.tensor_tensor(rw[:, :, 4:5], rw[:, :, 1:2], rw[:, :, 3:4], ALU.mult))
                for g in range(2):
                    V.tensor_scalar(rgate[:, g, :], iota8, rif[:, g, 0:1], rw[:, g, 3:4], ALU.is_equal, ALU.mult)
                    ins = V.tensor_scalar(r1[:, g, :], iota8, rif[:, g, 1:2], rw[:, g, 4:5], ALU.is_equal, ALU.mult)
                link(ins)
                V.tensor_tensor(rgate, rgate, r1, ALU.add)
                dve.wait_ge(place_done, 1)
                link(V.scalar_tensor_tensor(place, ps[:, 0, 0:2 * E].rearrange("p (g e) -> p g e", g=2), 1.0, sel,
                                            ALU.add, ALU.mult))
                V.tensor_scalar(place, place, -1.0, None, ALU.add)
                own(V.tensor_copy(count, ps[:, 0, 2 * E:3 * E]), place_ready, 1)

            def expert(e, base):
                one = bass.ds(e, 1)
                for g in range(2):
                    ins = V.tensor_scalar(pick[:, g, 0:P], con_("iota")[:, 0:P], place[:, g, one], None, ALU.is_equal)
                ins.then_inc(pick_ready, 1)
                dve.wait_ge(gather_done, e + 1)
                V.tensor_copy(hgT[:, 0, 0:4, :].rearrange("p k m -> p (k m)"), ps[:, 4, :]).then_inc(gather_read_dve, 1)
                n = dve.value_load(count[0:1, one])
                with dve.If(n > P):
                    for g in range(2):
                        V.tensor_scalar(pick[:, g, P:2 * P], con_("iota")[:, P:2 * P], place[:, g, one], None, ALU.is_equal)
                        ins = V.tensor_scalar(weigh[:, 0, g, :], con_("iota")[:, P:2 * P], place[:, g, one], rgate[:, g, one],
                                              ALU.is_equal, ALU.mult)
                    ins.then_inc(over_pick_ready, 1)
                    dve.wait_ge(over_gather_done, e + 1)
                    V.tensor_copy(hgT[:, 1].rearrange("p (b k) m -> p b (k m)", b=2), ps[:, 4:6, :]).then_inc(over_read_dve, 1)
                    ffn(2, base)
                    dve.wait_ge(over_sum_done, e + 1)
                    dve.wait_ge(over_sum_read, e + 1)
                    V.tensor_tensor(ff_y.rearrange("p g (b c) -> p (g b) c", b=2), ff_y.rearrange("p g (b c) -> p (g b) c", b=2),
                                    ps[:, 4:8, :], ALU.add).then_inc(over_sum_read, 1)
                with dve.Else():
                    dve.sem_inc(over_pick_ready, 1)
                    dve.sem_inc(over_read_dve, 1)
                    dve.sem_inc(over_sum_read, 1)
                    ffn(1, base)

            for l in range(L):
                mean_square(l, 0)
                dve.wait_ge(exps_ready, l + 1)
                for d, name in ((0, "mask_above"), (1, "mask_below")):
                    ins = V.tensor_tensor(ratt[:, d], ratt[:, d], con_(name).unsqueeze(1).broadcast_to([P, H, P]), ALU.mult)
                link(ins)
                V.tensor_tensor(decays, ratt[:, 0], ratt[:, 1], ALU.add)
                dve.wait_ge(s_bias, 16 * (l + 1))
                link(V.tensor_tensor(bias, bias, con_("window").unsqueeze(1).broadcast_to([P, H, P]), ALU.add))
                rows(l, 0)
                modulation(l)
                turn_read(l, 0)
                rotate(l, 0)
                turned(l, 0, pair(u1[:, 0:D]))
                rotate(l, 1)
                turned(l, 1, pair(u1[:, D:2 * D]))
                retention(l)
                V.memset(f_sufx, 1.0)
                turned(l, 2, pair(u2[:, 0:D]))
                turned(l, 3, pair(u2[:, D:2 * D]))
                logits1(l)
                turned(l, 4, pair(hq))
                logits0(l)
                V.memset(b_prex, 1.0)
                dve.wait_ge(pt1_done, l + 1)
                V.tensor_copy(pT1.rearrange("p s h t -> p s (h t)"), ps[:, 4:6, :]).then_inc(pt1_read, 1)
                forget(l, 0, f_pre, k_f)
                dve.wait_ge(pt0_done, l + 1)
                V.tensor_copy(pT0.rearrange("p h t -> p (h t)"), ps[:, 4, :]).then_inc(pt0_read, 1)
                forget(l, 1, f_suf, k_b)
                products(l, 0)
                attention_out(l)
                level_read(l, 0)
                products(l, 1)
                heads_turned(l, 0, 4)
                level_read(l, 1)
                products(l, 2)
                heads_turned(l, 1, 4)
                level_read(l, 2)
                products(l, 3)
                gated(l, 0)
                level_read(l, 3)
                products(l, 4)
                level_read(l, 4)
                products(l, 5)
                level_read(l, 5)
                products(l, 6)
                gated(l, 1)
                level_read(l, 6)
                products(l, NLEV)
                level_read(l, NLEV)
                recurrence_out(l)
                heads_turned(l, 2, 6)
                gated(l, 2)
                for g in range(2):
                    dve.wait_ge(mt_done, 2 * l + g + 1)
                    V.tensor_copy(hT[:, g].rearrange("p (b k) t -> p b (k t)", b=2), ps[:, 4 + 2 * g:6 + 2 * g, :])\
                        .then_inc(mt_read, 1)
                residual(l, 1)
                mean_square(l, 2)
                rows(l, 2)
                turn_read(l, 2)
                if l == 0:
                    ffn(2, 0)
                else:
                    routing()
                    own(V.memset(ff_y, 0.0), over_sum_read, 1)
                    with dve.Fori(0, E) as e:
                        expert(e, e * NFS + NFS)
                    for e in range(E):
                        if e >= 2:
                            dve.wait_ge(weigh_done, e - 1)
                        for g in range(2):
                            ins = V.tensor_scalar(weigh[:, e % 2, g, :], con_("iota")[:, 0:P], place[:, g, e:e + 1],
                                                  rgate[:, g, e:e + 1], ALU.is_equal, ALU.mult)
                        ins.then_inc(weigh_ready, 1)
                    dve.wait_ge(sum_done, 1)
                    dve.wait_ge(over_sum_read, E + 1)
                    V.tensor_tensor(ff_y.rearrange("p g (b c) -> p (g b) c", b=2), ff_y.rearrange("p g (b c) -> p (g b) c", b=2),
                                    ps[:, 0:4, :], ALU.add).then_inc(y_ready, 1)
                residual(l, 3)


def _layout(a):
    c = np.ascontiguousarray
    g = lambda n: np.asarray(a[n])
    rows = np.arange(P)

    def panels(w, width, blocks):
        lead = w.shape[:-2]
        n = w.shape[-1] // width
        v = w.reshape(lead + (blocks, P, n, width))
        k = len(lead)
        return v.transpose(tuple(range(k)) + (k + 2, k + 1, k, k + 3)).reshape(lead + (n, P, blocks * width))

    out = {}
    out["x"] = np.concatenate([g("x_prompt")[0], g("x_sample")[0]], axis=1)
    out["c_t"] = np.stack([g("c_ctx"), g("c")[0]]).reshape(2, KD, P).transpose(2, 1, 0).reshape(P, KD, 2)
    out["b_mod_t"] = g("b_mod").reshape(L, NMOD, P).transpose(2, 0, 1)
    out["norm_t"] = g("norm_g").reshape(L, 4, KD, P).transpose(3, 0, 1, 2)
    out["lb_t"] = g("hg_lb").reshape(L, 2, H, HD).transpose(3, 0, 1, 2).reshape(P, L, 8)
    out["decay"] = np.broadcast_to(g("ret_decay").reshape(1, L * 8), (P, L * 8))
    out["hgn"] = np.broadcast_to(g("hg_norm")[:, None, :], (L, P, W))
    r, q = rows // GRID_W, rows % GRID_W
    row_off = r[None, :] - r[:, None] + 7
    col_off = np.clip(q[None, :] - q[:, None] + NA_COLS - 1, 0, 2 * NA_COLS - 2)
    out["rpb"] = g("na_rpb")[:, :, row_off, col_off].transpose(0, 2, 1, 3)
    out["cache_kt"] = g("cache_na_k")[0].transpose(0, 3, 2, 1)
    out["cache_v"] = g("cache_na_v")[0].reshape(L, P, W)
    out["s_ret"] = g("state_ret")[0].transpose(0, 3, 1, 2, 4)
    out["s_hg"] = g("state_hgrn")[0].transpose(0, 3, 1, 2, 4)
    out["router"] = g("w_router")[0].reshape(KD, P, E).transpose(1, 0, 2)
    out["consts"] = _constants(rows)
    m, n = rows[:, None], rows[None, :]
    levels = [((m >> (v + 1)) == (n >> (v + 1))) & ((m >> v) != (n >> v)) for v in range(NLEV)] + [m == n]
    out["levels"] = np.stack(levels, axis=1).astype(np.int32)
    out["w_mod"] = panels(g("w_mod"), 512, KD)
    out["w_in"] = panels(g("w_in"), 512, KD)
    out["w_br"] = panels(g("w_br"), D, 4)[:, :, 0]
    out["w_o"] = panels(g("w_o"), 512, KD)
    gu = np.concatenate([g("w_ffn_gu"), g("w_exp_gu")[0]])
    gu = gu.reshape(E + 1, KD, P, 2, NFS, FS).transpose(0, 4, 2, 1, 3, 5).reshape(E + 1, NFS, P, KD * 2 * FS)
    down = np.concatenate([g("w_ffn_down"), g("w_exp_down")[0]])
    down = down.reshape(E + 1, NFS, 2, P, D).transpose(0, 1, 3, 2, 4).reshape(E + 1, NFS, P, 2 * D)
    out["w_ff"] = np.concatenate([gu, down], axis=3)
    return {k: c(v) for k, v in out.items()}


def _constants(rows):
    m, n = rows[:, None].astype(np.float64), rows[None, :].astype(np.float64)
    nf = HD // 4
    inv = 10000.0 ** (-np.arange(nf, dtype=np.float32) / np.float32(nf))
    pos = np.stack([rows // GRID_W, rows % GRID_W], axis=-1).astype(np.float32)
    ang = (pos[:, :, None] * inv.astype(np.float32)).astype(np.float32)
    cos = np.repeat(np.cos(ang)[:, :, None, :], 2, axis=2).reshape(P, HD)
    sin = np.stack([-np.sin(ang), np.sin(ang)], axis=2).reshape(P, HD)
    q = rows % GRID_W
    first = np.clip(q - NA_COLS // 2, 0, GRID_W - NA_COLS)[:, None]
    inside = (q[None, :] >= first) & (q[None, :] < first + NA_COLS)
    parts = {
        "ident": np.eye(P), "cos": cos, "sin": sin,
        "above": np.maximum(n - m, 0), "below": np.maximum(m - n, 0),
        "mask_above": (n >= m) * HD ** -0.5, "mask_below": (n <= m) * HD ** -0.5,
        "ramp_up": np.broadcast_to(n + 1, (P, P)), "ramp_down": np.broadcast_to(P - n, (P, P)),
        "window": np.where(inside, 0.0, -1e30), "iota": np.broadcast_to(np.arange(2 * P), (P, 2 * P)),
        "half": np.full((P, 2), -0.5), "age": np.concatenate([P - 1 - m, m], axis=1), "before": m < n, "ones": np.ones((P, P)),
    }
    return np.concatenate([parts[k] for k in CONST_W], axis=1).astype(np.float32)


_INS = ["x", "c_t", "b_mod_t", "norm_t", "lb_t", "decay", "hgn", "rpb", "cache_kt", "cache_v", "s_ret", "s_hg", "router",
        "consts", "levels", "w_mod", "w_in", "w_br", "w_o", "w_ff"]
_OUTS = [(P, 2 * D), (L, P, W), (L, P, W), (L, P, 2 * W), (L, P, 2 * W)]


def kernel(**inputs):
    import numpy as _np
    import concourse.bacc as _bacc
    from concourse import mybir as _mybir
    from concourse.bass_utils import run_bass_kernel_spmd as _run

    nc = _bacc.Bacc("TRN2", target_bir_lowering=False, num_devices=1)
    laid = _layout(inputs)
    arrays, args = {}, []
    for name in _INS:
        a = laid[name]
        arrays[f"in_{name}"] = a
        args.append(nc.dram_tensor(f"in_{name}", a.shape, _mybir.dt.from_np(a.dtype), kind="ExternalInput").ap())
    for i, shape in enumerate(_OUTS):
        args.append(nc.dram_tensor(f"out_{i}", shape, _mybir.dt.float32, kind="ExternalOutput").ap())
    program(nc, *args)
    r = _run(nc, [arrays], core_ids=[0])
    y, k, v, sr, sh = (r.results[0][f"out_{i}"] for i in range(len(_OUTS)))
    y = _np.asarray(y).reshape(P, 2, D)
    states = [_np.asarray(s).reshape(L, P, 2, H, HD).transpose(0, 2, 3, 1, 4)[None] for s in (sr, sh)]
    return (_np.ascontiguousarray(y[:, 0])[None], _np.ascontiguousarray(y[:, 1])[None],
            _np.asarray(k).reshape(1, L, P, H, HD), _np.asarray(v).reshape(1, L, P, H, HD),
            _np.ascontiguousarray(states[0]), _np.ascontiguousarray(states[1]))
```

```python
from contextlib import ExitStack

import numpy as np

import concourse.bass as bass
from concourse import mybir

F32 = mybir.dt.float32
R32 = mybir.dt.float32r
I32 = mybir.dt.int32
U32 = mybir.dt.uint32
ALU = mybir.AluOpType
ACT = mybir.ActivationFunctionType
AX_X = mybir.AxisListType.X

P = 128
D = 1024
KD = D // P
W = 512
H = 4
HD = W // H
L = 2
E = 8
FF = 2816
FS = 256
NFS = FF // FS
NMOD = 48
NWIN = 18
GRID_W, NA_COLS = 64, 16
EPS, F_MIN = 1e-6, 1e-30
SLOTS = 3
SLAB = KD * 2 * FS + 2 * D
UNIT = 2048
NPART = SLAB // UNIT
NLEV = 7

CONST_W = {"ident": P, "cos": HD, "sin": HD, "above": P, "below": P, "mask_above": P, "mask_below": P,
           "ramp_up": P, "ramp_down": P, "window": P, "iota": 2 * P, "half": 2, "age": 2, "before": P, "ones": P}
CONST_AT = {}
_at = 0
for _k, _n in CONST_W.items():
    CONST_AT[_k] = _at
    _at += _n
NCONST = _at

BR_AFTER = {13: 0, 15: 1, 17: 2}
STAGED = [0, 1, 4, 5, 7, 8, 9]


NSLAB_MOD = 12
MOD_FIRST = 4
MOD_TURNS = L * NSLAB_MOD // SLOTS
MOD_SPLIT = -(-MOD_FIRST // SLOTS) * SLOTS
MOD_GROUPS = [range(0, MOD_SPLIT), range(MOD_SPLIT, L * NSLAB_MOD)]
COND_PAD = 2 * max(len(r) for r in MOD_GROUPS) - 2


def layer_slabs(l):
    slabs = [("skip", l, 0)]
    if l == 0:
        slabs = [("mod", n // NSLAB_MOD, n % NSLAB_MOD) for n in range(L * NSLAB_MOD)] + slabs
    for j in range(NWIN):
        slabs.append(("win", l, j))
        if j in BR_AFTER:
            slabs.append(("br", l, BR_AFTER[j]))
    return slabs + [("wo", l, 0), ("wo", l, 1)]


MIX_SLABS = [[key for key in layer_slabs(l) if key[0] in ("win", "br", "wo")] for l in range(L)]
MIX_UNITS = 2 * len(MIX_SLABS[0])
STEP = {key[0:1] + key[2:]: c for c, key in enumerate(MIX_SLABS[0])}


def ring_plan():
    uses, before, at, plan = [0] * SLOTS, [None] * SLOTS, 0, {}
    for l in range(L):
        todo = layer_slabs(l)
        if l == 0:
            todo += [("ffn", 0, i) for i in range(NFS)] + [("skip", 0, 1)]
        for key in todo:
            s = at % SLOTS
            at += 1
            if key[0] != "skip":
                plan[key] = (s, uses[s], before[s])
                uses[s] += key[0] != "ffn"
                before[s] = key
    assert at % SLOTS == 0
    return plan, before


def program(nc, x, c_t, b_mod_t, norm_t, lb_t, decay, hgn, rpb, cache_kt, cache_v, s_ret, s_hg, router, consts, levels,
            w_mod, w_in, w_br, w_o, w_ff, y, new_k, new_v, new_ret, new_hg):
    plan, before0 = ring_plan()
    per_expert = [len(range(s, NFS, SLOTS)) for s in range(SLOTS)]

    with ExitStack() as ctx:
        def sb(name, width, dt=F32):
            return ctx.enter_context(nc.sbuf_tensor(name, [P, width], dt))[:, :]

        def sem(name):
            return ctx.enter_context(nc.semaphore(name))

        def shared(whole, parts):
            with ExitStack() as first:
                a = [first.enter_context(nc.sbuf_tensor(n, [P, w], F32))[:, :] for n, w in whole]
            return a, [sb(n, w, R32) for n, w in parts]

        rings = [shared([(f"ring{s}", SLAB)], [(f"ring_lo{s}", SLAB)]) for s in range(SLOTS)]
        ring, ring_lo = [r[0][0] for r in rings], [r[1][0] for r in rings]
        x_sb = sb("x_sb", 2 * D).rearrange("p (g c) -> p g c", g=2)
        gkt = "p (g k t) -> p g k t"
        h_hi, h_lo = (sb(n, 2 * D, R32).rearrange(gkt, g=2, k=KD) for n in ("h_hi", "h_lo"))
        wide = sb("wide", 2 * D)
        xn = wide.rearrange("p (g c) -> p g c", g=2)
        stage = wide.rearrange("p (b g c) -> p b g c", b=2, g=2)
        merged = xn
        h32 = wide.rearrange(gkt, g=2, k=KD)
        (rv_hi, rg_hg), (w_hi0,) = shared([("rv_hi", 2 * W), ("rg_hg", 2 * W)], [("w_hi0", UNIT)])
        w_hi1 = sb("w_hi1", UNIT, R32)
        bt_hi, bt_lo = (v.rearrange("p (g k t) -> p g k t", g=2, k=4) for v in (w_hi1[:, 0:D], w_hi1[:, D:2 * D]))
        (nv, state_out), (w_hi2,) = shared([("nv", 2 * W), ("state_out", 2 * W)], [("w_hi2", UNIT)])
        w_hi = [w_hi0, w_hi1, w_hi2]
        m_hi = [r[:, 2 * UNIT:3 * UNIT] for r in ring_lo]
        rv_hi = rv_hi.rearrange("p (g c) -> p g c", g=2)
        rg_hg = rg_hg.rearrange("p (g c) -> p g c", g=2)
        nv = nv.rearrange("p (g c) -> p g c", g=2)
        gate = sb("gate", 2 * D)
        gates = gate.rearrange("p (g c) -> p g c", g=2)
        q_dec = gate[:, 0:2 * W].rearrange("p (d h t) -> p d h t", d=2, h=H)
        decays = gate[:, 2 * W:3 * W].rearrange("p (h t) -> p h t", h=H)
        bias = gate[:, 3 * W:4 * W].rearrange("p (h t) -> p h t", h=H)
        (u,), (_, act_hi, act_lo, _) = shared([("u", 11 * D)], [("u_head", 2 * D), ("act_hi", W), ("act_lo", W), ("u_tail", 8 * D)])
        u1, u2 = u[:, 0:6 * D], u[:, 6 * D:11 * D]
        ght = "p (g h t) -> p g h t"
        rqT, rkT = (u1[:, i * D:(i + 1) * D].rearrange(ght, g=2, h=H) for i in (0, 1))
        kdec = u1[:, 2 * D:3 * D].rearrange("p (d c) -> p d c", d=2)
        ratt = u1[:, 3 * D:4 * D].rearrange(ght, g=2, h=H)
        qdec = u1[:, 4 * D:5 * D].rearrange("p (d h t) -> p d h t", d=2, h=H)
        rope = u1[:, 5 * D:6 * D].rearrange("p (b c) -> p b c", b=2)
        nqT, nkT = (u2[:, i * D:(i + 1) * D].rearrange(ght, g=2, h=H) for i in (0, 1))
        lg1 = u2[:, 2 * D:3 * D].rearrange("p (h s t) -> p h s t", h=H, s=2)
        lg0 = u2[:, 3 * D:3 * D + W].rearrange("p (h t) -> p h t", h=H)
        pT0 = u2[:, 3 * D + W:4 * D].rearrange("p (h t) -> p h t", h=H)
        pT1 = u2[:, 4 * D:5 * D].rearrange("p (s h t) -> p s h t", s=2, h=H)
        hq, f_pre, f_suf, k_f, k_b, f_sufx = (u1[:, i * D:(i + 1) * D] for i in range(6))
        b_prex, q_lev, k_lev = (u2[:, i * D:(i + 1) * D] for i in range(3))
        hatt = u2[:, 4 * D:5 * D]
        act_s = u[:, 0:2 * W].rearrange("p (t c) -> p t c", t=2)[:, :, 0:FS]
        act_v = u[:, D:2 * D].rearrange("p (b t c) -> p b t c", b=2, t=2)
        act_hi, act_lo = (v.rearrange("p (t j m) -> p t j m", t=2, j=2) for v in (act_hi, act_lo))
        e_out = u[:, 3 * D:11 * D]

        br_ = sb("br", 2 * D)
        br = br_.rearrange("p (b g c) -> p b g c", b=2, g=2)
        ff_y = br_.rearrange("p (g c) -> p g c", g=2)
        h_rows = xn
        pick = gate[:, 0:4 * P].rearrange("p (g m) -> p g m", g=2)
        weigh = gate[:, 4 * P:8 * P].rearrange("p (b g m) -> p b g m", b=2, g=2)
        weighT = gate[:, 8 * P:12 * P].rearrange("p (b g m) -> p b g m", b=2, g=2)
        state0 = sb("state0", 2 * W).rearrange("p (d h c) -> p d h c", d=2, h=H)
        cache = sb("cache", 2 * W)
        ckT = cache[:, 0:W].rearrange("p (h t) -> p h t", h=H)
        cv = cache[:, W:2 * W]
        over_out = cache
        level_mask = sb("level_mask", 8 * P, I32).rearrange("p (v t) -> p v t", v=8)
        con = sb("con", NCONST)
        hgn_sb = sb("hgn_sb", W)
        rout_w = sb("rout_w", KD * E).rearrange("p (k e) -> p k e", k=KD)
        cond = sb("cond", KD * 2).rearrange("p (k g) -> p k g", k=KD)
        bm = sb("bm", L * NMOD).rearrange("p (l n) -> p l n", l=L)
        ng = sb("ng", L * 4 * KD).rearrange("p (l n k) -> p l n k", l=L, n=4)
        modc = sb("modc", NMOD * 2).rearrange("p (m k g) -> p m k g", m=6, k=KD)
        cond_pad = sb("cond_pad", KD * (2 * COND_PAD + 2)).rearrange("p (k c) -> p k c", k=KD)
        mod_rows = sb("mod_rows", 2 * 512).rearrange("p (b c) -> p b c", b=2)
        mod_raw = sb("mod_raw", L * NMOD * 2)
        lbr = sb("lbr", L * 8).rearrange("p (l n) -> p l n", l=L)
        lbw = sb("lbw", 6 * 8).rearrange("p (n c) -> p n c", n=6)
        lb = sb("lb", L * 8).rearrange("p (l n) -> p l n", l=L)
        olb = sb("olb", L * 8).rearrange("p (l n) -> p l n", l=L)
        dec = sb("dec", L * 8)
        lgw = sb("lgw", 2 * L * 8).rearrange("p (n c) -> p n c", n=2)
        lg = sb("lg", L * 8).rearrange("p (l d h) -> p l d h", l=L, d=2)
        kd = sb("kd", L * 8).rearrange("p (l d h) -> p l d h", l=L, d=2)
        ss = sb("ss", 4)
        ms = sb("ms", 2)
        rs = sb("rs", 2)
        bnst = sb("bnst", 8 * 6).rearrange("p (n c) -> p n c", n=8)
        mv = sb("mv", 8 * 2).rearrange("p (n c) -> p n c", n=8)
        hms = sb("hms", 8)
        hss = sb("hss", 8)
        hrs = sb("hrs", 8)
        negmax = sb("negmax", 8)
        psums = sb("psums", 8)
        pinv = sb("pinv", 8)
        rl = sb("rl", 2 * E).rearrange("p (g e) -> p g e", g=2)
        rmax = sb("rmax", 2 * 8).rearrange("p (g e) -> p g e", g=2)
        ridx = sb("ridx", 2 * 8, U32).rearrange("p (g e) -> p g e", g=2)
        rif = sb("rif", 2 * 8).rearrange("p (g e) -> p g e", g=2)
        rw = sb("rw", 2 * 8).rearrange("p (g e) -> p g e", g=2)
        rgate = sb("rgate", 2 * E).rearrange("p (g e) -> p g e", g=2)
        sel = sb("sel", 2 * E).rearrange("p (g e) -> p g e", g=2)
        place = sb("place", 2 * E).rearrange("p (g e) -> p g e", g=2)
        count = sb("count", E, I32)
        r1 = sb("r1", 2 * E).rearrange("p (g e) -> p g e", g=2)

        ps = ctx.enter_context(nc.psum_tensor("ps", [P, 8, 512], F32))

        def con_(name):
            return con[:, CONST_AT[name]:CONST_AT[name] + CONST_W[name]]

        ident = con_("ident")

        s_const = sem("constants_loaded")
        s_x = sem("x_loaded")
        slab_in = [sem(f"slab_in{s}") for s in range(SLOTS)]
        part_in = [[sem(f"part{p}_in{s}") for s in range(SLOTS)] for p in range(NPART)]
        s_bias = sem("bias_loaded")
        s_cache = sem("cache_loaded")
        s_sret = sem("state_ret_loaded")
        s_shg = sem("state_hgrn_loaded")
        s_hgn = sem("hgrn_norm_loaded")
        s_kout = sem("new_k_stored")
        s_vout = sem("new_v_stored")
        s_srout = sem("new_ret_stored")
        s_shout = sem("new_hgrn_stored")
        s_yout = sem("y_stored")

        cond_ready = sem("cond_ready")
        dve_step = sem("dve_step")
        act_step = sem("act_step")
        pool_step = sem("pool_step")
        lbexp_ready = sem("lbexp_ready")
        lbsub_ready = sem("lbsub_ready")
        decabs_ready = sem("decabs_ready")
        declog_ready = sem("declog_ready")
        lg_ready = sem("lg_ready")
        kdx_ready = sem("kdx_ready")
        kdexp_ready = sem("kdexp_ready")
        kd_ready = sem("kd_ready")
        mod_done = sem("mod_slab_done")
        pad_ready = sem("cond_pad_zero")
        mod_copied = sem("mod_rows_copied")
        mod_turned = sem("mod_rows_turned")
        mod_read = sem("mod_read")
        mod_rest = sem("mod_rest_ready")
        mod_ready = sem("mod_ready")
        sq_ready = sem("sq_ready")
        ms_ready = sem("ms_ready")
        rs_ready = sem("rs_ready")
        xn_ready = sem("xn_ready")
        xt_done = sem("xt_done")
        ht_dve = sem("ht_dve")
        ht_act = sem("ht_act")
        x_new = sem("x_new")
        win_done = sem("win_done")
        win_read = sem("win_read")
        exps_ready = sem("decay_exps_ready")
        decays_ready = sem("decays_ready")
        bias_ready = sem("bias_ready")
        rope_ready = sem("rope_ready")
        t_done = sem("turned")
        t_read_dve = sem("turned_read_dve")
        t_read_act = sem("turned_read_act")
        ratt_done = sem("ratt_done")
        ratt_ready = sem("ratt_ready")
        qdec_ready = sem("qdec_ready")
        kdec_ready = sem("kdec_ready")
        ro_done = sem("ro_done")
        ve_ready = sem("ve_ready")
        rsr_ready = sem("rsr_ready")
        ro_read = sem("ro_read")
        br_ready = sem("br_ready")
        rst_done = sem("ret_state_done")
        rst_read = sem("ret_state_read")
        na1_done = sem("na1_done")
        na1_read = sem("na1_read")
        na0_done = sem("na0_done")
        na0_read = sem("na0_read")
        max1_ready = sem("max1_ready")
        max0_ready = sem("max0_ready")
        p1_ready = sem("p1_ready")
        p0_ready = sem("p0_ready")
        pt1_done = sem("pt1_done")
        pt1_read = sem("pt1_read")
        pt0_done = sem("pt0_done")
        pt0_read = sem("pt0_read")
        pv_done = sem("pv_done")
        brt_done = sem("brt_done")
        brt_hi = sem("brt_hi_ready")
        brt_read = sem("brt_read")
        mix_hi = sem("mix_hi_ready")
        mix_lo = sem("mix_lo_ready")
        mix_half = sem("mix_half_used")
        mt_hi = sem("merged_hi_ready")
        lev_ready = sem("lev_ready")
        lev_done = sem("lev_done")
        lev_read = sem("lev_read")
        qk_end = sem("state_products_ready")
        ho_done = sem("ho_done")
        hsq_ready = sem("hsq_ready")
        hms_ready = sem("hms_ready")
        hrs_ready = sem("hrs_ready")
        ks_done = sem("ks_done")
        ks_read = sem("ks_read")
        hst_done = sem("hgrn_state_done")
        hst_read = sem("hgrn_state_read")
        pr_done = sem("proj_done")
        pr_read = sem("proj_read")
        merged_ready = sem("merged_ready")
        mt_done = sem("merged_turned")
        mt_read = sem("merged_T_ready")
        wo_done = sem("wo_done")
        post_read = sem("post_scaled")
        gb_done = sem("gate_rows_done")
        gua_done = sem("gu_first_done")
        gu_done = sem("gu_done")
        hi_ready = [sem(f"hi_ready{p}") for p in range(NPART)]
        lo_ready = [sem(f"lo_ready{p}") for p in range(NPART)]
        h_hi_ready = sem("h_hi_ready")
        h_lo_ready = sem("h_lo_ready")
        sil_ready = sem("silu_ready")
        act_ready = sem("act_ready")
        at_done = sem("act_turned")
        acth_ready = sem("act_hi_ready")
        actT_ready = sem("act_T_ready")
        down_done = sem("down_done")
        acc_read = sem("ffn_acc_read")
        pick_ready = sem("pick_ready")
        gather_done = sem("gather_done")
        gather_read_dve = sem("gather_read_dve")
        gather_read_act = sem("gather_read_act")
        over_pick_ready = sem("over_pick_ready")
        over_gather_done = sem("over_gather_done")
        over_read_dve = sem("over_read_dve")
        over_read_act = sem("over_read_act")
        over_acc_read = sem("over_acc_read")
        over_sum_done = sem("over_sum_done")
        over_sum_read = sem("over_sum_read")
        sel_ready = sem("sel_ready")
        place_done = sem("place_done")
        place_ready = sem("place_ready")
        back_done = sem("h_rows_done")
        back_read = sem("h_rows_ready")
        weigh_ready = sem("weigh_ready")
        weigh_done = sem("weigh_turned")
        weigh_read = sem("weigh_T_ready")
        sum_done = sem("expert_sums_done")
        y_ready = sem("ffn_rows_ready")
        rlog_done = sem("router_done")
        rcopy_ready = sem("router_read")
        rdiff_ready = sem("router_diff_ready")
        rexp_ready = sem("router_exp_ready")

        block = ctx.enter_context(nc.Block())

        def released(key):
            kind, l, i = key
            return {"mod": (mod_done, NSLAB_MOD * l + i + 1), "win": (win_done, NWIN * l + i + 1),
                    "br": (pr_done, 6 * l + 2 * i + 2), "wo": (wo_done, 2 * l + i + 1),
                    "ffn": (down_done, i + 1)}[kind]

        def input_count(l, n, g):
            return 4 * l + n + g + 1

        def mix_unit(l, m):
            return MIX_SLABS[l][m // 2], m % 2, (MIX_UNITS * l + m) % SLOTS, MIX_UNITS * l + m

        def mix_used(l, m):
            key, half, _, count = mix_unit(l, m)
            return released(key) if half else (mix_half, count // 2 + 1)

        part_used = (gua_done, gu_done, down_done)

        def part_loaded(p, e, i):
            return part_in[p][i % SLOTS], e * (16 * per_expert[i % SLOTS]) + 16 * (i // SLOTS + 1)

        @block.sync
        def _(sp):
            source = {"win": w_in, "br": w_br, "wo": w_o, "ffn": w_ff}

            def load(key):
                s, _, before = plan[key]
                if before is not None and before[0] != "ffn":
                    sp.wait_ge(*released(before))
                if key[0] == "ffn":
                    if before[0] == "ffn":
                        load_parts(0, key[2], before[2] + 1)
                    else:
                        load_parts(0, key[2], None, 0, NPART - 1)
                        if key[2] == SLOTS - 1:
                            last_parts(0, 0)
                    return
                if before is not None and before[0] == "ffn":
                    sp.wait_ge(*released(before))
                src = w_mod[key[1] * NSLAB_MOD + key[2]] if key[0] == "mod" else source[key[0]][key[1], key[2]]
                sp.dma_start(ring[s][:, 0:src.shape[1]], src).then_inc(slab_in[s], 16)

            def last_parts(l, n):
                sp.wait_ge(wo_done, 2 * l + 2)
                for i in range(SLOTS):
                    load_parts(n, i, None, NPART - 1, NPART)

            def load_parts(n, i, used, first=0, end=NPART):
                for p in range(first, end):
                    if used is not None:
                        sp.wait_ge(part_used[p], used)
                    part = slice(p * UNIT, (p + 1) * UNIT)
                    sp.dma_start(ring[i % SLOTS][:, part], w_ff[n, i][:, part]).then_inc(part_in[p][i % SLOTS], 16)

            for l in range(L):
                slabs = layer_slabs(l)
                if l == 0:
                    for s in range(SLOTS):
                        load(slabs[s])
                    with sp.Fori(1, MOD_TURNS) as t:
                        for s in range(SLOTS):
                            sp.wait_ge(mod_done, t * SLOTS + (s - SLOTS + 1))
                            sp.dma_start(ring[s][:, 0:KD * 512], w_mod[t * SLOTS + s]).then_inc(slab_in[s], 16)
                    slabs = slabs[MOD_TURNS * SLOTS:]
                for key in slabs:
                    if key[0] != "skip":
                        load(key)
                if l == 0:
                    for i in range(NFS):
                        load(("ffn", 0, i))
            for s in range(SLOTS):
                sp.wait_ge(*released(before0[s]))
                load_parts(1, s, None, 0, NPART - 1)
            last_parts(1, 1)

            def rest_of(e):
                for i in range(SLOTS, NFS):
                    load_parts(e + 1, i, e * NFS + (NFS + i - SLOTS + 1))

            with sp.Fori(0, E - 1) as e:
                rest_of(e)
                for s in range(SLOTS):
                    load_parts(e + 2, s, e * NFS + (NFS + max(i for i in range(NFS) if i % SLOTS == s) + 1))
            rest_of(E - 1)
            for q in (s_kout, s_vout, s_srout, s_shout):
                sp.wait_ge(q, 16 * L)
            sp.wait_ge(s_yout, 16)

        @block.gpsimd
        def _(pool):
            for dst, src in ((con, consts), (cond, c_t), (bm, b_mod_t), (ng, norm_t), (lbr, lb_t), (dec, decay),
                             (rout_w, router), (level_mask, levels)):
                pool.dma_start(dst, src).then_inc(s_const, 16)
            pool.dma_start(x_sb, x).then_inc(s_x, 16)

            def power(out, in_, done, n):
                pool.tensor_tensor(out, in_, con_("half")[:, 0:1].broadcast_to([P, n]), ALU.pow).then_inc(done, 1)

            for l in range(L):
                if l:
                    pool.wait_ge(pr_read, 6 * l)
                pool.dma_start(bias, rpb[l]).then_inc(s_bias, 16)
                if l:
                    pool.wait_ge(pv_done, l)
                    pool.wait_ge(ho_done, l)
                pool.dma_start(ckT, cache_kt[l]).then_inc(s_cache, 16)
                pool.dma_start(cv, cache_v[l]).then_inc(s_cache, 16)
                pool.dma_start(state0, s_ret[l]).then_inc(s_sret, 16)
                if l:
                    pool.wait_ge(br_ready, 3 * l)
                pool.dma_start(hgn_sb, hgn[l]).then_inc(s_hgn, 16)
                if l == 0:
                    pool.wait_ge(s_const, 16 * 8)
                pool.wait_ge(ms_ready, 4 * l + 1)
                power(rs, ms, rs_ready, 2)
                pool.wait_ge(kd_ready, 1)
                pool.wait_ge(win_read, NWIN * l + 2)
                for d in range(2):
                    for h in range(H):
                        last = pool.tensor_scalar(kdec[:, d, h * HD:(h + 1) * HD], stage[:, 1, 0, h * HD:(h + 1) * HD],
                                                  kd[:, l, d, h:h + 1], None, ALU.mult)
                last.then_inc(kdec_ready, 1)
                pool.wait_ge(ve_ready, l + 1)
                power(hrs, hms, rsr_ready, 8)
                pool.wait_ge(win_read, NWIN * l + 6)
                pool.dma_start(new_k[l], stage[:, 1, 0, :]).then_inc(s_kout, 16)
                pool.wait_ge(win_read, NWIN * l + 7)
                pool.dma_start(new_v[l], nv[:, 0, :]).then_inc(s_vout, 16)
                pool.wait_ge(rst_read, l + 1)
                pool.dma_start(new_ret[l], state_out).then_inc(s_srout, 16)
                pool.wait_ge(ro_done, l + 1)
                pool.dma_start(state0, s_hg[l]).then_inc(s_shg, 16)
                pool.wait_ge(hms_ready, l + 1)
                power(hrs, hms, hrs_ready, 8)
                pool.wait_ge(hst_read, l + 1)
                pool.dma_start(new_hg[l], state_out).then_inc(s_shout, 16)
                for n in (1, 2, 3):
                    pool.wait_ge(ms_ready, 4 * l + n + 1)
                    power(rs, ms, rs_ready, 2)
            pool.wait_ge(x_new, 2 * L)
            pool.dma_start(y, x_sb).then_inc(s_yout, 16)

        @block.scalar
        def _(act):
            A = nc.scalar.activation
            chain = [0]

            def pair(v):
                return v.rearrange("p (b c) -> p b c", b=2)

            def link(ins):
                chain[0] += 1
                ins.then_inc(act_step, 1)
                act.wait_ge(act_step, chain[0])

            act.wait_ge(s_const, 16 * 8)
            act.wait_ge(pad_ready, 1)
            A(cond_pad[:, :, COND_PAD:COND_PAD + 2], cond, ACT.Silu).then_inc(cond_ready, 1)
            act.wait_ge(lbsub_ready, 1)
            A(lbw[:, 1:3, :], lbw[:, 1:3, :], ACT.Exp).then_inc(lbexp_ready, 1)
            act.wait_ge(decabs_ready, 1)
            link(A(lgw[:, 0, :], lgw[:, 0, :], ACT.Exp, scale=-1.0))
            A(lgw[:, 0, :], lgw[:, 0, :], ACT.Ln, bias=con_("ones")[:, 0:1]).then_inc(declog_ready, 1)
            act.wait_ge(kdx_ready, 1)
            A(kd, kd, ACT.Exp).then_inc(kdexp_ready, 1)

            def squares_x(l, n):
                if n == 0 and l == 0:
                    act.wait_ge(s_x, 16)
                else:
                    act.wait_ge(x_new, 2 * l + (n == 2))
                for g in range(2):
                    ins = A(xn[:, g, :], x_sb[:, g, :], ACT.Square, accum_out=ss[:, g:g + 1])
                ins.then_inc(sq_ready, 1)

            def copy_mod(part):
                slabs = MOD_GROUPS[part]
                act.wait_ge(mod_done, slabs[-1] + 1)
                A(mod_rows[0:2 * len(slabs), part, :], ps[0:2 * len(slabs), part, :], ACT.Copy).then_inc(mod_copied, 1)

            def turn_read(l, n):
                w = 4 * l + 2 * (n == 2)
                for g in range(2):
                    act.wait_ge(xt_done, w + g + 1)
                    for k in range(4, KD):
                        m = 0 if n == 0 else 3
                        ins = A(h32[:, g, k, :], ps[:, 5 + 2 * g, (k - 4) * P:(k - 3) * P], ACT.Identity,
                                scale=modc[:, m + 1, k, g:g + 1], bias=modc[:, m, k, g:g + 1])
                    ins.then_inc(ht_act, 1)

            def post_norm(l, n, src):
                for g in range(2):
                    ins = A(xn[:, g, :], src[g], ACT.Square, accum_out=ss[:, g:g + 1])
                ins.then_inc(sq_ready, 1)
                act.wait_ge(rs_ready, 4 * l + n + 1)
                for g in range(2):
                    ins = A(xn[:, g, :], src[g], ACT.Copy, scale=rs[:, g:g + 1])
                ins.then_inc(post_read, 1)

            def softmax(l, lgt, off, done, ready):
                act.wait_ge(done, l + 1)
                for h in range(H):
                    v = lgt[:, h] if off else lgt[:, h, :]
                    v = v.rearrange("p s t -> p (s t)") if off else v
                    ins = A(v, v, ACT.Exp, bias=negmax[:, off + h:off + h + 1],
                            accum_out=psums[:, off + h:off + h + 1])
                ins.then_inc(ready, 1)

            def panel(l, j):
                act.wait_ge(win_done, NWIN * l + j + 1)
                func = ACT.Copy
                if j in STAGED:
                    q = STAGED.index(j)
                    if q >= 2:
                        act.wait_ge(t_done, 7 * l + q - 1)
                    if q == 3:
                        act.wait_ge(kdec_ready, l + 1)
                    if q == 5:
                        act.wait_ge(s_kout, 16 * (l + 1))
                    dst = [stage[:, q % 2, g, :] for g in range(2)]
                    if j == 7:
                        func = ACT.Silu
                elif j in (2, 10):
                    dst = [rv_hi[:, g, :] for g in range(2)]
                elif j in (3, 11):
                    if j == 11:
                        act.wait_ge(br_ready, 3 * l + 1)
                    dst = [rg_hg[:, g, :] for g in range(2)]
                    func = ACT.Silu
                elif j == 6:
                    if l:
                        act.wait_ge(s_vout, 16 * l)
                    dst = [nv[:, g, :] for g in range(2)]
                else:
                    if j == 12:
                        act.wait_ge(na1_read, l + 1)
                    elif j > 13:
                        act.wait_ge(pr_read, 6 * l + j - 13)
                    o = 512 * (j % 2)
                    dst = [gates[:, g, o:o + 512] for g in range(2)]
                    func = ACT.Sigmoid
                for g in range(2):
                    ins = A(dst[g], ps[:, 2 * (j % 2) + g, :], func)
                ins.then_inc(win_read, 1)

            def input_hi(l, n):
                for g in range(2):
                    act.wait_ge(ht_dve, 4 * l + n + g + 1)
                    act.wait_ge(ht_act, 4 * l + n + g + 1)
                    A(h_hi[:, g], h32[:, g], ACT.Copy).then_inc(h_hi_ready, 1)

            def mix_split(l, m):
                if m >= MIX_UNITS:
                    return
                key, half, b, count = mix_unit(l, m)
                s, u, _ = plan[key]
                act.wait_ge(slab_in[s], 16 * (u + 1))
                if m >= SLOTS:
                    act.wait_ge(*mix_used(l, m - SLOTS))
                elif l:
                    act.wait_ge(down_done, NFS)
                A(m_hi[b], ring[s][:, half * UNIT:(half + 1) * UNIT], ACT.Copy).then_inc(mix_hi, 1)

            def branch_hi(l, n, bank):
                act.wait_ge(brt_done, 3 * l + n + 1)
                A(bt_hi.rearrange("p g k t -> p g (k t)"), ps[:, bank:bank + 2, :], ACT.Copy).then_inc(brt_hi, 1)

            def split(p, e, i, count):
                act.wait_ge(*part_loaded(p, e, i))
                if count is not None:
                    act.wait_ge(part_used[p], count)
                A(w_hi[p], ring[i % SLOTS][:, p * UNIT:(p + 1) * UNIT], ACT.Copy).then_inc(hi_ready[p], 1)

            def ffn(tiles, e, last, first=False):
                base = e * NFS
                for i in range(NFS):
                    ahead = (e + 1, 0) if i == NFS - 1 else (e, i + 1)
                    if i < NFS - 1 or not last:
                        split(0, *ahead, base + (i + 1))
                    act.wait_ge(gu_done, base + (i + 1))
                    if not (i == 0 and first):
                        act.wait_ge(act_ready, base + i)
                    A(act_s[:, 0:tiles, :], ps[:, 4:4 + tiles, 0:FS], ACT.Silu).then_inc(sil_ready, 1)
                    if i < NFS - 1 or not last:
                        split(1, *ahead, base + (i + 1))
                    act.wait_ge(at_done, base + (i + 1))
                    A(act_hi[:, 0:tiles].rearrange("p t j m -> p t (j m)"), ps[:, 6:6 + tiles, 0:FS], ACT.Copy)\
                        .then_inc(acth_ready, 1)
                    split(2, e, i, None if i == 0 and first else base + i)

            def split_first(l, p):
                if p == 0:
                    act.wait_ge(br_ready, 3 * (l + 1))
                else:
                    act.wait_ge(pr_done, 6 * (l + 1))
                split(p, l, 0, l * NFS if l else None)

            def expert(e, last):
                base = e * NFS + NFS
                act.wait_ge(gather_done, e + 1)
                for b in range(2):
                    A(h_hi[:, 0, 4 * b:4 * b + 4, :].rearrange("p k m -> p (k m)"), ps[:, 4 + b, :], ACT.Copy)\
                        .then_inc(gather_read_act, 1)
                rows_out = e_out[:, bass.ds(e * D, D)].rearrange("p (b c) -> p b c", b=2)

                def read_sums():
                    act.wait_ge(down_done, base + NFS)
                    A(rows_out, ps[:, 0:2, :], ACT.Copy).then_inc(acc_read, 1)

                n = act.value_load(count[0:1, bass.ds(e, 1)])
                with act.If(n > P):
                    act.wait_ge(over_gather_done, e + 1)
                    A(h_hi[:, 1].rearrange("p (b k) m -> p b (k m)", b=2), ps[:, 4:6, :], ACT.Copy)
                    A(weighT[:, 0], ps[:, 6, 0:2 * P].rearrange("p (g m) -> p g m", g=2), ACT.Copy).then_inc(over_read_act, 1)
                    ffn(2, e + 1, last)
                    read_sums()
                    A(pair(over_out), ps[:, 2:4, :], ACT.Copy).then_inc(over_acc_read, 1)
                with act.Else():
                    act.sem_inc(over_read_act, 1)
                    act.sem_inc(over_acc_read, 1)
                    ffn(1, e + 1, last)
                    read_sums()

            for l in range(L):
                squares_x(l, 0)
                act.wait_ge(lg_ready, 1)
                if l:
                    act.wait_ge(pr_read, 6 * l)
                for d in range(2):
                    for h in range(H):
                        A(ratt[:, d, h, :], con_(("above", "below")[d]), ACT.Exp, scale=lg[:, l, d, h:h + 1])
                        ins = A(q_dec[:, d, h, :], con_(("ramp_up", "ramp_down")[d]), ACT.Exp,
                                scale=lg[:, l, d, h:h + 1])
                ins.then_inc(exps_ready, 1)
                if l:
                    mix_split(l, 0)
                else:
                    copy_mod(0)
                act.wait_ge(mod_ready, l + 1)
                turn_read(l, 0)
                input_hi(l, 0)
                if l == 0:
                    copy_mod(1)
                for m in range(l, SLOTS):
                    mix_split(l, m)
                for j in range(NWIN):
                    c = STEP["win", j]
                    mix_split(l, 2 * c + 3)
                    panel(l, j)
                    mix_split(l, 2 * c + 4)
                    if j in BR_AFTER and j < NWIN - 1:
                        mix_split(l, 2 * c + 5)
                        mix_split(l, 2 * c + 6)
                    if j == 12:
                        branch_hi(l, 0, 4)
                    if j == 14:
                        branch_hi(l, 1, 4)
                    if j == 6:
                        act.wait_ge(rst_done, l + 1)
                        if l:
                            act.wait_ge(s_shout, 16 * l)
                        A(state_out.rearrange("p (b c) -> p b c", b=2), ps[:, 4:6, :], ACT.Copy).then_inc(rst_read, 1)
                    if j == 8:
                        softmax(l, lg1, 4, max1_ready, p1_ready)
                    if j == 9:
                        softmax(l, lg0, 0, max0_ready, p0_ready)
                    if j in (9, 10):
                        q = j - 4
                        act.wait_ge(t_done, 7 * l + q + 1)
                        dst = (f_pre, f_suf)[q - 5].rearrange("p (g c) -> p g c", g=2)
                        A(dst, ps[:, 6:8, :], ACT.Sigmoid).then_inc(t_read_act, 1)
                act.wait_ge(ho_done, l + 1)
                for g in range(2):
                    for h in range(H):
                        ins = A(f_pre[:, (4 * g + h) * HD:(4 * g + h + 1) * HD], ps[:, 6 + g, h * HD:(h + 1) * HD], ACT.Square,
                                accum_out=hss[:, 4 * g + h:4 * g + h + 1])
                ins.then_inc(hsq_ready, 1)
                act.wait_ge(ks_done, l + 1)
                A(q_lev.rearrange("p (b c) -> p b c", b=2), ps[:, 4:6, :], ACT.Copy).then_inc(ks_read, 1)
                act.wait_ge(hst_done, l + 1)
                act.wait_ge(s_srout, 16 * (l + 1))
                A(state_out.rearrange("p (b c) -> p b c", b=2), ps[:, 4:6, :], ACT.Copy).then_inc(hst_read, 1)
                branch_hi(l, 2, 6)
                mix_split(l, MIX_UNITS - 3)
                mix_split(l, MIX_UNITS - 2)
                for g in range(2):
                    act.wait_ge(mt_done, 2 * l + g + 1)
                    A(h_hi[:, g].rearrange("p (b k) t -> p b (k t)", b=2), ps[:, 4 + 2 * g:6 + 2 * g, :], ACT.Copy)\
                        .then_inc(mt_hi, 1)
                mix_split(l, MIX_UNITS - 1)
                split_first(l, 0)
                split_first(l, 1)
                act.wait_ge(wo_done, 2 * l + 2)
                post_norm(l, 1, [ps[:, 2 * g:2 * g + 2, :].rearrange("p b c -> p (b c)") for g in range(2)])
                squares_x(l, 2)
                if l == 0:
                    act.wait_ge(mod_rest, 1)
                turn_read(l, 2)
                act.wait_ge(s_vout, 16 * (l + 1))
                act.wait_ge(s_shout, 16 * (l + 1))
                if l == 0:
                    input_hi(0, 2)
                    ffn(2, 0, True, True)
                    act.wait_ge(down_done, NFS)
                    post_norm(l, 3, [ps[:, 2 * g:2 * g + 2, :].rearrange("p b c -> p (b c)") for g in range(2)])
                else:
                    act.wait_ge(rdiff_ready, 1)
                    A(rw[:, :, 1:2], rw[:, :, 1:2], ACT.Exp).then_inc(rexp_ready, 1)
                    act.wait_ge(place_ready, 1)
                    act.sem_inc(acc_read, 1)
                    with act.Fori(0, E - 1) as e:
                        expert(e, False)
                    expert(E - 1, True)
                    for e in range(E):
                        act.wait_ge(weigh_done, e + 1)
                        A(weighT[:, e % 2], ps[:, 4 + e % 2, 0:2 * P].rearrange("p (g m) -> p g m", g=2), ACT.Copy)\
                            .then_inc(weigh_read, 1)
                    act.wait_ge(y_ready, 1)
                    post_norm(l, 3, [ff_y[:, g, :] for g in range(2)])

        @block.tensor
        def _(pe):
            mm = nc.tensor.matmul

            def modulate(part):
                slabs = MOD_GROUPS[part]
                rows_ = 2 * len(slabs)
                for i, n in enumerate(slabs):
                    s, u, _ = plan[("mod", n // NSLAB_MOD, n % NSLAB_MOD)]
                    pe.wait_ge(slab_in[s], 16 * (u + 1))
                    w = ring[s][:, 0:KD * 512].rearrange("p (k c) -> p k c", k=KD)
                    at = COND_PAD - 2 * i
                    for k in range(KD):
                        ins = mm(ps[0:rows_, part, :], cond_pad[:, k, at:at + rows_], w[:, k, :],
                                 start=(i == 0 and k == 0), stop=(n == slabs[-1] and k == KD - 1), skip_group_check=True)
                    ins.then_inc(mod_done, 1)

            def turn_mod(part):
                rows_ = 2 * len(MOD_GROUPS[part])
                pe.wait_ge(mod_copied, part + 1)
                for c in range(4):
                    ins = nc.tensor.transpose(ps[:, 2 + part, c * rows_:(c + 1) * rows_],
                                              mod_rows[0:rows_, part, c * P:(c + 1) * P], ident[0:rows_, 0:rows_])
                ins.then_inc(mod_turned, 1)

            def turn_rows(l, n):
                w = 4 * l + 2 * (n == 2)
                for g in range(2):
                    pe.wait_ge(xn_ready, w + g + 1)
                    for k in range(KD):
                        ins = nc.tensor.transpose(ps[:, 4 + 2 * g + k // 4, (k % 4) * P:(k % 4 + 1) * P],
                                                  xn[:, g, k * P:(k + 1) * P], ident)
                    ins.then_inc(xt_done, 1)

            def product(out, a_hi, a_lo, b_hi, b_lo, start, stop):
                mm(out, a_hi, b_lo, start=start, stop=False, skip_group_check=True)
                mm(out, a_lo, b_hi, start=False, stop=False, skip_group_check=True)
                return mm(out, a_hi, b_hi, start=False, stop=stop, skip_group_check=True)

            def unit(l, step, half, blocks):
                key, half, b, count = mix_unit(l, 2 * step + half)
                pe.wait_ge(mix_lo, count + 1)
                pe.wait_ge(mix_hi, count + 1)
                lo = ring_lo[plan[key][0]][:, half * UNIT:(half + 1) * UNIT]
                return [v.rearrange("p (k c) -> p k c", k=blocks) for v in (m_hi[b], lo)]

            def panel(l, j):
                if j >= 2:
                    pe.wait_ge(win_read, NWIN * l + j - 1)
                if j >= 14:
                    pe.wait_ge(pr_read, 6 * l + j - 13)
                if j == 0:
                    pe.wait_ge(h_hi_ready, input_count(l, 0, 1))
                    pe.wait_ge(h_lo_ready, input_count(l, 0, 1))
                    pe.wait_ge(mod_ready, l + 1)
                    pe.wait_ge(mod_read, 1)
                for half in range(2):
                    hi, lo = unit(l, STEP["win", j], half, 4)
                    for g in range(2):
                        for k in range(4):
                            ins = product(ps[:, 2 * (j % 2) + g, :], h_hi[:, g, 4 * half + k, :], h_lo[:, g, 4 * half + k, :],
                                          hi[:, k, :], lo[:, k, :], half == 0 and k == 0, half == 1 and k == 3)
                    ins.then_inc((mix_half, win_done)[half], 1)

            def turn_panel(l, q):
                pe.wait_ge(win_read, NWIN * l + STAGED[q] + 1)
                if q < 2:
                    pe.wait_ge(rope_ready, 2 * l + q + 1)
                if 1 <= q <= 5:
                    pe.wait_ge(t_read_dve, 5 * l + q)
                elif q == 6:
                    pe.wait_ge(t_read_act, 2 * l + 1)
                for g in range(2):
                    src = rope[:, 0, :] if (q < 2 and g == 1) else stage[:, q % 2, g, :]
                    for h in range(H):
                        ins = nc.tensor.transpose(ps[:, 6 + g, h * P:(h + 1) * P], src[:, h * HD:(h + 1) * HD], ident)
                ins.then_inc(t_done, 1)

            def turn_heads(l, n, src, bank):
                pe.wait_ge(br_ready, 3 * l + n + 1)
                for g in range(2):
                    for h in range(H):
                        ins = nc.tensor.transpose(ps[:, bank + g, h * P:(h + 1) * P], src[:, g, h * HD:(h + 1) * HD], ident)
                ins.then_inc(brt_done, 1)

            def level(l, v):
                pe.wait_ge(lev_ready, 8 * l + v + 1)
                if v == 0:
                    pe.wait_ge(t_read_act, 2 * l + 2)
                else:
                    pe.wait_ge(lev_read, 8 * l + v)
                q = hq if v == NLEV else q_lev
                for u in range(8):
                    ins = mm(ps[:, 6 + u // 4, (u % 4) * P:(u % 4 + 1) * P], k_lev[:, u * P:(u + 1) * P],
                             q[:, u * P:(u + 1) * P], start=True, stop=True)
                ins.then_inc(lev_done, 1)

            def project(l, n):
                pe.wait_ge(brt_read, 3 * l + n + 1)
                pe.wait_ge(brt_hi, 3 * l + n + 1)
                pe.wait_ge(win_read, NWIN * l + 14 + 2 * n)
                for part in range(2):
                    hi, lo = unit(l, STEP["br", n], part, 2)
                    for half in range(2):
                        cols = slice(half * 512, (half + 1) * 512)
                        for g in range(2):
                            for k in range(2):
                                ins = product(ps[:, 2 * half + g, :], bt_hi[:, g, 2 * part + k, :], bt_lo[:, g, 2 * part + k, :],
                                              hi[:, k, cols], lo[:, k, cols], part == 0 and k == 0, part == 1 and k == 1)
                        if part == 1:
                            ins.then_inc(pr_done, 1)
                    if part == 0:
                        ins.then_inc(mix_half, 1)

            def turn_merged(l):
                pe.wait_ge(merged_ready, l + 1)
                pe.wait_ge(hst_read, l + 1)
                for g in range(2):
                    for k in range(KD):
                        ins = nc.tensor.transpose(ps[:, 4 + 2 * g + k // 4, (k % 4) * P:(k % 4 + 1) * P],
                                                  merged[:, g, k * P:(k + 1) * P], ident)
                    ins.then_inc(mt_done, 1)

            def output(l):
                pe.wait_ge(mt_hi, 2 * l + 2)
                pe.wait_ge(mt_read, 2 * l + 2)
                pe.wait_ge(pr_read, 6 * l + 6)
                for half in range(2):
                    for part in range(2):
                        hi, lo = unit(l, STEP["wo", half], part, 4)
                        for g in range(2):
                            for k in range(4):
                                ins = product(ps[:, 2 * g + half, :], h_hi[:, g, 4 * part + k, :], h_lo[:, g, 4 * part + k, :],
                                              hi[:, k, :], lo[:, k, :], part == 0 and k == 0, part == 1 and k == 3)
                        ins.then_inc((mix_half, wo_done)[part], 1)

            def gate_rows(l, n, m):
                if l == 0 and n == 0:
                    pe.wait_ge(mod_rest, 1)
                if n == 1:
                    pe.wait_ge(actT_ready, NFS if l == 0 else NFS * (E + 1))
                    pe.wait_ge(act_ready, NFS if l == 0 else NFS * (E + 1))
                    if l:
                        pe.wait_ge(weigh_read, E)
                for g in range(2):
                    for k in range(KD):
                        col = modc[:, m, k, g:g + 1].broadcast_to([P, P])
                        ins = mm(ps[:, 4 + 2 * g + k // 4, (k % 4) * P:(k % 4 + 1) * P], col, ident, start=True, stop=True)
                ins.then_inc(gb_done, 1)

            def ffn(tiles, base, acc_wait):
                for i in range(NFS + 1):
                    if i:
                        pe.wait_ge(act_ready, base + i)
                        for t in range(tiles):
                            for j in range(2):
                                ins = nc.tensor.transpose(ps[:, 6 + t, j * P:(j + 1) * P],
                                                          act_v[:, (i - 1) % 2, t, j * P:(j + 1) * P], ident)
                        ins.then_inc(at_done, 1)
                    if i < NFS:
                        for p, done in ((0, gua_done), (1, gu_done)):
                            pe.wait_ge(lo_ready[p], base + (i + 1))
                            pe.wait_ge(hi_ready[p], base + (i + 1))
                            blocks = [v.rearrange("p (k c) -> p k c", k=4)
                                      for v in (w_hi[p], ring_lo[i % SLOTS][:, p * UNIT:(p + 1) * UNIT])]
                            for t in range(tiles):
                                for k in range(4):
                                    ins = product(ps[:, 4 + t, :], h_hi[:, t, 4 * p + k, :], h_lo[:, t, 4 * p + k, :],
                                                  blocks[0][:, k, :], blocks[1][:, k, :], p == 0 and k == 0, p == 1 and k == 3)
                            ins.then_inc(done, 1)
                    if i:
                        blocks = [v.rearrange("p (j c) -> p j c", j=2)
                                  for v in (w_hi[2], ring_lo[(i - 1) % SLOTS][:, 2 * UNIT:3 * UNIT])]
                        pe.wait_ge(lo_ready[2], base + i)
                        pe.wait_ge(hi_ready[2], base + i)
                        pe.wait_ge(acth_ready, base + i)
                        pe.wait_ge(actT_ready, base + i)
                        if i == 1:
                            acc_wait()
                        for t in range(tiles):
                            for half in range(2):
                                cols = slice(half * 512, (half + 1) * 512)
                                for j in range(2):
                                    ins = product(ps[:, 2 * t + half, :], act_hi[:, t, j, :], act_lo[:, t, j, :],
                                                  blocks[0][:, j, cols], blocks[1][:, j, cols],
                                                  i == 1 and j == 0, i == NFS and j == 1)
                        ins.then_inc(down_done, 1)

            def gather(t):
                for k in range(KD):
                    for g in range(2):
                        ins = mm(ps[:, 4 + k // 4, (k % 4) * P:(k % 4 + 1) * P], h_rows[:, g, k * P:(k + 1) * P],
                                 pick[:, g, t * P:(t + 1) * P], start=(g == 0), stop=(g == 1))
                return ins

            def expert(e, base):
                pe.wait_ge(pick_ready, e + 1)
                gather(0).then_inc(gather_done, 1)
                pe.wait_ge(gather_read_dve, e + 1)
                pe.wait_ge(gather_read_act, e * 2 + 2)

                def acc_wait():
                    pe.wait_ge(acc_read, e + 1)

                n = pe.value_load(count[0:1, bass.ds(e, 1)])
                with pe.If(n > P):
                    pe.wait_ge(over_pick_ready, e + 1)
                    gather(1)
                    for g in range(2):
                        ins = nc.tensor.transpose(ps[:, 6, g * P:(g + 1) * P], weigh[:, 0, g, :], ident)
                    ins.then_inc(over_gather_done, 1)
                    pe.wait_ge(over_read_dve, e + 1)
                    pe.wait_ge(over_read_act, e + 1)
                    ffn(2, base, acc_wait)
                    pe.wait_ge(over_acc_read, e + 1)
                    for g in range(2):
                        for half in range(2):
                            ins = mm(ps[:, 4 + 2 * g + half, :], weighT[:, 0, g, :], over_out[:, half * 512:(half + 1) * 512],
                                     start=True, stop=True)
                    ins.then_inc(over_sum_done, 1)
                    pe.wait_ge(over_sum_read, e + 2)
                with pe.Else():
                    pe.sem_inc(over_gather_done, 1)
                    pe.sem_inc(over_sum_done, 1)
                    ffn(1, base, acc_wait)

            def pieces(l, j):
                if j in (1, 2, 5, 6, 8, 9, 10):
                    turn_panel(l, (1, 2, 5, 6, 8, 9, 10).index(j))
                if j == 3:
                    pe.wait_ge(t_read_dve, 5 * l + 2)
                    for g in range(2):
                        for h in range(H):
                            ins = mm(ps[:, 4 + g, h * P:(h + 1) * P], rkT[:, g, h, :], rqT[:, g, h, :], start=True, stop=True)
                    ins.then_inc(ratt_done, 1)
                if j == 4:
                    pe.wait_ge(ratt_ready, l + 1)
                    pe.wait_ge(qdec_ready, l + 1)
                    pe.wait_ge(s_sret, 16 * (l + 1))
                    pe.wait_ge(win_read, NWIN * l + 3)
                    for g in range(2):
                        for h in range(H):
                            out = ps[:, 4 + g, h * HD:(h + 1) * HD]
                            ins = mm(out, ratt[:, g, h, :], rv_hi[:, g, h * HD:(h + 1) * HD], start=True, stop=(g == 0))
                            if g:
                                mm(out, qdec[:, 0, h, :], state0[:, 0, h, :], start=False, stop=False)
                                ins = mm(out, qdec[:, 1, h, :], state0[:, 1, h, :], start=False, stop=True)
                    ins.then_inc(ro_done, 1)
                if j == 6:
                    pe.wait_ge(ro_read, l + 1)
                    pe.wait_ge(kdec_ready, l + 1)
                    for d in range(2):
                        for h in range(H):
                            ins = mm(ps[:, 4 + d, h * HD:(h + 1) * HD], kdec[:, d, h * HD:(h + 1) * HD],
                                     rv_hi[:, 0, h * HD:(h + 1) * HD], start=True, stop=True)
                    ins.then_inc(rst_done, 1)
                if j == 7:
                    pe.wait_ge(t_read_dve, 5 * l + 4)
                    pe.wait_ge(s_cache, 32 * (l + 1))
                    pe.wait_ge(rst_read, l + 1)
                    for s, keys in ((0, nkT[:, 1]), (1, ckT)):
                        for h in range(H):
                            ins = mm(ps[:, 4 + s, h * P:(h + 1) * P], nqT[:, 1, h, :], keys[:, h, :], start=True, stop=True)
                    ins.then_inc(na1_done, 1)
                if j == 8:
                    pe.wait_ge(na1_read, l + 1)
                    for h in range(H):
                        ins = mm(ps[:, 4, h * P:(h + 1) * P], nqT[:, 0, h, :], nkT[:, 0, h, :], start=True, stop=True)
                    ins.then_inc(na0_done, 1)
                if j == 9:
                    pe.wait_ge(p1_ready, l + 1)
                    pe.wait_ge(na0_read, l + 1)
                    for s in range(2):
                        for h in range(H):
                            ins = nc.tensor.transpose(ps[:, 4 + s, h * P:(h + 1) * P], lg1[:, h, s, :], ident)
                    ins.then_inc(pt1_done, 1)
                if j == 10:
                    pe.wait_ge(p0_ready, l + 1)
                    pe.wait_ge(pt1_read, l + 1)
                    for h in range(H):
                        ins = nc.tensor.transpose(ps[:, 4, h * P:(h + 1) * P], lg0[:, h, :], ident)
                    ins.then_inc(pt0_done, 1)
                if j == 11:
                    pe.wait_ge(pt0_read, l + 1)
                    for h in range(H):
                        hc = slice(h * HD, (h + 1) * HD)
                        mm(ps[:, 4, hc], pT0[:, h, :], nv[:, 0, hc], start=True, stop=True)
                    for h in range(H):
                        hc = slice(h * HD, (h + 1) * HD)
                        mm(ps[:, 5, hc], pT1[:, 0, h, :], nv[:, 1, hc], start=True, stop=False)
                        ins = mm(ps[:, 5, hc], pT1[:, 1, h, :], cv[:, hc], start=False, stop=True)
                    ins.then_inc(pv_done, 1)
                    level(l, 0)
                if j == 12:
                    pe.wait_ge(br_ready, 3 * l + 2)
                    turn_heads(l, 0, br[:, 0], 4)
                    level(l, 1)
                if j == 13:
                    level(l, 2)
                if j == 14:
                    turn_heads(l, 1, br[:, 1], 4)
                if j in (14, 15):
                    level(l, j - 10)
                if j == 16:
                    level(l, NLEV)
                if j == 17:
                    recurrence_out(l)

            def recurrence_out(l):
                pe.wait_ge(lev_read, 8 * l + 8)
                pe.wait_ge(qk_end, l + 1)
                pe.wait_ge(s_shg, 16 * (l + 1))
                for g in range(2):
                    for h in range(H):
                        hc = slice(h * HD, (h + 1) * HD)
                        u = 4 * g + h
                        ins = mm(ps[:, 6 + g, hc], hatt[:, u * P:(u + 1) * P], rv_hi[:, g, hc], start=True, stop=(g == 0))
                        if g:
                            mm(ps[:, 7, hc], q_lev[:, hc], state0[:, 0, h, :], start=False, stop=False)
                            ins = mm(ps[:, 7, hc], q_lev[:, W + h * HD:W + (h + 1) * HD], state0[:, 1, h, :],
                                     start=False, stop=True)
                ins.then_inc(ho_done, 1)
                pe.wait_ge(brt_read, 3 * l + 2)
                for d in range(2):
                    for h in range(H):
                        a = d * W + h * HD
                        ins = nc.tensor.transpose(ps[:, 4 + d, h * P:(h + 1) * P], k_lev[:, a:a + HD], ident)
                ins.then_inc(ks_done, 1)
                pe.wait_ge(ks_read, l + 1)
                for d in range(2):
                    for h in range(H):
                        hc = slice(h * HD, (h + 1) * HD)
                        ins = mm(ps[:, 4 + d, hc], q_lev[:, d * W + h * HD:d * W + (h + 1) * HD], rv_hi[:, 0, hc],
                                 start=True, stop=True)
                ins.then_inc(hst_done, 1)
                turn_heads(l, 2, br[:, 0], 6)

            pe.wait_ge(cond_ready, 1)
            modulate(0)
            turn_rows(0, 0)
            turn_mod(0)
            modulate(1)
            turn_mod(1)
            for l in range(L):
                if l:
                    turn_rows(l, 0)
                for j in range(NWIN):
                    panel(l, j)
                    pieces(l, j)
                    if j in BR_AFTER:
                        project(l, BR_AFTER[j])
                        if j < NWIN - 1:
                            level(l, 3 if j == 13 else 6)
                turn_merged(l)
                output(l)
                gate_rows(l, 0, 2)
                turn_rows(l, 2)
                pe.wait_ge(ht_dve, 4 * l + 4)
                pe.wait_ge(ht_act, 4 * l + 4)
                if l == 0:
                    pe.wait_ge(h_hi_ready, input_count(0, 2, 1))
                    pe.wait_ge(h_lo_ready, input_count(0, 2, 1))
                    ffn(2, 0, lambda: pe.wait_ge(post_read, 1))
                else:
                    for g in range(2):
                        for k in range(KD):
                            ins = mm(ps[:, 0, g * E:(g + 1) * E], h32[:, g, k, :], rout_w[:, k, :], start=(k == 0), stop=(k == KD - 1))
                    ins.then_inc(rlog_done, 1)
                    for g in range(2):
                        for k in range(KD):
                            ins = nc.tensor.transpose(ps[:, 4 + 2 * g + k // 4, (k % 4) * P:(k % 4 + 1) * P], h32[:, g, k, :], ident)
                    ins.then_inc(back_done, 1)
                    pe.wait_ge(sel_ready, 1)
                    mm(ps[:, 0, 0:E], con_("before"), sel[:, 0, :], start=True, stop=True)
                    mm(ps[:, 0, E:2 * E], con_("before"), sel[:, 1, :], start=True, stop=False)
                    mm(ps[:, 0, E:2 * E], con_("ones"), sel[:, 0, :], start=False, stop=True)
                    for g in range(2):
                        ins = mm(ps[:, 0, 2 * E:3 * E], con_("ones"), sel[:, g, :], start=(g == 0), stop=(g == 1))
                    ins.then_inc(place_done, 1)
                    pe.wait_ge(place_ready, 1)
                    pe.wait_ge(back_read, 1)
                    with pe.Fori(0, E) as e:
                        expert(e, e * NFS + NFS)
                    pe.wait_ge(acc_read, E + 1)
                    for e in range(E + 1):
                        if e < E:
                            pe.wait_ge(weigh_ready, e + 1)
                            if e >= 2:
                                pe.wait_ge(weigh_read, e - 1)
                            for g in range(2):
                                ins = nc.tensor.transpose(ps[:, 4 + e % 2, g * P:(g + 1) * P], weigh[:, e % 2, g, :], ident)
                            ins.then_inc(weigh_done, 1)
                        if e:
                            pe.wait_ge(weigh_read, e)
                            for g in range(2):
                                for half in range(2):
                                    a = (e - 1) * D + half * 512
                                    ins = mm(ps[:, 2 * g + half, :], weighT[:, (e - 1) % 2, g, :], e_out[:, a:a + 512],
                                             start=(e == 1), stop=(e == E), skip_group_check=True)
                    ins.then_inc(sum_done, 1)
                gate_rows(l, 1, 5)

        @block.vector
        def _(dve):
            V = nc.vector
            chain = [0]

            def link(ins):
                chain[0] += 1
                ins.then_inc(dve_step, 1)
                dve.wait_ge(dve_step, chain[0])

            def own(ins, s, value):
                ins.then_inc(s, 1)
                dve.wait_ge(s, value)

            V.memset(cond_pad, 0.0).then_inc(pad_ready, 1)
            dve.wait_ge(s_const, 16 * 8)
            link(V.tensor_tensor(lbw[:, 0, :], lbr[:, 0, :], lbr[:, 1, :], ALU.max))
            V.tensor_tensor(lbw[:, 1, :], lbr[:, 0, :], lbw[:, 0, :], ALU.subtract)
            V.tensor_tensor(lbw[:, 2, :], lbr[:, 1, :], lbw[:, 0, :], ALU.subtract).then_inc(lbsub_ready, 1)
            dve.wait_ge(lbexp_ready, 1)
            link(V.tensor_tensor(lbw[:, 3, :], lbw[:, 1, :], lbw[:, 2, :], ALU.add))
            link(V.reciprocal(lbw[:, 4, :], lbw[:, 3, :]))
            link(V.tensor_tensor(lbw[:, 1:3, :], lbw[:, 1:3, :], lbw[:, 4, :].unsqueeze(1).broadcast_to([P, 2, 8]), ALU.mult))
            V.tensor_tensor(lb[:, 0, :], lbw[:, 1, :], lbw[:, 1, :], ALU.subtract)
            link(V.tensor_tensor(lbw[:, 5, :], lbw[:, 1, :], lbw[:, 2, :], ALU.add))
            link(V.tensor_tensor(lb[:, 1, :], lbw[:, 5, :], lbw[:, 1, :], ALU.subtract))
            V.tensor_scalar(olb, lb, -1.0, 1.0, ALU.mult, ALU.add)
            V.scalar_tensor_tensor(lgw[:, 0, :], dec, -1.0, dec, ALU.mult, ALU.max).then_inc(decabs_ready, 1)
            dve.wait_ge(declog_ready, 1)
            lgf = lg.rearrange("p l d h -> p (l d h)")
            own(V.scalar_tensor_tensor(lgf, dec, 0.0, lgw[:, 0, :], ALU.min, ALU.subtract), lg_ready, 1)
            for d in range(2):
                ins = V.tensor_scalar(kd[:, :, d, :], lg[:, :, d, :], con_("age")[:, d:d + 1], None, ALU.mult)
            ins.then_inc(kdx_ready, 1)
            dve.wait_ge(kdexp_ready, 1)
            V.tensor_scalar(kd, kd, HD ** -0.5, None, ALU.mult).then_inc(kd_ready, 1)

            def mean_square(l, n):
                dve.wait_ge(sq_ready, 4 * l + n + 1)
                V.tensor_scalar(ms, ss[:, 0:2], 1.0 / D, EPS, ALU.mult, ALU.add).then_inc(ms_ready, 1)

            def rows(l, n):
                dve.wait_ge(rs_ready, 4 * l + n + 1)
                for g in range(2):
                    V.tensor_scalar(xn[:, g, :], x_sb[:, g, :], rs[:, g:g + 1], None, ALU.mult).then_inc(xn_ready, 1)

            def turn_read(l, n):
                w = 4 * l + 2 * (n == 2)
                m = 0 if n == 0 else 3
                for g in range(2):
                    dve.wait_ge(xt_done, w + g + 1)
                    for k in range(4):
                        ins = V.tensor_scalar(h32[:, g, k, :], ps[:, 4 + 2 * g, k * P:(k + 1) * P],
                                              modc[:, m + 1, k, g:g + 1], modc[:, m, k, g:g + 1], ALU.mult, ALU.add)
                    ins.then_inc(ht_dve, 1)

            def read_mod(part):
                slabs = MOD_GROUPS[part]
                dve.wait_ge(mod_turned, part + 1)
                return V.tensor_copy(mod_raw[:, 8 * slabs[0]:8 * slabs[-1] + 8].rearrange("p (n c g) -> p n c g", c=4, g=2),
                                     ps[:, 2 + part, 0:8 * len(slabs)].rearrange("p (c n g) -> p n c g", c=4, g=2))

            def modulation(l, first, end, raw, done, value):
                blocks = slice(first * KD, end * KD)
                link(V.tensor_tensor(modc.rearrange("p m k g -> p (m k) g")[:, blocks], raw.rearrange("p (n g) -> p n g", g=2),
                                     bm[:, l, blocks].unsqueeze(2).broadcast_to([P, (end - first) * KD, 2]), ALU.add))
                for m, n in ((1, 0), (4, 2)):
                    if first <= m < end:
                        ins = V.scalar_tensor_tensor(modc[:, m], modc[:, m], 1.0,
                                                     ng[:, l, n, :].unsqueeze(2).broadcast_to([P, KD, 2]), ALU.add, ALU.mult)
                for m, n in ((2, 1), (5, 3)):
                    if first <= m < end:
                        ins = V.tensor_tensor(modc[:, m], modc[:, m], ng[:, l, n, :].unsqueeze(2).broadcast_to([P, KD, 2]), ALU.mult)
                own(ins, done, value)

            def rotate(l, q):
                dve.wait_ge(win_read, NWIN * l + q + 1)
                if q:
                    dve.wait_ge(t_done, 7 * l + 1)
                haf = dict(h=H, a=2, two=2)
                split = "p (h a two f) -> p h a two f"
                src = stage[:, q % 2, 1, :]
                V.tensor_tensor(rope[:, 0, :].rearrange("p (h c) -> p h c", h=H), src.rearrange("p (h c) -> p h c", h=H),
                                con_("cos").unsqueeze(1).broadcast_to([P, H, HD]), ALU.mult)
                sin = con_("sin").rearrange("p (a two f) -> p a two f", a=2, two=2)
                for two in range(2):
                    ins = V.tensor_tensor(rope[:, 1, :].rearrange(split, **haf)[:, :, :, two, :],
                                          src.rearrange(split, **haf)[:, :, :, 1 - two, :],
                                          sin[:, :, two, :].unsqueeze(1).broadcast_to([P, H, 2, HD // 4]), ALU.mult)
                link(ins)
                V.tensor_tensor(rope[:, 0, :], rope[:, 0, :], rope[:, 1, :], ALU.add).then_inc(rope_ready, 1)

            def turned(l, q, dst):
                dve.wait_ge(t_done, 7 * l + q + 1)
                V.tensor_copy(dst, ps[:, 6:8, :]).then_inc(t_read_dve, 1)

            def pair(v):
                return v.rearrange("p (b c) -> p b c", b=2)

            def retention(l):
                dve.wait_ge(ratt_done, l + 1)
                V.tensor_tensor(ratt.rearrange("p g h t -> p g (h t)"), ps[:, 4:6, :],
                                decays.rearrange("p h t -> p (h t)").unsqueeze(1).broadcast_to([P, 2, W]), ALU.mult)\
                    .then_inc(ratt_ready, 1)
                V.tensor_tensor(qdec.rearrange("p d h t -> p d (h t)"), q_dec.rearrange("p d h t -> p d (h t)"),
                                rqT[:, 1].rearrange("p h t -> p (h t)").unsqueeze(1).broadcast_to([P, 2, W]), ALU.mult)\
                    .then_inc(qdec_ready, 1)

            def retention_out(l):
                dve.wait_ge(ro_done, l + 1)
                for u in range(8):
                    ins = V.bn_stats(bnst[:, u, :], ps[:, 4 + u // 4, (u % 4) * HD:(u % 4 + 1) * HD])
                link(ins)
                for u in range(8):
                    ins = V.bn_aggr(mv[:, u, :], bnst[:, u, :])
                link(ins)
                V.tensor_scalar(hms, mv[:, :, 1], 1e-5, None, ALU.add).then_inc(ve_ready, 1)
                dve.wait_ge(rsr_ready, l + 1)
                for u in range(8):
                    hc = slice((u % 4) * HD, (u % 4 + 1) * HD)
                    ins = V.tensor_scalar(br[:, 0, u // 4, hc], ps[:, 4 + u // 4, hc], mv[:, u, 0:1], hrs[:, u:u + 1],
                                          ALU.subtract, ALU.mult)
                own(ins, ro_read, l + 1)
                dve.wait_ge(win_read, NWIN * l + 4)
                V.tensor_tensor(br[:, 0], br[:, 0], rg_hg, ALU.mult).then_inc(br_ready, 1)

            def logits1(l):
                dve.wait_ge(na1_done, l + 1)
                V.scalar_tensor_tensor(lg1[:, :, 0, :], ps[:, 4, :].rearrange("p (h t) -> p h t", h=H), HD ** -0.5, bias,
                                       ALU.mult, ALU.add)
                own(V.tensor_scalar(lg1[:, :, 1, :], ps[:, 5, :].rearrange("p (h t) -> p h t", h=H), HD ** -0.5, None, ALU.mult),
                    na1_read, l + 1)
                link(V.tensor_reduce(negmax[:, 4:8], lg1.rearrange("p h s t -> p h (s t)"), AX_X, ALU.max))
                V.tensor_scalar(negmax[:, 4:8], negmax[:, 4:8], -1.0, None, ALU.mult).then_inc(max1_ready, 1)

            def logits0(l):
                dve.wait_ge(na0_done, l + 1)
                own(V.tensor_scalar(lg0, ps[:, 4, :].rearrange("p (h t) -> p h t", h=H), HD ** -0.5, None, ALU.mult),
                    na0_read, l + 1)
                link(V.tensor_reduce(negmax[:, 0:4], lg0, AX_X, ALU.max))
                V.tensor_scalar(negmax[:, 0:4], negmax[:, 0:4], -1.0, None, ALU.mult).then_inc(max0_ready, 1)

            def attention_out(l):
                dve.wait_ge(p1_ready, l + 1)
                dve.wait_ge(p0_ready, l + 1)
                link(V.reciprocal(pinv, psums))
                dve.wait_ge(pv_done, l + 1)
                for u in range(8):
                    hc = slice((u % 4) * HD, (u % 4 + 1) * HD)
                    ins = V.tensor_scalar(br[:, 1, u // 4, hc], ps[:, 4 + u // 4, hc], pinv[:, u:u + 1], None, ALU.mult)
                ins.then_inc(br_ready, 1)

            def forget(l, d, f, k):
                dve.wait_ge(t_read_act, 2 * l + d + 1)
                for h in range(H):
                    v = f.rearrange("p (g h t) -> p g h t", g=2, h=H)[:, :, h, :]
                    c = 4 * d + h
                    ins = V.tensor_scalar(v, v, olb[:, l, c:c + 1], lb[:, l, c:c + 1], ALU.mult, ALU.add)
                link(ins)
                link(V.tensor_scalar(f, f, F_MIN, None, ALU.max))
                link(V.tensor_scalar(k, f, -1.0, 1.0, ALU.mult, ALU.add))

            def halves(v, s):
                w = v.rearrange("p (b two s) -> p b two s", two=2, s=s)
                return w[:, :, 0, :], w[:, :, 1, :]

            def products(l, v):
                if v:
                    dve.wait_ge(lev_done, 8 * l + v)
                if v == NLEV:
                    V.tensor_tensor(k_lev, k_f, k_b, ALU.add).then_inc(lev_ready, 1)
                    return
                s = 1 << v
                (ql, qr), (kl, kr), (hl, hr) = halves(q_lev, s), halves(k_lev, s), halves(hq, s)
                V.tensor_tensor(qr, hr, halves(f_pre, s)[1], ALU.mult)
                V.tensor_tensor(ql, hl, halves(f_suf, s)[0], ALU.mult)
                V.tensor_tensor(kl, halves(k_f, s)[0], halves(f_sufx, s)[0], ALU.mult)
                V.tensor_tensor(kr, halves(k_b, s)[1], halves(b_prex, s)[1], ALU.mult).then_inc(lev_ready, 1)
                shape = [P, 2 * D // (4 * s), s]
                (pl, pr), (sl, sr) = halves(f_pre, s), halves(f_suf, s)
                xl, xr = halves(f_sufx, s)[0], halves(b_prex, s)[1]
                V.tensor_tensor(xl, xl, pr[:, :, s - 1:s].broadcast_to(shape), ALU.mult)
                link(V.tensor_tensor(xr, xr, sl[:, :, 0:1].broadcast_to(shape), ALU.mult))
                V.tensor_tensor(pr, pr, pl[:, :, s - 1:s].broadcast_to(shape), ALU.mult)
                link(V.tensor_tensor(sl, sl, sr[:, :, 0:1].broadcast_to(shape), ALU.mult))

            def level_read(l, v):
                dve.wait_ge(lev_done, 8 * l + v + 1)
                V.copy_predicated(hatt.rearrange("p (u t) -> p u t", u=8),
                                  level_mask[:, v, :].unsqueeze(1).broadcast_to([P, 8, P]),
                                  ps[:, 6:8, :].rearrange("p b (h t) -> p (b h) t", h=H)).then_inc(lev_read, 1)

            def heads_turned(l, n, bank):
                dve.wait_ge(brt_hi, 3 * l + n + 1)
                V.tensor_tensor(bt_lo.rearrange("p g k t -> p g (k t)"), ps[:, bank:bank + 2, :],
                                bt_hi.bitcast(F32).rearrange("p g k t -> p g (k t)"), ALU.subtract).then_inc(brt_read, 1)

            def input_lo(l, n):
                for g in range(2):
                    dve.wait_ge(h_hi_ready, input_count(l, n, g))
                    V.tensor_tensor(h_lo[:, g], h32[:, g], h_hi.bitcast(F32)[:, g], ALU.subtract).then_inc(h_lo_ready, 1)

            def mix_split(l, m):
                key, half, b, count = mix_unit(l, m)
                s = plan[key][0]
                dve.wait_ge(mix_hi, count + 1)
                part = slice(half * UNIT, (half + 1) * UNIT)
                V.tensor_tensor(ring_lo[s][:, part], ring[s][:, part], m_hi[b].bitcast(F32), ALU.subtract).then_inc(mix_lo, 1)

            def ahead(l, kind, i):
                for m in (2 * STEP[kind, i] + 3, 2 * STEP[kind, i] + 4):
                    mix_split(l, m)

            def gated(l, n):
                if n:
                    dve.wait_ge(brt_done, 3 * l + 2)
                dve.wait_ge(win_read, NWIN * l + 14 + 2 * n)
                for half in range(2):
                    dve.wait_ge(pr_done, 6 * l + 2 * n + half + 1)
                    cols = slice(half * 512, (half + 1) * 512)
                    src = ps[:, 2 * half:2 * half + 2, :]
                    dst = merged[:, :, cols] if n == 0 else br[:, 1]
                    ins = V.tensor_tensor(dst, src, gates[:, :, cols], ALU.mult)
                    own(ins, pr_read, 6 * l + 2 * n + half + 1)
                    if n:
                        ins = V.tensor_tensor(merged[:, :, cols], merged[:, :, cols], br[:, 1], ALU.add)
                        if n == 2 and half == 1:
                            ins.then_inc(merged_ready, 1)
                        else:
                            link(ins)

            def recurrence_keys(l):
                V.tensor_tensor(q_lev[:, 0:W], hq[:, W:2 * W], f_pre[:, W:2 * W], ALU.mult)
                V.tensor_tensor(q_lev[:, W:2 * W], hq[:, W:2 * W], f_suf[:, W:2 * W], ALU.mult)
                dve.wait_ge(lev_done, 8 * l + 8)
                V.tensor_tensor(k_lev[:, 0:W], k_f[:, 0:W], f_sufx[:, 0:W], ALU.mult)
                V.tensor_tensor(k_lev[:, W:2 * W], k_b[:, 0:W], b_prex[:, 0:W], ALU.mult).then_inc(qk_end, 1)

            def recurrence_out(l):
                dve.wait_ge(win_read, NWIN * l + 12)
                dve.wait_ge(s_hgn, 16 * (l + 1))
                V.tensor_tensor(rg_hg, rg_hg, hgn_sb.unsqueeze(1).broadcast_to([P, 2, W]), ALU.mult)
                dve.wait_ge(hsq_ready, l + 1)
                V.tensor_scalar(hms, hss, 1.0 / HD, EPS, ALU.mult, ALU.add).then_inc(hms_ready, 1)
                dve.wait_ge(hrs_ready, l + 1)
                for u in range(8):
                    hc = slice((u % 4) * HD, (u % 4 + 1) * HD)
                    ins = V.scalar_tensor_tensor(br[:, 0, u // 4, hc], ps[:, 6 + u // 4, hc], hrs[:, u:u + 1],
                                                 rg_hg[:, u // 4, hc], ALU.mult, ALU.mult)
                ins.then_inc(br_ready, 1)

            def residual(l, n):
                mean_square(l, n)
                w = 2 * l + (n == 3) + 1
                dve.wait_ge(post_read, w)
                dve.wait_ge(gb_done, w)
                link(V.tensor_tensor(pair(wide).rearrange("p g (b c) -> p (g b) c", b=2),
                                     pair(wide).rearrange("p g (b c) -> p (g b) c", b=2), ps[:, 4:8, :], ALU.mult))
                own(V.tensor_tensor(x_sb, x_sb, xn, ALU.add), x_new, w)

            def split(p, i, count):
                dve.wait_ge(hi_ready[p], count + 1)
                part = slice(p * UNIT, (p + 1) * UNIT)
                V.tensor_tensor(ring_lo[i % SLOTS][:, part], ring[i % SLOTS][:, part], w_hi[p].bitcast(F32), ALU.subtract)\
                    .then_inc(lo_ready[p], 1)

            def ffn(tiles, base, last):
                for i in range(NFS):
                    ahead = 0 if i == NFS - 1 else i + 1
                    if i < NFS - 1 or not last:
                        split(0, ahead, base + (i + 1))
                    dve.wait_ge(sil_ready, base + (i + 1))
                    V.tensor_tensor(act_v[:, i % 2, 0:tiles, :], act_s[:, 0:tiles, :], ps[:, 4:4 + tiles, FS:2 * FS], ALU.mult)\
                        .then_inc(act_ready, 1)
                    if i < NFS - 1 or not last:
                        split(1, ahead, base + (i + 1))
                    dve.wait_ge(acth_ready, base + (i + 1))
                    V.tensor_tensor(act_lo[:, 0:tiles].rearrange("p t j m -> p t (j m)"), ps[:, 6:6 + tiles, 0:FS],
                                    act_hi.bitcast(F32)[:, 0:tiles].rearrange("p t j m -> p t (j m)"), ALU.subtract)\
                        .then_inc(actT_ready, 1)
                    split(2, i, base + i)

            def routing():
                dve.wait_ge(rlog_done, 1)
                own(V.tensor_copy(rl.rearrange("p g e -> p (g e)"), ps[:, 0, 0:2 * E]), rcopy_ready, 1)
                for g in range(2):
                    ins = V.max(rmax[:, g, :], rl[:, g, :])
                link(ins)
                for g in range(2):
                    ins = V.max_index(ridx[:, g, :], rmax[:, g, :], rl[:, g, :])
                V.tensor_tensor(rw[:, :, 1:2], rmax[:, :, 1:2], rmax[:, :, 0:1], ALU.subtract).then_inc(rdiff_ready, 1)
                dve.wait_ge(rdiff_ready, 1)
                link(V.tensor_copy(rif, ridx))
                iota8 = con_("iota")[:, 0:E]
                for g in range(2):
                    V.tensor_scalar(sel[:, g, :], iota8, rif[:, g, 0:1], None, ALU.is_equal)
                    ins = V.tensor_scalar(r1[:, g, :], iota8, rif[:, g, 1:2], None, ALU.is_equal)
                link(ins)
                own(V.tensor_tensor(sel, sel, r1, ALU.add), sel_ready, 1)
                dve.wait_ge(back_done, 1)
                V.tensor_copy(h_rows.rearrange("p g (b c) -> p (g b) c", b=2), ps[:, 4:8, :]).then_inc(back_read, 1)
                dve.wait_ge(rexp_ready, 1)
                link(V.tensor_scalar(rw[:, :, 2:3], rw[:, :, 1:2], 1.0, None, ALU.add))
                link(V.reciprocal(rw[:, :, 3:4], rw[:, :, 2:3]))
                link(V.tensor_tensor(rw[:, :, 4:5], rw[:, :, 1:2], rw[:, :, 3:4], ALU.mult))
                for g in range(2):
                    V.tensor_scalar(rgate[:, g, :], iota8, rif[:, g, 0:1], rw[:, g, 3:4], ALU.is_equal, ALU.mult)
                    ins = V.tensor_scalar(r1[:, g, :], iota8, rif[:, g, 1:2], rw[:, g, 4:5], ALU.is_equal, ALU.mult)
                link(ins)
                V.tensor_tensor(rgate, rgate, r1, ALU.add)
                dve.wait_ge(place_done, 1)
                link(V.scalar_tensor_tensor(place, ps[:, 0, 0:2 * E].rearrange("p (g e) -> p g e", g=2), 1.0, sel,
                                            ALU.add, ALU.mult))
                V.tensor_scalar(place, place, -1.0, None, ALU.add)
                own(V.tensor_copy(count, ps[:, 0, 2 * E:3 * E]), place_ready, 1)

            def expert(e, base, last):
                one = bass.ds(e, 1)
                for g in range(2):
                    ins = V.tensor_scalar(pick[:, g, 0:P], con_("iota")[:, 0:P], place[:, g, one], None, ALU.is_equal)
                ins.then_inc(pick_ready, 1)
                dve.wait_ge(gather_done, e + 1)
                for b in range(2):
                    dve.wait_ge(gather_read_act, e * 2 + (b + 1))
                    blocks = slice(4 * b, 4 * b + 4)
                    ins = V.tensor_tensor(h_lo[:, 0, blocks, :].rearrange("p k m -> p (k m)"), ps[:, 4 + b, :],
                                          h_hi.bitcast(F32)[:, 0, blocks, :].rearrange("p k m -> p (k m)"), ALU.subtract)
                ins.then_inc(gather_read_dve, 1)
                n = dve.value_load(count[0:1, one])
                with dve.If(n > P):
                    for g in range(2):
                        V.tensor_scalar(pick[:, g, P:2 * P], con_("iota")[:, P:2 * P], place[:, g, one], None, ALU.is_equal)
                        ins = V.tensor_scalar(weigh[:, 0, g, :], con_("iota")[:, P:2 * P], place[:, g, one], rgate[:, g, one],
                                              ALU.is_equal, ALU.mult)
                    ins.then_inc(over_pick_ready, 1)
                    dve.wait_ge(over_read_act, e + 1)
                    V.tensor_tensor(h_lo[:, 1].rearrange("p (b k) m -> p b (k m)", b=2), ps[:, 4:6, :],
                                    h_hi.bitcast(F32)[:, 1].rearrange("p (b k) m -> p b (k m)", b=2), ALU.subtract)\
                        .then_inc(over_read_dve, 1)
                    ffn(2, base, last)
                    dve.wait_ge(over_sum_done, e + 1)
                    dve.wait_ge(over_sum_read, e + 1)
                    V.tensor_tensor(ff_y.rearrange("p g (b c) -> p (g b) c", b=2), ff_y.rearrange("p g (b c) -> p (g b) c", b=2),
                                    ps[:, 4:8, :], ALU.add).then_inc(over_sum_read, 1)
                with dve.Else():
                    dve.sem_inc(over_pick_ready, 1)
                    dve.sem_inc(over_read_dve, 1)
                    dve.sem_inc(over_sum_read, 1)
                    ffn(1, base, last)

            for l in range(L):
                mean_square(l, 0)
                dve.wait_ge(exps_ready, l + 1)
                for d, name in ((0, "mask_above"), (1, "mask_below")):
                    ins = V.tensor_tensor(ratt[:, d], ratt[:, d], con_(name).unsqueeze(1).broadcast_to([P, H, P]), ALU.mult)
                link(ins)
                V.tensor_tensor(decays, ratt[:, 0], ratt[:, 1], ALU.add)
                dve.wait_ge(s_bias, 16 * (l + 1))
                link(V.tensor_tensor(bias, bias, con_("window").unsqueeze(1).broadcast_to([P, H, P]), ALU.add))
                if l:
                    mix_split(l, 0)
                rows(l, 0)
                if l == 0:
                    link(read_mod(0))
                    modulation(0, 0, 2, mod_raw[:, 0:8 * MOD_FIRST], mod_ready, 1)
                else:
                    dve.wait_ge(mod_read, 1)
                    modulation(1, 0, 6, mod_raw[:, 2 * NMOD:4 * NMOD], mod_ready, 2)
                turn_read(l, 0)
                input_lo(l, 0)
                for m in range(l, SLOTS):
                    mix_split(l, m)
                if l == 0:
                    own(read_mod(1), mod_read, 1)
                    modulation(0, 2, 6, mod_raw[:, 8 * MOD_FIRST:2 * NMOD], mod_rest, 1)
                ahead(l, "win", 0)
                rotate(l, 0)
                ahead(l, "win", 1)
                turned(l, 0, pair(u1[:, 0:D]))
                rotate(l, 1)
                ahead(l, "win", 2)
                turned(l, 1, pair(u1[:, D:2 * D]))
                ahead(l, "win", 3)
                retention(l)
                ahead(l, "win", 4)
                retention_out(l)
                V.memset(f_sufx, 1.0)
                ahead(l, "win", 5)
                turned(l, 2, pair(u2[:, 0:D]))
                ahead(l, "win", 6)
                turned(l, 3, pair(u2[:, D:2 * D]))
                ahead(l, "win", 7)
                logits1(l)
                ahead(l, "win", 8)
                turned(l, 4, pair(hq))
                logits0(l)
                V.memset(b_prex, 1.0)
                ahead(l, "win", 9)
                dve.wait_ge(pt1_done, l + 1)
                V.tensor_copy(pT1.rearrange("p s h t -> p s (h t)"), ps[:, 4:6, :]).then_inc(pt1_read, 1)
                forget(l, 0, f_pre, k_f)
                ahead(l, "win", 10)
                dve.wait_ge(pt0_done, l + 1)
                V.tensor_copy(pT0.rearrange("p h t -> p (h t)"), ps[:, 4, :]).then_inc(pt0_read, 1)
                forget(l, 1, f_suf, k_b)
                products(l, 0)
                ahead(l, "win", 11)
                attention_out(l)
                level_read(l, 0)
                products(l, 1)
                ahead(l, "win", 12)
                heads_turned(l, 0, 4)
                level_read(l, 1)
                products(l, 2)
                ahead(l, "win", 13)
                level_read(l, 2)
                products(l, 3)
                ahead(l, "br", 0)
                gated(l, 0)
                level_read(l, 3)
                products(l, 4)
                ahead(l, "win", 14)
                heads_turned(l, 1, 4)
                level_read(l, 4)
                products(l, 5)
                ahead(l, "win", 15)
                level_read(l, 5)
                products(l, 6)
                ahead(l, "br", 1)
                gated(l, 1)
                level_read(l, 6)
                products(l, NLEV)
                ahead(l, "win", 16)
                level_read(l, NLEV)
                recurrence_keys(l)
                ahead(l, "win", 17)
                recurrence_out(l)
                heads_turned(l, 2, 6)
                mix_split(l, MIX_UNITS - 3)
                gated(l, 2)
                mix_split(l, MIX_UNITS - 2)
                for g in range(2):
                    dve.wait_ge(mt_hi, 2 * l + g + 1)
                    V.tensor_tensor(h_lo[:, g].rearrange("p (b k) t -> p b (k t)", b=2), ps[:, 4 + 2 * g:6 + 2 * g, :],
                                    h_hi.bitcast(F32)[:, g].rearrange("p (b k) t -> p b (k t)", b=2), ALU.subtract)\
                        .then_inc(mt_read, 1)
                mix_split(l, MIX_UNITS - 1)
                for p in range(2):
                    split(p, 0, l * NFS)
                residual(l, 1)
                mean_square(l, 2)
                rows(l, 2)
                turn_read(l, 2)
                if l == 0:
                    input_lo(0, 2)
                    ffn(2, 0, True)
                else:
                    routing()
                    own(V.memset(ff_y, 0.0), over_sum_read, 1)
                    with dve.Fori(0, E - 1) as e:
                        expert(e, e * NFS + NFS, False)
                    expert(E - 1, E * NFS, True)
                    for e in range(E):
                        if e >= 2:
                            dve.wait_ge(weigh_done, e - 1)
                        for g in range(2):
                            ins = V.tensor_scalar(weigh[:, e % 2, g, :], con_("iota")[:, 0:P], place[:, g, e:e + 1],
                                                  rgate[:, g, e:e + 1], ALU.is_equal, ALU.mult)
                        ins.then_inc(weigh_ready, 1)
                    dve.wait_ge(sum_done, 1)
                    dve.wait_ge(over_sum_read, E + 1)
                    V.tensor_tensor(ff_y.rearrange("p g (b c) -> p (g b) c", b=2), ff_y.rearrange("p g (b c) -> p (g b) c", b=2),
                                    ps[:, 0:4, :], ALU.add).then_inc(y_ready, 1)
                residual(l, 3)


def _layout(a):
    c = np.ascontiguousarray
    g = lambda n: np.asarray(a[n])
    rows = np.arange(P)

    def panels(w, width, blocks):
        lead = w.shape[:-2]
        n = w.shape[-1] // width
        v = w.reshape(lead + (blocks, P, n, width))
        k = len(lead)
        return v.transpose(tuple(range(k)) + (k + 2, k + 1, k, k + 3)).reshape(lead + (n, P, blocks * width))

    out = {}
    out["x"] = np.concatenate([g("x_prompt")[0], g("x_sample")[0]], axis=1)
    out["c_t"] = np.stack([g("c_ctx"), g("c")[0]]).reshape(2, KD, P).transpose(2, 1, 0).reshape(P, KD, 2)
    out["b_mod_t"] = g("b_mod").reshape(L, NMOD, P).transpose(2, 0, 1)
    out["norm_t"] = g("norm_g").reshape(L, 4, KD, P).transpose(3, 0, 1, 2)
    out["lb_t"] = g("hg_lb").reshape(L, 2, H, HD).transpose(3, 0, 1, 2).reshape(P, L, 8)
    out["decay"] = np.broadcast_to(g("ret_decay").reshape(1, L * 8), (P, L * 8))
    out["hgn"] = np.broadcast_to(g("hg_norm")[:, None, :], (L, P, W))
    r, q = rows // GRID_W, rows % GRID_W
    row_off = r[None, :] - r[:, None] + 7
    col_off = np.clip(q[None, :] - q[:, None] + NA_COLS - 1, 0, 2 * NA_COLS - 2)
    out["rpb"] = g("na_rpb")[:, :, row_off, col_off].transpose(0, 2, 1, 3)
    out["cache_kt"] = g("cache_na_k")[0].transpose(0, 3, 2, 1)
    out["cache_v"] = g("cache_na_v")[0].reshape(L, P, W)
    out["s_ret"] = g("state_ret")[0].transpose(0, 3, 1, 2, 4)
    out["s_hg"] = g("state_hgrn")[0].transpose(0, 3, 1, 2, 4)
    out["router"] = g("w_router")[0].reshape(KD, P, E).transpose(1, 0, 2)
    out["consts"] = _constants(rows)
    m, n = rows[:, None], rows[None, :]
    levels = [((m >> (v + 1)) == (n >> (v + 1))) & ((m >> v) != (n >> v)) for v in range(NLEV)] + [m == n]
    out["levels"] = np.stack(levels, axis=1).astype(np.int32)
    out["w_mod"] = panels(g("w_mod"), 512, KD).reshape(L * NSLAB_MOD, P, KD * 512)
    out["w_in"] = panels(g("w_in"), 512, KD)
    out["w_br"] = panels(g("w_br"), D, 4)[:, :, 0]
    out["w_o"] = panels(g("w_o"), 512, KD)
    gu = np.concatenate([g("w_ffn_gu"), g("w_exp_gu")[0]])
    gu = gu.reshape(E + 1, KD, P, 2, NFS, FS).transpose(0, 4, 2, 1, 3, 5).reshape(E + 1, NFS, P, KD * 2 * FS)
    down = np.concatenate([g("w_ffn_down"), g("w_exp_down")[0]])
    down = down.reshape(E + 1, NFS, 2, P, D).transpose(0, 1, 3, 2, 4).reshape(E + 1, NFS, P, 2 * D)
    out["w_ff"] = np.concatenate([gu, down], axis=3)
    return {k: c(v) for k, v in out.items()}


def _constants(rows):
    m, n = rows[:, None].astype(np.float64), rows[None, :].astype(np.float64)
    nf = HD // 4
    inv = 10000.0 ** (-np.arange(nf, dtype=np.float32) / np.float32(nf))
    pos = np.stack([rows // GRID_W, rows % GRID_W], axis=-1).astype(np.float32)
    ang = (pos[:, :, None] * inv.astype(np.float32)).astype(np.float32)
    cos = np.repeat(np.cos(ang)[:, :, None, :], 2, axis=2).reshape(P, HD)
    sin = np.stack([-np.sin(ang), np.sin(ang)], axis=2).reshape(P, HD)
    q = rows % GRID_W
    first = np.clip(q - NA_COLS // 2, 0, GRID_W - NA_COLS)[:, None]
    inside = (q[None, :] >= first) & (q[None, :] < first + NA_COLS)
    parts = {
        "ident": np.eye(P), "cos": cos, "sin": sin,
        "above": np.maximum(n - m, 0), "below": np.maximum(m - n, 0),
        "mask_above": (n >= m) * HD ** -0.5, "mask_below": (n <= m) * HD ** -0.5,
        "ramp_up": np.broadcast_to(n + 1, (P, P)), "ramp_down": np.broadcast_to(P - n, (P, P)),
        "window": np.where(inside, 0.0, -1e30), "iota": np.broadcast_to(np.arange(2 * P), (P, 2 * P)),
        "half": np.full((P, 2), -0.5), "age": np.concatenate([P - 1 - m, m], axis=1), "before": m < n, "ones": np.ones((P, P)),
    }
    return np.concatenate([parts[k] for k in CONST_W], axis=1).astype(np.float32)


_INS = ["x", "c_t", "b_mod_t", "norm_t", "lb_t", "decay", "hgn", "rpb", "cache_kt", "cache_v", "s_ret", "s_hg", "router",
        "consts", "levels", "w_mod", "w_in", "w_br", "w_o", "w_ff"]
_OUTS = [(P, 2 * D), (L, P, W), (L, P, W), (L, P, 2 * W), (L, P, 2 * W)]


def kernel(**inputs):
    import numpy as _np
    import concourse.bacc as _bacc
    from concourse import mybir as _mybir
    from concourse.bass_utils import run_bass_kernel_spmd as _run

    nc = _bacc.Bacc("TRN2", target_bir_lowering=False, num_devices=1, dynamic_dma_scratch_size=4096)
    laid = _layout(inputs)
    arrays, args = {}, []
    for name in _INS:
        a = laid[name]
        arrays[f"in_{name}"] = a
        args.append(nc.dram_tensor(f"in_{name}", a.shape, _mybir.dt.from_np(a.dtype), kind="ExternalInput").ap())
    for i, shape in enumerate(_OUTS):
        args.append(nc.dram_tensor(f"out_{i}", shape, _mybir.dt.float32, kind="ExternalOutput").ap())
    program(nc, *args)
    r = _run(nc, [arrays], core_ids=[0])
    y, k, v, sr, sh = (r.results[0][f"out_{i}"] for i in range(len(_OUTS)))
    y = _np.asarray(y).reshape(P, 2, D)
    states = [_np.asarray(s).reshape(L, P, 2, H, HD).transpose(0, 2, 3, 1, 4)[None] for s in (sr, sh)]
    return (_np.ascontiguousarray(y[:, 0])[None], _np.ascontiguousarray(y[:, 1])[None],
            _np.asarray(k).reshape(1, L, P, H, HD), _np.asarray(v).reshape(1, L, P, H, HD),
            _np.ascontiguousarray(states[0]), _np.ascontiguousarray(states[1]))
```
